# Optimizing a Trainium2 kernel written in Bass

```python
import jax, jax.numpy as jnp
from jax import lax
import numpy as np

D_MODEL = 1024
BATCH = 1
SEQ = 256
DEPTH = 2

D_MIX = D_MODEL
N_GROUPS = 4
GROUP_W = D_MIX // N_GROUPS
HEAD_DIM = 64
ROT_DIM = HEAD_DIM // 4
ROPE_THETA = 500000.0
EPS = 1e-6
D_FF = 2816
SG_HEADS = GROUP_W // HEAD_DIM
SG_CHUNK = 128
SC_WIDTH = 3
DSA_HEADS = GROUP_W // HEAD_DIM
KV_LATENT = 128
IDX_HEADS = 4
IDX_DIM = 64
IDX_TOPK = 256
DSA_BLOCK = 128
GDN_HEADS = GROUP_W // HEAD_DIM
GDN_CONV = 4
GDN_CHUNK = 64
MEM_LEN = 256
XA_HEADS = 4
XA_HEAD_DIM = D_MODEL // XA_HEADS

SPLIT_SIZES = (2 * GROUP_W, 3 * GROUP_W, GROUP_W, KV_LATENT, IDX_HEADS * IDX_DIM, IDX_DIM,
               IDX_HEADS, 3 * GROUP_W, GDN_HEADS, GDN_HEADS, GROUP_W)
N_MIX_IN = sum(SPLIT_SIZES)

kernel_name = "hybrid_parallel_group_decoder"

def rmsnorm(x, g):
    xf = x.astype(jnp.float32)
    y = xf * lax.rsqrt(jnp.mean(xf * xf, axis=-1, keepdims=True) + EPS)
    return (y * g.astype(jnp.float32)).astype(x.dtype)

def swiglu(h, wg, wu, wd):
    return (jax.nn.silu(h @ wg) * (h @ wu)) @ wd

def causal_dwconv(x, w):
    K = w.shape[-1]
    S = x.shape[1]
    xp = jnp.pad(x, ((0, 0), (K - 1, 0), (0, 0)))
    return sum(xp[:, j:j + S, :] * w[:, j] for j in range(K))

def partial_rope(x, pos):
    half = ROT_DIM // 2
    inv = ROPE_THETA ** (-jnp.arange(half, dtype=jnp.float32) * (2.0 / ROT_DIM))
    ang = pos.astype(jnp.float32)[:, :, None, None] * inv
    cos, sin = jnp.cos(ang), jnp.sin(ang)
    xf = x.astype(jnp.float32)
    x1, x2, xp = xf[..., :half], xf[..., half:ROT_DIM], xf[..., ROT_DIM:]
    return jnp.concatenate([x1 * cos - x2 * sin, x2 * cos + x1 * sin, xp], -1).astype(x.dtype)

def spatial_gating(uv, norm_g, w_s, b_s):
    Bsz, S, _ = uv.shape
    u, v = jnp.split(jax.nn.gelu(uv), 2, axis=-1)
    v = rmsnorm(v, norm_g)
    n = S // SG_CHUNK
    vc = v.reshape(Bsz, n, SG_CHUNK, SG_HEADS, HEAD_DIM)
    causal = jnp.tril(jnp.ones((SG_CHUNK, SG_CHUNK), bool))
    w = jnp.where(causal, w_s, 0.0).astype(v.dtype)
    mixed = jnp.einsum('hts,bnshd->bnthd', w, vc) + b_s.T.astype(v.dtype)[None, None, :, :, None]
    return u * mixed.reshape(Bsz, S, GROUP_W)

def short_gated_conv(bch, w_conv):
    b, c, h = jnp.split(bch, 3, axis=-1)
    return b * causal_dwconv(c * h, w_conv)

def sparse_indexed_attention(q, ckv, iq, ik, iw, pos, kv_norm, w_uk, w_uv, ik_norm):
    Bsz, S, _ = q.shape
    c = rmsnorm(ckv, kv_norm)
    k = partial_rope((c @ w_uk).reshape(Bsz, S, DSA_HEADS, HEAD_DIM), pos)
    v = (c @ w_uv).reshape(Bsz, S, DSA_HEADS, HEAD_DIM)
    q = partial_rope(q.reshape(Bsz, S, DSA_HEADS, HEAD_DIM), pos)
    iq = partial_rope(iq.reshape(Bsz, S, IDX_HEADS, IDX_DIM), pos)
    ik = partial_rope(rmsnorm(ik, ik_norm)[:, :, None, :], pos)[:, :, 0, :]
    iw = iw.astype(jnp.float32) * (IDX_HEADS ** -0.5)
    topk = min(IDX_TOPK, S // 4)
    nb = S // DSA_BLOCK
    kv = jnp.concatenate([k, v], axis=-1)
    key_idx = jnp.arange(S)

    def to_blocks(t):
        return jnp.swapaxes(t.reshape(Bsz, nb, DSA_BLOCK, *t.shape[2:]), 0, 1)

    def block(args):
        qb, iqb, iwb, start = args
        qpos = start + jnp.arange(DSA_BLOCK)
        s = jnp.einsum('bqhd,bsd->bqhs', iqb, ik, preferred_element_type=jnp.float32) * (IDX_DIM ** -0.5)
        score = jnp.einsum('bqh,bqhs->bqs', iwb, jax.nn.relu(s))
        score = jnp.where(key_idx[None, None, :] <= qpos[None, :, None], score, -jnp.inf)
        _, idx = lax.top_k(score, topk)
        kvg = jax.vmap(lambda a, i: a[i])(kv, idx)
        kg, vg = kvg[..., :HEAD_DIM], kvg[..., HEAD_DIM:]
        logits = jnp.einsum('bqhd,bqkhd->bqhk', qb, kg, preferred_element_type=jnp.float32) * (HEAD_DIM ** -0.5)
        valid = (idx <= qpos[None, :, None])[:, :, None, :]
        p = jax.nn.softmax(jnp.where(valid, logits, -jnp.inf), axis=-1)
        return jnp.einsum('bqhk,bqkhd->bqhd', p.astype(vg.dtype), vg)

    starts = jnp.arange(nb) * DSA_BLOCK
    out = lax.map(block, (to_blocks(q), to_blocks(iq), to_blocks(iw), starts))
    return jnp.swapaxes(out, 0, 1).reshape(Bsz, S, GROUP_W)

def chunk_gated_delta_rule(q, k, v, g, beta):
    Bsz, S, H, dk = q.shape
    dv = v.shape[-1]
    C = GDN_CHUNK
    n = S // C

    def blk(t):
        return jnp.moveaxis(t.reshape(Bsz, n, C, H, -1), 3, 1)

    q, k, v = blk(q), blk(k), blk(v)
    beta = blk(beta[..., None])[..., 0]
    gc = jnp.cumsum(blk(g[..., None])[..., 0], axis=-1)
    incl = jnp.tril(jnp.ones((C, C), bool))
    strict = jnp.tril(jnp.ones((C, C), bool), -1)
    decay = jnp.exp(jnp.where(incl, gc[..., :, None] - gc[..., None, :], -jnp.inf))
    kb = k * beta[..., None]
    a_mat = jnp.where(strict, jnp.einsum('bhnid,bhnjd->bhnij', kb, k) * decay, 0.0)
    lhs = a_mat + jnp.eye(C, dtype=jnp.float32)
    rhs = jnp.concatenate([v * beta[..., None], kb * jnp.exp(gc)[..., None]], axis=-1)
    sol = lax.linalg.triangular_solve(lhs, rhs, left_side=True, lower=True, unit_diagonal=True)
    u, w = sol[..., :dv], sol[..., dv:]
    attn = jnp.where(incl, jnp.einsum('bhnid,bhnjd->bhnij', q, k) * decay, 0.0)

    def step(state, xs):
        q_i, k_i, u_i, w_i, attn_i, gc_i = xs
        v_new = u_i - jnp.einsum('bhck,bhkv->bhcv', w_i, state)
        o_i = (jnp.einsum('bhck,bhkv->bhcv', q_i * jnp.exp(gc_i)[..., None], state)
               + jnp.einsum('bhcs,bhsv->bhcv', attn_i, v_new))
        g_last = gc_i[..., -1:]
        state = (state * jnp.exp(g_last)[..., None]
                 + jnp.einsum('bhck,bhcv->bhkv', k_i * jnp.exp(g_last - gc_i)[..., None], v_new))
        return state, o_i

    xs = tuple(jnp.moveaxis(t, 2, 0) for t in (q, k, u, w, attn, gc))
    state0 = jnp.zeros((Bsz, H, dk, dv), jnp.float32)
    _, o = lax.scan(step, state0, xs)
    return o.transpose(1, 0, 3, 2, 4).reshape(Bsz, S, H, dv)

def gated_deltanet(qkv, a, b, gate, w_conv, a_log, dt_bias, out_norm):
    Bsz, S, _ = qkv.shape
    dtype = qkv.dtype
    qkv = jax.nn.silu(causal_dwconv(qkv, w_conv))
    q, k, v = [t.reshape(Bsz, S, GDN_HEADS, HEAD_DIM).astype(jnp.float32) for t in jnp.split(qkv, 3, axis=-1)]
    q = q * lax.rsqrt(jnp.sum(q * q, axis=-1, keepdims=True) + EPS)
    k = k * lax.rsqrt(jnp.sum(k * k, axis=-1, keepdims=True) + EPS)
    beta = jax.nn.sigmoid(b.astype(jnp.float32))
    g = -jnp.exp(a_log.astype(jnp.float32)) * jax.nn.softplus(a.astype(jnp.float32) + dt_bias.astype(jnp.float32))
    o = chunk_gated_delta_rule(q * (HEAD_DIM ** -0.5), k, v, g, beta)
    o = rmsnorm(o, out_norm) * jax.nn.silu(gate.reshape(Bsz, S, GDN_HEADS, HEAD_DIM).astype(jnp.float32))
    return o.reshape(Bsz, S, GROUP_W).astype(dtype)

def memory_cross_attention(h, m, wq, wk, wv, wo):
    Bsz, S, _ = h.shape
    q = (h @ wq).reshape(Bsz, S, XA_HEADS, XA_HEAD_DIM)
    k = (m @ wk).reshape(Bsz, -1, XA_HEADS, XA_HEAD_DIM)
    v = (m @ wv).reshape(Bsz, -1, XA_HEADS, XA_HEAD_DIM)
    logits = jnp.einsum('bqhd,bkhd->bhqk', q, k, preferred_element_type=jnp.float32) * (XA_HEAD_DIM ** -0.5)
    p = jax.nn.softmax(logits, axis=-1)
    o = jnp.einsum('bhqk,bkhd->bqhd', p.astype(v.dtype), v).reshape(Bsz, S, D_MODEL)
    return o @ wo

def setup_inputs(seed: int = 0) -> dict:
    key = jax.random.key(seed)
    ks = iter(list(jax.random.split(key, 48)))
    L = DEPTH

    def nrm(shape, fan_in):
        return jax.random.normal(next(ks), shape, jnp.float32) * (fan_in ** -0.5)

    def gain(shape):
        return 1.0 + 0.05 * jax.random.normal(next(ks), shape, jnp.float32)

    x = jax.random.normal(next(ks), (BATCH, SEQ, D_MODEL), jnp.float32)
    mem = jax.random.normal(next(ks), (BATCH, MEM_LEN, D_MODEL), jnp.float32)
    offset = jax.random.randint(next(ks), (BATCH, 1), 0, 4096, dtype=jnp.int32)
    positions = offset + jnp.arange(SEQ, dtype=jnp.int32)[None, :]
    d = {"x": x, "mem": mem, "positions": positions}
    d["ffn1_norm"] = gain((L, D_MODEL))
    d["ffn1_wg"] = nrm((L, D_MODEL, D_FF), D_MODEL)
    d["ffn1_wu"] = nrm((L, D_MODEL, D_FF), D_MODEL)
    d["ffn1_wd"] = nrm((L, D_FF, D_MODEL), D_FF)
    d["mix_norm"] = gain((L, D_MODEL))
    d["w_mix_in"] = nrm((L, D_MODEL, N_MIX_IN), D_MODEL)
    d["w_mix_out"] = nrm((L, D_MIX, D_MODEL), D_MIX)
    d["sg_norm"] = gain((L, GROUP_W))
    d["sg_w"] = nrm((L, SG_HEADS, SG_CHUNK, SG_CHUNK), SG_CHUNK)
    d["sg_b"] = 1.0 + 0.1 * jax.random.normal(next(ks), (L, SG_HEADS, SG_CHUNK), jnp.float32)
    d["sc_conv"] = nrm((L, GROUP_W, SC_WIDTH), SC_WIDTH)
    d["kv_norm"] = gain((L, KV_LATENT))
    d["w_uk"] = nrm((L, KV_LATENT, GROUP_W), KV_LATENT)
    d["w_uv"] = nrm((L, KV_LATENT, GROUP_W), KV_LATENT)
    d["idx_k_norm"] = gain((L, IDX_DIM))
    d["gdn_conv"] = nrm((L, 3 * GROUP_W, GDN_CONV), GDN_CONV)
    d["gdn_a_log"] = jnp.log(jax.random.uniform(next(ks), (L, GDN_HEADS), jnp.float32, 1.0, 16.0))
    dt = jnp.exp(jax.random.uniform(next(ks), (L, GDN_HEADS), jnp.float32, np.log(1e-3), np.log(1e-1)))
    d["gdn_dt_bias"] = dt + jnp.log(-jnp.expm1(-dt))
    d["gdn_out_norm"] = gain((L, HEAD_DIM))
    d["xa_norm"] = gain((L, D_MODEL))
    d["mem_norm"] = gain((L, D_MODEL))
    d["xa_wq"] = nrm((L, D_MODEL, D_MODEL), D_MODEL)
    d["xa_wk"] = nrm((L, D_MODEL, D_MODEL), D_MODEL)
    d["xa_wv"] = nrm((L, D_MODEL, D_MODEL), D_MODEL)
    d["xa_wo"] = nrm((L, D_MODEL, D_MODEL), D_MODEL)
    d["ffn2_norm"] = gain((L, D_MODEL))
    d["ffn2_wg"] = nrm((L, D_MODEL, D_FF), D_MODEL)
    d["ffn2_wu"] = nrm((L, D_MODEL, D_FF), D_MODEL)
    d["ffn2_wd"] = nrm((L, D_FF, D_MODEL), D_FF)
    d["final_norm"] = gain((D_MODEL,))
    return d

def reference(x, mem, positions, ffn1_norm, ffn1_wg, ffn1_wu, ffn1_wd, mix_norm, w_mix_in, w_mix_out,
              sg_norm, sg_w, sg_b, sc_conv, kv_norm, w_uk, w_uv, idx_k_norm, gdn_conv, gdn_a_log,
              gdn_dt_bias, gdn_out_norm, xa_norm, mem_norm, xa_wq, xa_wk, xa_wv, xa_wo,
              ffn2_norm, ffn2_wg, ffn2_wu, ffn2_wd, final_norm):
    split_points = [int(p) for p in np.cumsum(SPLIT_SIZES)[:-1]]
    for l in range(DEPTH):
        x = x + 0.5 * swiglu(rmsnorm(x, ffn1_norm[l]), ffn1_wg[l], ffn1_wu[l], ffn1_wd[l])
        h = rmsnorm(x, mix_norm[l])
        (p_sg, p_sc, p_q, p_ckv, p_iq, p_ik, p_iw,
         p_gqkv, p_ga, p_gb, p_gg) = jnp.split(h @ w_mix_in[l], split_points, axis=-1)
        y_a = spatial_gating(p_sg, sg_norm[l], sg_w[l], sg_b[l])
        y_b = short_gated_conv(p_sc, sc_conv[l])
        y_c = sparse_indexed_attention(p_q, p_ckv, p_iq, p_ik, p_iw, positions,
                                       kv_norm[l], w_uk[l], w_uv[l], idx_k_norm[l])
        y_d = gated_deltanet(p_gqkv, p_ga, p_gb, p_gg, gdn_conv[l], gdn_a_log[l],
                             gdn_dt_bias[l], gdn_out_norm[l])
        x = x + jnp.concatenate([y_a, y_b, y_c, y_d], axis=-1) @ w_mix_out[l]
        x = x + memory_cross_attention(rmsnorm(x, xa_norm[l]), rmsnorm(mem, mem_norm[l]),
                                       xa_wq[l], xa_wk[l], xa_wv[l], xa_wo[l])
        x = x + 0.5 * swiglu(rmsnorm(x, ffn2_norm[l]), ffn2_wg[l], ffn2_wu[l], ffn2_wd[l])
    return rmsnorm(x, final_norm)


_drawn_inputs = setup_inputs


def setup_inputs(seed=0):
    import zlib

    import numpy as np

    out = dict(_drawn_inputs(seed))
    spreads = {}
    factors = {'sg_norm': 3.781,
     'kv_norm': 4.603,
     'idx_k_norm': 2.952,
     'gdn_out_norm': 3.03,
     'xa_norm': 7.617,
     'mem_norm': 5.428}
    for name, (base, spread) in spreads.items():
        noise = np.random.default_rng([zlib.crc32(name.encode()), seed]).standard_normal(out[name].shape)
        drawn = base * np.exp(spread * noise) if base else spread * noise
        out[name] = __import__('jax').numpy.asarray(drawn.astype(out[name].dtype))
    for name, factor in factors.items():
        out[name] = (out[name] * factor).astype(out[name].dtype)
    return out
```

```python
from contextlib import ExitStack

import concourse.bass as bass
import numpy as np
from concourse import mybir

F32 = mybir.dt.float32
I32 = mybir.dt.int32
ALU = mybir.AluOpType
ACT = mybir.ActivationFunctionType
AX = mybir.AxisListType.X

P = 128
D = 1024
KC = D // P
S = 256
NT = S // P
DEPTH = 2
D_FF = 2816
STEPS = D_FF // 256
PAIRS = (STEPS - 1) // 2
GW = 256
HD = 64
H = 4
LAT = 128
ROT = 8
THETA = 500000.0
EPS = 1e-6
TOPK = 64
CH = 64
NCH = S // CH
LEVELS = (1, 2, 4, 8, 16, 32)
N_IN = 3020
FILL = -3.0e38
TAKEN = -3.4e38
TAKEN_BELOW = -3.2e38
AWAY = -1.0e30

C_SGU, C_SGV, C_SCB, C_SCC, C_SCH, C_Q, C_CKV, C_IQ1, C_GQKV, C_GA, C_GG = (
    0, 256, 512, 768, 1024, 1280, 1536, 1792, 1988, 2756, 2764)
W_IQ1 = C_GQKV - C_IQ1

RING = 6
FFN_UNITS = 3 * STEPS
MIX_COLS = [(C_GQKV, 256), (C_GQKV + 256, 256), (C_GQKV + 512, 256), (C_Q, 256), (C_CKV, 256),
            (C_IQ1, W_IQ1), (C_SGV, 256), (C_SGU, 256), (C_SCC, 256), (C_SCH, 256), (C_SCB, 256),
            (C_GG, 256)]
U_FFN1 = 0
U_MIX = U_FFN1 + FFN_UNITS
(U_GQ, U_GK, U_GV, U_Q, U_CKV, U_IQ1, U_SGV, U_SGU, U_SCC, U_SCH, U_SCB, U_GG) = range(
    U_MIX, U_MIX + len(MIX_COLS))
U_XK = U_GG + 1
U_XV = U_XK + 4
U_OUT = U_XV + 4
U_XQ = U_OUT + 4
U_XO = U_XQ + 4
U_FFN2 = U_XO + 4
N_UNITS = U_FFN2 + FFN_UNITS

N_ROWS = 5 * KC + H + 1
R_FFN1, R_MIX, R_XA, R_MEM, R_FFN2, R_SGB, R_KV = 0, KC, 2 * KC, 3 * KC, 4 * KC, 5 * KC, 5 * KC + H

NAMES = ['x', 'mem', 'positions', 'ffn1_norm', 'ffn1_wg', 'ffn1_wu', 'ffn1_wd', 'mix_norm', 'w_mix_in',
         'w_mix_out', 'sg_norm', 'sg_w', 'sg_b', 'sc_conv', 'kv_norm', 'w_uk', 'w_uv', 'idx_k_norm',
         'gdn_conv', 'gdn_a_log', 'gdn_dt_bias', 'gdn_out_norm', 'xa_norm', 'mem_norm', 'xa_wq', 'xa_wk',
         'xa_wv', 'xa_wo', 'ffn2_norm', 'ffn2_wg', 'ffn2_wu', 'ffn2_wd', 'final_norm']


class Signals:

    def __init__(self, nc, ctx, per):
        self.nc, self.ctx, self.per = nc, ctx, per
        self.sems, self.counts = {}, {}

    def sem(self, name):
        if name not in self.sems:
            self.sems[name] = self.ctx.enter_context(self.nc.semaphore(name))
        return self.sems[name]

    def inc(self, name, times=1):
        self.counts[name] = self.counts.get(name, 0) + times
        return self.sem(name)

    def at(self, name, layer, k=None):
        per = self.per.get(name, 0)
        return self.sem(name), layer * per + (per if k is None else k)


def broadcast_last(ap, n):
    return ap.unsqueeze(len(ap.shape)).broadcast_to([*ap.shape, n])


def build(nc, a, out, mem_scratch, per):
    with ExitStack() as ctx:
        sg = Signals(nc, ctx, per)

        def sb(name, shape, dt=F32):
            return ctx.enter_context(nc.sbuf_tensor(name, shape, dt))

        x = sb("x", [P, NT, D])
        hT = sb("hT", [P, KC, S])
        hn = sb("hn", [P, NT, D])
        memn = hn[:, :, :].rearrange("p t d -> p (t d)").rearrange("p (c s) -> p c s", c=KC)
        kxT = sb("kxT", [P, KC, S])
        vx = sb("vx", [P, NT, D])
        yT = sb("yT", [P, KC, S])
        ring = [sb(f"ring{i}", [P, 2048]) for i in range(RING)]
        ffn_buf = sb("ffn_buf", [P, 2048])
        sil = ffn_buf[:, 0:1024].rearrange("p (b k s) -> p b k s", b=2, k=2)
        hid = ffn_buf[:, 1024:2048].rearrange("p (b k s) -> p b k s", b=2, k=2)
        sgu = ffn_buf[:, 0:512].rearrange("p (t c) -> p t c", t=NT)
        sgv = ffn_buf[:, 512:1024].rearrange("p (t c) -> p t c", t=NT)
        sgn = ffn_buf[:, 1024:1536].rearrange("p (t c) -> p t c", t=NT)
        sgj = ffn_buf[:, 1536:2048].rearrange("p (t c) -> p t c", t=NT)
        arena_a = sb("arena_a", [P, 6 * (S + 3)])
        z = arena_a[:, :].rearrange("p (b s) -> p b s", b=6)
        ET = arena_a[:, 0:1024].rearrange("p (t h c) -> p t h c", t=NT, h=H)
        arena_b = sb("arena_b", [P, 1536])
        cv = arena_b[:, :].rearrange("p (b s) -> p b s", b=6)
        Tm = arena_b[:, 0:1024].rearrange("p (t h c) -> p t h c", t=NT, h=H)
        us = arena_b[:, 1024:1536].rearrange("p (t c) -> p t c", t=NT)
        qk_buf = sb("qk_buf", [P, 1024])
        qk = qk_buf[:, :].rearrange("p (t h c) -> p t h c", t=NT, h=2 * H)
        Um = qk_buf[:, :].rearrange("p (t h c) -> p t h c", t=NT, h=H)
        Sm_buf = sb("Sm_buf", [P, 1024])
        Sm = Sm_buf[:, :].rearrange("p (t h c) -> p t h c", t=NT, h=H)
        Bm = [sb(f"Bm{i}", [P, NT, H, P]) for i in range(2)]
        g1 = sb("g1", [P, 2048])
        kb, vb, kbg, kd = (g1[:, 512 * i:512 * i + 512].rearrange("p (t c) -> p t c", t=NT) for i in range(4))
        g2 = sb("g2", [P, 2048])
        kT, kbT, qT, qgT = (g2[:, 512 * i:512 * i + 512].rearrange("p (b s) -> p b s", b=2) for i in range(4))
        os_ = kb.rearrange("p t (h c) -> p t h c", h=H)
        PT = g2[:, 0:1536]
        g3 = sb("g3", [P, 2048])
        AE = g3[:, 0:1024].rearrange("p (t h c) -> p t h c", t=NT, h=H)
        AT = g3[:, 1024:2048].rearrange("p (t h c) -> p t h c", t=NT, h=H)
        wT = sb("wT", [P, 2, S])
        qg = wT[:, :, :].rearrange("p b s -> p (b s)").rearrange("p (t c) -> p t c", t=NT)
        vnew = sb("vnew", [P, NT, GW])
        gv = vnew
        state = sb("state", [P, 2, HD])
        state_d = sb("state_d", [P, 2, HD])
        gate = sb("gate", [P, NT, GW])
        R_buf = sb("R_buf", [P, NT * 10 * HD])
        R = R_buf[:, :].rearrange("p (t h c) -> p t h c", t=NT, h=10)
        rel = R_buf[:, 0:1024]
        Pd = R_buf[:, 0:1024]
        dk = sb("dk", [P, NT, GW])
        dv = sb("dv", [P, NT, GW])
        dqT = sb("dqT", [P, 2, S])
        diqT = arena_a[:, 1024:1536].rearrange("p (b s) -> p b s", b=2)
        dikT = sb("dikT", [P, S])
        dkT = sb("dkT", [P, 2, S])
        cT = sb("cT", [P, S])
        score = sb("score", [P, 3 * P])
        work = [score[:, 0:P], score[:, P:3 * P]]
        nbias = sb("nbias", [P, 3 * P])
        cn = nbias[:, 0:NT * LAT].rearrange("p (t c) -> p t c", t=NT)
        nb = [nbias[:, 0:P], nbias[:, P:3 * P]]
        scz = sb("scz", [P, 2, S + 2])
        sch = sb("sch", [P, 2, S])
        sco = sb("sco", [P, 2, S])
        xP = g1[:, 0:1024].rearrange("p (b t s) -> p b t s", b=2, t=NT)
        xPT = g1[:, 1024:2048].rearrange("p (b k s) -> p b k s", b=2, k=2)
        xqT = g2[:, :].rearrange("p (c s) -> p c s", c=KC)
        oT = yT
        rows = sb("rows", [N_ROWS, P])
        cols = sb("cols", [P, N_ROWS])
        wab = sb("wab", [P, KC, 8])
        w_kv = sb("w_kv", [P, 2, GW])
        sgw = sb("sgw", [P, H, P])
        sgwT = arena_a[:, 1024:1536].rearrange("p (h s) -> p h s", h=H)
        scw = sb("scw", [P, 2, 3])
        gcw = sb("gcw", [P, 6, 4])
        bc = sb("bc", [P, GW + HD + HD + 2 * H])
        b_sgn, b_ikn, b_gon, b_alog, b_dt = (bc[:, 0:256], bc[:, 256:320], bc[:, 320:384], bc[:, 384:388],
                                             bc[:, 388:392])
        ident = sb("ident", [P, P])
        zeros = Bm[1][:, 0, 0, :]
        onesm = sb("onesm", [P, P])
        incl = sb("incl", [P, P])
        away = sb("away", [P, P])
        up = sb("up", [P, P])
        same = sb("same", [P, P])
        half = sb("half", [P, NT, P])
        lev = sb("lev", [P, len(LEVELS), P])
        cfill = sb("cfill", [P, 3 * P])
        cfills = [cfill[:, 0:P], cfill[:, P:3 * P]]
        rc = sb("rc", [P, NT, 2 * ROT])
        rs = sb("rs", [P, NT, 2 * ROT])
        rtmp = sb("rtmp", [P, NT, 9, 2 * ROT])
        rtmp2 = sb("rtmp2", [P, NT, 9, 2 * ROT])
        inv = sb("inv", [P, ROT])
        posi = sb("posi", [P, NT], I32)
        posf = sb("posf", [P, NT])
        mhalf = sb("mhalf", [P, 16])
        sm = sb("sm", [P, 320])
        ms, rstd = sm[:, 0:2], sm[:, 2:4]
        msa, rsa = sm[:, 4:8], sm[:, 8:12]
        mss, rss = sm[:, 12:14], sm[:, 14:16]
        l2s, l2r = sm[:, 16:32], sm[:, 32:48]
        ab = sm[:, 48:64].rearrange("p (t c) -> p t c", t=NT)
        ga1, ga2, ga3 = sm[:, 64:72], sm[:, 72:80], sm[:, 80:88]
        gg_, beta = sm[:, 88:96], sm[:, 96:104]
        gc, glast = sm[:, 104:112], sm[:, 112:120]
        ngc, egc, ekd = sm[:, 120:128], sm[:, 128:136], sm[:, 136:144]
        alog = sm[:, 144:148]
        egl = sm[:, 148:164].rearrange("p (c h) -> p c h", c=NCH)
        egl2 = sm[:, 164:172].rearrange("p (c b) -> p c b", c=NCH)
        iw = sm[:, 172:180].rearrange("p (t h) -> p t h", t=NT)
        m8 = sm[:, 180:196].rearrange("p (t k) -> p t k", t=NT)
        dmx, dsum = sm[:, 196:204], sm[:, 204:212]
        xmx, xnb, xsum = sm[:, 212:220], sm[:, 220:228], sm[:, 228:236]
        gos, gor = sm[:, 236:244], sm[:, 244:252]
        msb = sm[:, 252:268]

        bank = [ctx.enter_context(nc.psum_tensor(f"bank{i}", [P, 512], F32)) for i in range(8)]

        def b2(i):
            return bank[i][:, :].rearrange("p (k s) -> p k s", k=2)

        def b4(i):
            return bank[i][:, :].rearrange("p (k s) -> p k s", k=4)

        wide = {n: a[n].rearrange("l (c p) n -> p l c n", p=P)
                for n in ("ffn1_wg", "ffn1_wu", "ffn1_wd", "ffn2_wg", "ffn2_wu", "ffn2_wd", "w_mix_in",
                          "w_mix_out", "xa_wq", "xa_wk", "xa_wv", "xa_wo")}
        x_v = a["x"].rearrange("b (t p) d -> p (b t) d", p=P)
        mem_v = a["mem"].rearrange("b (t p) d -> p (b t) d", p=P)
        out_v = out.rearrange("b (t p) d -> p (b t) d", p=P)

        landed = [sg.sem(f"unit_landed{i}") for i in range(RING)]
        used = [sg.sem(f"unit_used{i}") for i in range(RING)]

        def uses(slot):
            return len(range(slot, N_UNITS, RING))

        def unit_landed(pos, layer, it=0):
            s = pos % RING
            return landed[s], (layer * uses(s) + pos // RING + it) * 16 + 16

        def unit_used(pos, layer, it=0):
            s = pos % RING
            return used[s], layer * uses(s) + pos // RING + it + 1

        def unit_free(pos, layer, it=0):
            s = pos % RING
            return used[s], layer * uses(s) + pos // RING + it

        def as_cols(pos, w=256):
            return ring[pos % RING][:, 0:KC * w].rearrange("p (c n) -> p c n", c=KC)

        def as_rows(pos):
            return ring[pos % RING][:, :].rearrange("p (c n) -> p c n", c=2)

        x_loaded, mem_stored, out_done = sg.sem("x_loaded"), sg.sem("mem_stored"), sg.sem("out_done")
        consts_done, rope_loaded = sg.sem("consts_done"), sg.sem("rope_loaded")
        fgain_loaded, mem_loaded, par_loaded = sg.sem("fgain_loaded"), sg.sem("mem_loaded"), sg.sem("par_loaded")
        N_PARAMS = 18

        def apart(eng):
            eng.sem_inc(sg.sem("waited"), 1)

        block = ctx.enter_context(nc.Block())

        @block.sync
        def _(sp):
            sp.dma_start(hn[:, :, :], mem_v).then_inc(x_loaded, 16)
            sp.dma_start(x[:, :, :], x_v).then_inc(x_loaded, 16)
            sp.dma_start(posi[:, :], a["positions"].rearrange("b (t p) -> p (b t)", p=P),
                         allow_slow_non_contiguous=True).then_inc(rope_loaded, 16)

            def params(l):
                def load(dst, src):
                    sp.dma_start(dst, src).then_inc(par_loaded, 16)
                sp.wait_ge(*sg.at("params_used", l, 0))
                apart(sp)
                for r, n in ((R_FFN1, "ffn1_norm"), (R_MIX, "mix_norm"), (R_XA, "xa_norm"), (R_MEM, "mem_norm"),
                             (R_FFN2, "ffn2_norm")):
                    load(rows[r:r + KC, :], a[n].rearrange("l (c p) -> c l p", p=P)[:, l, :])
                load(rows[R_SGB:R_SGB + H, :], a["sg_b"].rearrange("l h t -> h l t")[:, l, :])
                load(rows[R_KV:R_KV + 1, :], a["kv_norm"][bass.ds(l, 1), :])
                load(wab[:, :, :], wide["w_mix_in"][:, l, :, C_GA:C_GA + 8])
                load(w_kv[:, 0, :], a["w_uk"].rearrange("l p n -> p l n")[:, l, :])
                load(w_kv[:, 1, :], a["w_uv"].rearrange("l p n -> p l n")[:, l, :])
                load(sgw[:, :, :], a["sg_w"].rearrange("l h t s -> t l h s")[:, l, :, :])
                load(scw[:, :, :], a["sc_conv"].rearrange("l (b p) j -> p l b j", p=P)[:, l, :, :])
                load(gcw[:, :, :], a["gdn_conv"].rearrange("l (b p) j -> p l b j", p=P)[:, l, :, :])
                for dst, n, w in ((b_sgn, "sg_norm", GW), (b_ikn, "idx_k_norm", HD), (b_gon, "gdn_out_norm", HD),
                                  (b_alog, "gdn_a_log", H), (b_dt, "gdn_dt_bias", H)):
                    load(dst, a[n][bass.ds(l, 1), :].broadcast_to([P, w]))

            def unit(dst, src, pos, l, it=0):
                sp.wait_ge(*unit_free(pos, l, it))
                apart(sp)
                sp.dma_start(dst, src).then_inc(landed[pos % RING], 16)

            def ffn_units(l, n, base):
                def gate_up(pos, c0, it=0):
                    for i, w in enumerate(("wg", "wu")):
                        unit(as_cols(pos + i), wide[f"{n}_{w}"][:, l, :, c0], pos + i, l, it)

                def down(pos, r0, it=0):
                    unit(as_rows(pos), wide[f"{n}_wd"][:, l, r0, :], pos, l, it)

                gate_up(base, slice(0, 256))
                gate_up(base + 2, slice(256, 512))
                down(base + 4, slice(0, 2))
                gate_up(base + 5, slice(512, 768))
                down(base + 7, slice(2, 4))
                with sp.Fori(1, PAIRS) as it:
                    gate_up(base + 2, bass.ds(it * 512 + 256, 256), it)
                    down(base + 4, bass.ds(it * 4, 2), it)
                    gate_up(base + 5, bass.ds(it * 512 + 512, 256), it)
                    down(base + 7, bass.ds(it * 4 + 2, 2), it)
                down(base + 2 + 6 * PAIRS, slice(2 * STEPS - 2, 2 * STEPS))

            with sp.Fori(0, DEPTH) as l:
                params(l)
                ffn_units(l, "ffn1", U_FFN1)
                for i, (c, w) in enumerate(MIX_COLS):
                    unit(as_cols(U_MIX + i, w), wide["w_mix_in"][:, l, :, c:c + w], U_MIX + i, l)
                    if i == 5:
                        sp.wait_ge(*sg.at("hT_transposed", l, 8))
                        sp.wait_ge(mem_stored, 16)
                        sp.dma_start(memn, mem_scratch).then_inc(mem_loaded, 16)
                for u, n in ((U_XK, "xa_wk"), (U_XV, "xa_wv")):
                    for i in range(4):
                        unit(as_cols(u + i), wide[n][:, l, :, 256 * i:256 * i + 256], u + i, l)
                for i in range(4):
                    unit(as_rows(U_OUT + i), wide["w_mix_out"][:, l, 2 * i:2 * i + 2, :], U_OUT + i, l)
                for i in range(4):
                    unit(as_cols(U_XQ + i), wide["xa_wq"][:, l, :, 256 * i:256 * i + 256], U_XQ + i, l)
                for i in range(4):
                    unit(as_rows(U_XO + i), wide["xa_wo"][:, l, 2 * i:2 * i + 2, :], U_XO + i, l)
                ffn_units(l, "ffn2", U_FFN2)
            sp.wait_ge(*sg.at("x_updated", DEPTH - 1))
            sp.dma_start(vx[:, 0, :], a["final_norm"].rearrange("(o d) -> o d", o=1).broadcast_to([P, D]))\
                .then_inc(fgain_loaded, 16)
            for t in range(NT):
                sp.wait_ge(sg.sem("out_ready"), t + 1)
                sp.dma_start(out_v[:, t, :], hn[:, t, :]).then_inc(out_done, 16)
            sp.wait_ge(out_done, 16 * NT)

        @block.tensor
        def _(pe):
            def norm_transposes(ready):
                for t in range(NT):
                    pe.wait_ge(*ready(t))
                    for c in range(KC):
                        tr = pe.transpose(b2(4 + c // 2)[:, c % 2, t * P:t * P + P],
                                          hn[:, t, c * P:c * P + P], ident[:, :])
                        if t == NT - 1 and c % 2:
                            yield tr

            def norm(l, k):
                for tr in norm_transposes(lambda t: sg.at("hn_ready", l, NT * k + t + 1)):
                    tr.then_inc(sg.inc("hT_transposed"), 1)
                pe.wait_ge(*sg.at("hT_scalar", l, 4 * k + 4))
                pe.wait_ge(*sg.at("hT_vector", l, 2 * k + 2))

            pe.wait_ge(consts_done, 1)
            for tr in norm_transposes(lambda t: (sg.sem("mem_hn_ready"), t + 1)):
                tr.then_inc(sg.sem("mem_transposed"), 1)

            def feature_major(pos, bk, src, l):
                pe.wait_ge(*unit_landed(pos, l))
                w = as_cols(pos)
                for b in range(2):
                    for c in range(KC):
                        mm = pe.matmul(b2(bk)[:, b, :], w[:, c, b * P:b * P + P], src[:, c, :],
                                       start=(c == 0), stop=(c == KC - 1))
                mm.then_inc(used[pos % RING], 1)

            def token_major(pos, bk, src, l, w=256):
                pe.wait_ge(*unit_landed(pos, l))
                wt = as_cols(pos, w)
                for t in range(NT):
                    for c in range(KC):
                        mm = pe.matmul(b2(bk)[:, t, 0:w], src[:, c, t * P:t * P + P], wt[:, c, :],
                                       start=(c == 0), stop=(c == KC - 1))
                mm.then_inc(used[pos % RING], 1)

            def rows_product(pos, src, c0, bk, l, first, last, it=0):
                pe.wait_ge(*unit_landed(pos, l, it))
                w = as_rows(pos)
                for t in range(NT):
                    for n in range(2):
                        for c in range(2):
                            mm = pe.matmul(bank[bk + 2 * t + n][:, :], src[:, c0 + c, t * P:t * P + P],
                                           w[:, c, 512 * n:512 * n + 512],
                                           start=(first and c == 0), stop=(last and c == 1),
                                           skip_group_check=True)
                mm.then_inc(used[pos % RING], 1)

            def ffn(l, which, base):
                ready = sg.sem("hid_ready")
                half_done = sg.sem("first_block_done")

                def hid_at(step):
                    return l * 4 * STEPS + which * 2 * STEPS + 2 * step

                def gate_up(pos, par, step, it=0):
                    pe.wait_ge(*unit_landed(pos, l, it))
                    pe.wait_ge(*unit_landed(pos + 1, l, it))
                    if not (isinstance(step, int) and step < 2):
                        pe.wait_ge(ready, hid_at(step - 1))
                    for b in range(2):
                        for i in range(2):
                            w = as_cols(pos + i)
                            for c in range(KC):
                                mm = pe.matmul(b2(4 + 2 * par + b)[:, i, :], w[:, c, b * P:b * P + P], hT[:, c, :],
                                               start=(c == 0), stop=(c == KC - 1))
                            if b == 0 and i == 1:
                                mm.then_inc(half_done, 1)
                            if b == 1:
                                mm.then_inc(used[(pos + i) % RING], 1)

                def down(pos, par, step, it=0, first=False, last=False):
                    pe.wait_ge(ready, hid_at(step + 1))
                    rows_product(pos, hid[:, par], 0, 0, l, first, last, it)

                gate_up(base, 0, 0)
                gate_up(base + 2, 1, 1)
                down(base + 4, 0, 0, first=True)
                gate_up(base + 5, 0, 2)
                down(base + 7, 1, 1)
                with pe.Fori(1, PAIRS) as it:
                    gate_up(base + 2, 1, it * 2 + 1, it)
                    down(base + 4, 0, it * 2, it)
                    gate_up(base + 5, 0, it * 2 + 2, it)
                    down(base + 7, 1, it * 2 + 1, it)
                down(base + 2 + 6 * PAIRS, 0, STEPS - 1, last=True)

            def hs(h):
                return slice(HD * (h % 2), HD * (h % 2) + HD)

            def mixer(l):
                feature_major(U_GQ, 0, hT, l)
                feature_major(U_GK, 1, hT, l)
                feature_major(U_GV, 2, hT, l)
                for t in range(NT):
                    for c in range(KC):
                        mm = pe.matmul(bank[3][:, 8 * t:8 * t + 8], hT[:, c, t * P:t * P + P], wab[:, c, :],
                                       start=(c == 0), stop=(c == KC - 1))
                mm.then_inc(sg.inc("ab_projected"), 1)
                token_major(U_Q, 4, hT, l)
                token_major(U_CKV, 5, hT, l)
                token_major(U_IQ1, 6, hT, l, W_IQ1)
                pe.wait_ge(*sg.at("g_ready", l))
                pe.matmul(bank[3][:, 32:40], incl[:, :], gg_, start=True, stop=True)
                pe.matmul(bank[3][:, 64:72], same[:, :], gg_, start=True, stop=True)
                for c in range(NCH):
                    mm = pe.matmul(bank[3][:, 96 + 4 * c:100 + 4 * c], half[:, c % 2, :],
                                   gg_[:, 4 * (c // 2):4 * (c // 2) + 4], start=True, stop=True)
                mm.then_inc(sg.inc("gates_summed"), 1)
                token_major(U_SGV, 7, hT, l)
                pe.wait_ge(*sg.at("silu_done", l))
                for t in range(NT):
                    for b in range(4):
                        tr = pe.transpose(b4(t)[:, b, :], cv[:, b, t * P:t * P + P], ident[:, :])
                    tr.then_inc(sg.inc("qkv_transposed"), 1)
                for t in range(NT):
                    for b in range(2):
                        tr = pe.transpose(b4(2)[:, 2 * t + b, :], cv[:, 4 + b, t * P:t * P + P], ident[:, :])
                tr.then_inc(sg.inc("qkv_transposed"), 1)
                pe.wait_ge(*sg.at("cn_ready", l))
                pe.wait_ge(*sg.at("q_copied", l))
                for t in range(NT):
                    tr = pe.transpose(bank[4][:, t * P:t * P + P], cn[:, t, :], ident[:, :])
                tr.then_inc(sg.inc("c_transposed"), 1)
                pe.wait_ge(*sg.at("iq1_copied", l))
                token_major(U_SGU, 6, hT, l)
                pe.wait_ge(*sg.at("cT_ready", l))
                for t in range(NT):
                    pe.matmul(bank[4 + t][:, :], cT[:, t * P:t * P + P],
                              w_kv[:, :, :].rearrange("p i n -> p (i n)"), start=True, stop=True)\
                        .then_inc(sg.inc("kv_up"), 1)
                pe.wait_ge(*sg.at("gm_ready", l))
                pe.wait_ge(*sg.at("sums_copied", l))
                pe.matmul(bank[3][:, :], onesm[:, :], Sm_buf[:, 0:512], start=True, stop=True)\
                    .then_inc(sg.inc("gc_rows"), 1)
                pe.wait_ge(*sg.at("v_copied", l))
                pe.matmul(bank[2][:, :], onesm[:, :], Sm_buf[:, 512:1024], start=True, stop=True)\
                    .then_inc(sg.inc("gc_rows"), 1)
                pe.wait_ge(*sg.at("sgv_gelu", l))
                feature_major(U_SCC, 7, hT, l)
                for i, (src, bk, ev) in enumerate(((lambda t, b: qk[:, t, 4 + 2 * b:6 + 2 * b, :].rearrange("p h c -> p (h c)"), 0, "qk_scaled"),
                                                   (lambda t, b: kb[:, t, b * P:b * P + P], 1, "kb_ready"),
                                                   (lambda t, b: qk[:, t, 2 * b:2 * b + 2, :].rearrange("p h c -> p (h c)"), 0, "qk_scaled"),
                                                   (lambda t, b: qg[:, t, b * P:b * P + P], 1, "qg_ready"))):
                    pe.wait_ge(*sg.at(ev, l))
                    if i >= 2:
                        pe.wait_ge(*sg.at("gT_copied", l, i - 1))
                    for b in range(2):
                        for t in range(NT):
                            tr = pe.transpose(b2(bk)[:, b, t * P:t * P + P], src(t, b), ident[:, :])
                    tr.then_inc(sg.inc("gT_transposed"), 1)
                pe.wait_ge(*sg.at("sgu_gelu", l))
                feature_major(U_SCH, 6, hT, l)
                pe.wait_ge(*sg.at("rope_q", l))
                pe.wait_ge(*sg.at("kv_copied", l))
                for bk, s0, n in ((4, 0, 2), (5, 4, 2), (4, 8, 1), (5, -1, 2)):
                    if (bk, s0) == (4, 8):
                        pe.wait_ge(*sg.at("dT_copied", l, 1))
                    if s0 < 0:
                        pe.wait_ge(*sg.at("dT_copied", l, 2))
                        pe.wait_ge(*sg.at("rope_k", l))
                    for b in range(n):
                        for t in range(NT):
                            src = (dk[:, t, b * P:b * P + P] if s0 < 0 else
                                   R[:, t, s0 + 2 * b:s0 + 2 * b + 2, :].rearrange("p h c -> p (h c)"))
                            tr = pe.transpose(b2(bk)[:, b, t * P:t * P + P], src, ident[:, :])
                    tr.then_inc(sg.inc("dT_transposed"), 1)
                pe.wait_ge(*sg.at("gT_copied", l))
                pe.wait_ge(*sg.at("ET_read", l))
                for t in range(NT):
                    for odd in range(2):
                        for i, src in enumerate((kbT, qT)):
                            for b in range(2):
                                h = 2 * b + odd
                                mm = pe.matmul(b4(2 * t + odd)[:, 2 * i + b, :], kT[hs(h), b, t * P:t * P + P],
                                               src[hs(h), b, t * P:t * P + P], start=True, stop=True)
                        mm.then_inc(sg.inc("kq_done"), 1)
                pe.wait_ge(*sg.at("dT_copied", l))
                for t in range(NT):
                    n = P * (t + 1)
                    for odd in range(2):
                        if t:
                            pe.wait_ge(*sg.at("relu_done", l, odd + 1))
                        for b in range(2):
                            h = 2 * b + odd
                            mm = pe.matmul(bank[4 + odd][:, n * b:n * b + n], diqT[hs(h), b, t * P:t * P + P],
                                           dikT[hs(h), 0:n], start=True, stop=True)
                        mm.then_inc(sg.inc("index_scores"), 1)
                pe.wait_ge(*sg.at("scc_copied", l))
                feature_major(U_SCB, 7, hT, l)

                def level_u(i, t):
                    pe.wait_ge(*sg.at("B_ready", l, NT * i + t + 1))
                    if i:
                        pe.wait_ge(*sg.at("TS_ready", l, 2 * (NT * (i - 1) + t) + 2))
                    else:
                        pe.wait_ge(*sg.at("AE_ready", l))
                    for h in range(H):
                        mm = pe.matmul(b4(2 * t)[:, h, :], Bm[i % 2][:, t, h, :],
                                       ident[:, :] if i == 0 else Tm[:, t, h, :], start=True, stop=True)
                    mm.then_inc(sg.inc("U_done"), 1)

                def level_ts(i, t):
                    pe.wait_ge(*sg.at("U_copied", l, NT * (i - 1) + t + 1))
                    if i < len(LEVELS) - 1:
                        for h in range(H):
                            mm = pe.matmul(b4(2 * t + 1)[:, h, :], Sm[:, t, h, :], Um[:, t, h, :], start=True, stop=True)
                        mm.then_inc(sg.inc("TS_done"), 1)
                    for h in range(H):
                        mm = pe.matmul(b4(2 * t)[:, h, :], Um[:, t, h, :], Sm[:, t, h, :], start=True, stop=True)
                    mm.then_inc(sg.inc("TS_done"), 1)

                fillers = {1: lambda: (pe.wait_ge(*sg.at("sch_copied", l)), token_major(U_GG, 6, hT, l)),
                           2: lambda: xa_key(0), 3: lambda: xa_key(1), 4: lambda: xa_key(2), 5: lambda: xa_key(3)}

                def xa_bank(i):
                    if i == 0:
                        pe.wait_ge(*sg.at("scb_copied", l))
                        pe.wait_ge(*sg.at("memn_ready", l))
                    elif i == 1:
                        pe.wait_ge(*sg.at("gate_read", l))
                    else:
                        pe.wait_ge(*sg.at("xkv_copied", l, i - 1))
                    return 7 - i % 2

                def xa_key(i):
                    feature_major(U_XK + i, xa_bank(i), memn, l)

                def xa_value(i):
                    token_major(U_XV + i, xa_bank(4 + i), memn, l)

                for t in range(NT):
                    level_u(0, t)
                for i in range(1, len(LEVELS)):
                    for t in range(NT):
                        level_u(i, t)
                    fillers[i]()
                    for t in range(NT):
                        level_ts(i, t)
                xa_value(0)
                pe.wait_ge(*sg.at("TS_ready", l))
                for t in range(NT):
                    for h in range(H):
                        mm = pe.matmul(b2(0)[:, t, HD * h:HD * h + HD], Sm[:, t, h, :],
                                       vb[:, t, HD * h:HD * h + HD], start=True, stop=True)
                mm.then_inc(sg.inc("u_done"), 1)
                for t in range(NT):
                    for h in range(H):
                        mm = pe.matmul(b2(1)[hs(h), h // 2, t * P:t * P + P], kbg[:, t, HD * h:HD * h + HD],
                                       Sm[:, t, h, :], start=True, stop=True)
                mm.then_inc(sg.inc("w_done"), 1)
                xa_value(1)
                def chunk_read(c):
                    t, r = c // 2, CH * (c % 2)
                    pe.wait_ge(*sg.at("uw_copied", l))
                    pe.wait_ge(*sg.at("state_ready", l, c + 1))
                    if c:
                        pe.wait_ge(*sg.at("qs_copied", l, 2 * c))
                    apart(pe)
                    for odd in range(2):
                        for i, src in enumerate((wT, qgT)):
                            for b in range(2):
                                rows_ = slice(HD * odd, HD * odd + HD)
                                mm = pe.matmul(bank[odd][r:r + CH, P * i + HD * b:P * i + HD * b + HD],
                                               src[rows_, b, t * P + r:t * P + r + CH], state[rows_, b, :],
                                               start=True, stop=True)
                    mm.then_inc(sg.inc("ws_done"), 1)

                def chunk_write(c):
                    t, r = c // 2, CH * (c % 2)
                    pe.wait_ge(*sg.at("vnew_ready", l, 2 * c + 2))
                    apart(pe)
                    for h in range(H):
                        mm = pe.matmul(bank[2][hs(h), HD * (h // 2):HD * (h // 2) + HD], kd[r:r + CH, t, HD * h:HD * h + HD],
                                       vnew[r:r + CH, t, HD * h:HD * h + HD], start=True, stop=True)
                    mm.then_inc(sg.inc("kv_done"), 1)
                    for h in range(H):
                        mm = pe.matmul(b2(3)[r:r + CH, t, HD * h:HD * h + HD], AT[r:r + CH, t, h, r:r + CH],
                                       vnew[r:r + CH, t, HD * h:HD * h + HD], start=True, stop=True)
                    mm.then_inc(sg.inc("o_done"), 1)

                def dsa_logits(t):
                    pe.wait_ge(*(sg.at("logits_read", l, 2) if t else sg.at("relu_done", l)))
                    n = P * (t + 1)
                    for odd in range(2):
                        for b in range(2):
                            h = 2 * b + odd
                            mm = pe.matmul(bank[4 + odd][:, n * b:n * b + n], dqT[hs(h), b, t * P:t * P + P],
                                           dkT[hs(h), b, 0:n], start=True, stop=True)
                    mm.then_inc(sg.inc("logits_done"), 1)

                def dsa_transposes(i):
                    if i == 0:
                        pe.wait_ge(*sg.at("probs_ready", l, 1))
                        for h in range(H):
                            tr = pe.transpose(b4(7)[:, h, :], Pd[:, P * h:P * h + P], ident[:, :])
                    else:
                        pe.wait_ge(*sg.at("probs_ready", l, 2))
                        pe.wait_ge(*sg.at("logits_read", l))
                        for h in range(H):
                            tr = pe.transpose(b4(5 if i == 1 else 4)[:, h, :],
                                              Pd[:, 2 * P * h + P * (i - 1):2 * P * h + P * i], ident[:, :])
                    tr.then_inc(sg.inc("PT_transposed"), 1)

                def dsa_values():
                    pe.wait_ge(*sg.at("PT_copied", l))
                    for i, h in enumerate((0, 2, 1, 3)):
                        pe.matmul(b2(5)[hs(h), h // 2, 0:P], dv[:, 0, HD * h:HD * h + HD], PT[:, P * i:P * i + P],
                                  start=True, stop=True)
                        for k in range(2):
                            mm = pe.matmul(b2(5)[hs(h), h // 2, P:2 * P], dv[:, k, HD * h:HD * h + HD],
                                           PT[:, 512 * (k + 1) + P * i:512 * (k + 1) + P * i + P],
                                           start=(k == 0), stop=(k == 1))
                    mm.then_inc(sg.inc("dsa_out"), 1)

                chunk_read(0)
                dsa_logits(0)
                chunk_write(0)
                chunk_read(1)
                dsa_logits(1)
                xa_value(2)
                chunk_write(1)
                chunk_read(2)
                xa_value(3)
                chunk_write(2)
                chunk_read(3)
                pe.wait_ge(*sg.at("xkv_copied", l, 7))
                for h in range(H):
                    tr = pe.transpose(b4(7)[:, h, :], sgw[:, h, :], ident[:, :])
                tr.then_inc(sg.inc("sgw_transposed"), 1)
                chunk_write(3)
                pe.wait_ge(*sg.at("xkv_copied", l))
                pe.wait_ge(*sg.at("sgwT_ready", l))
                pe.wait_ge(*sg.at("sgn_ready", l))
                for t in range(NT):
                    for h in range(H):
                        mm = pe.matmul(b2(6)[:, t, HD * h:HD * h + HD], sgwT[:, h, :], sgn[:, t, HD * h:HD * h + HD],
                                       start=True, stop=True)
                mm.then_inc(sg.inc("sg_mixed"), 1)
                dsa_transposes(0)
                pe.wait_ge(*sg.at("sg_out", l))
                for b in range(2):
                    for t in range(NT):
                        tr = pe.transpose(b2(2)[:, b, t * P:t * P + P], sgj[:, t, b * P:b * P + P], ident[:, :])
                tr.then_inc(sg.inc("sg_transposed"), 1)
                dsa_transposes(1)
                dsa_transposes(2)
                dsa_values()
                pe.wait_ge(*sg.at("gdn_out", l))
                for b in range(2):
                    for t in range(NT):
                        tr = pe.transpose(b2(0)[:, b, t * P:t * P + P], vnew[:, t, b * P:b * P + P], ident[:, :])
                tr.then_inc(sg.inc("gdn_transposed"), 1)
                pe.wait_ge(*sg.at("yT_ready", l, 3))
                pe.wait_ge(*sg.at("sc_out", l))
                rows_product(U_OUT, yT, 0, 4, l, True, False)
                rows_product(U_OUT + 1, yT, 2, 4, l, False, False)
                rows_product(U_OUT + 2, yT, 4, 4, l, False, False)
                rows_product(U_OUT + 3, yT, 6, 4, l, False, True)

            def cross(l):
                def queries(h):
                    feature_major(U_XQ + h, 4 * (h % 2), hT, l)

                def logits(h):
                    pe.wait_ge(*sg.at("xq_copied", l, h + 1))
                    bk = (1, 5, 1, 0)[h]
                    if h == 2:
                        pe.wait_ge(*sg.at("xexp_done", l, NT))
                    for t in range(NT):
                        for b in range(2):
                            mm = pe.matmul(b2(bk)[:, t, :], xqT[:, 2 * h + b, t * P:t * P + P], kxT[:, 2 * h + b, :],
                                           start=(b == 0), stop=(b == 1))
                    mm.then_inc(sg.inc("xlogits"), 1)

                def transposes(h):
                    pe.wait_ge(*sg.at("xprobs", l, h + 1))
                    if h:
                        pe.wait_ge(*sg.at("xPT_copied", l, h))
                    for k in range(2):
                        for t in range(NT):
                            tr = pe.transpose(b2(2)[:, k, t * P:t * P + P], xP[:, h % 2, t, k * P:k * P + P], ident[:, :])
                    tr.then_inc(sg.inc("xPT"), 1)

                def values(h):
                    pe.wait_ge(*sg.at("xPT_copied", l, h + 1))
                    if h:
                        pe.wait_ge(*sg.at("oT_copied", l, h))
                    for b in range(2):
                        for k in range(2):
                            mm = pe.matmul(b2(3)[:, b, :], vx[:, k, 256 * h + b * P:256 * h + b * P + P],
                                           xPT[:, h % 2, k, :], start=(k == 0), stop=(k == 1))
                    mm.then_inc(sg.inc("xvalues"), 1)

                def project(h):
                    pe.wait_ge(*sg.at("oT_copied", l, h + 1))
                    if h == 0:
                        pe.wait_ge(*sg.at("xq_copied", l))
                        pe.wait_ge(*sg.at("xexp_done", l, 2 * NT))
                    rows_product(U_XO + h, oT, 2 * h, 4, l, h == 0, h == H - 1)

                queries(0), queries(1), logits(0), queries(2), logits(1), transposes(0), queries(3), values(0)
                logits(2), transposes(1), project(0), values(1), logits(3), transposes(2), project(1)
                values(2), transposes(3), project(2), values(3), project(3)

            with pe.Fori(0, DEPTH) as l:
                pe.wait_ge(par_loaded, (l + 1) * N_PARAMS * 16)
                pe.wait_ge(sg.sem("memT_copied"), 4)
                pe.wait_ge(sg.sem("hid_ready"), l * 4 * STEPS)
                apart(pe)
                pe.transpose(bank[7][:, 0:N_ROWS], rows[:, :], ident[0:N_ROWS, 0:N_ROWS])\
                    .then_inc(sg.inc("rows_transposed"), 1)
                pe.wait_ge(*sg.at("cols_ready", l))
                norm(l, 0)
                ffn(l, 0, U_FFN1)
                norm(l, 1)
                mixer(l)
                norm(l, 2)
                cross(l)
                norm(l, 3)
                ffn(l, 1, U_FFN2)

        @block.scalar
        def _(act):
            def mean_squares(src, ready, done):
                for t in range(NT):
                    act.wait_ge(*ready(t))
                    act.activation(hn[:, t, :], src[:, t, :], ACT.Square, scale=float(D) ** -0.5,
                                   accum_out=ms[:, t:t + 1]).then_inc(done, 1)

            def link(ins, l):
                ins.then_inc(sg.inc("scalar_link"), 1)
                act.wait_ge(*sg.at("scalar_link", l, sg.counts["scalar_link"]))

            for t in range(NT):
                act.wait_ge(x_loaded, 32)
                act.activation(yT[:, 4 * t:4 * t + 4, :].rearrange("p c s -> p (c s)"), hn[:, t, :], ACT.Square,
                               scale=float(D) ** -0.5, accum_out=ms[:, t:t + 1]).then_inc(sg.sem("mem_ms"), 1)
            for i in range(4):
                act.wait_ge(sg.sem("mem_transposed"), i + 1)
                act.activation(hT[:, 2 * i:2 * i + 2, :], b2(4 + i), ACT.Copy).then_inc(sg.sem("memT_copied"), 1)
            act.wait_ge(sg.sem("memT_copied"), 4)
            act.dma_start(mem_scratch, hT[:, :, :]).then_inc(mem_stored, 16)
            act.wait_ge(sg.sem("angles_ready"), 2)
            act.activation(rs[:, :, ROT:2 * ROT], rtmp[:, :, 0, 0:ROT], ACT.Sin).then_inc(sg.sem("trig_done"), 1)
            act.activation(rc[:, :, 0:ROT], rtmp[:, :, 1, 0:ROT], ACT.Sin).then_inc(sg.sem("trig_done"), 1)
            act.wait_ge(sg.sem("trig_done"), 2)
            act.activation(rs[:, :, 0:ROT], rs[:, :, ROT:2 * ROT], ACT.Copy, scale=-1.0).then_inc(sg.sem("trig_done"), 1)
            act.activation(rc[:, :, ROT:2 * ROT], rc[:, :, 0:ROT], ACT.Copy).then_inc(sg.sem("trig_done"), 1)
            act.wait_ge(mem_stored, 16)

            def norm(l, k, row):
                if k == 0:
                    act.wait_ge(x_loaded, 32)
                for t in range(NT):
                    act.wait_ge(*sg.at("x_updated", l, 4 * k + (2 * t + 2 if k else 0) - (4 if k else 0)))
                    act.activation(hn[:, t, :], x[:, t, :], ACT.Square, scale=float(D) ** -0.5,
                                   accum_out=ms[:, t:t + 1]).then_inc(sg.inc("ms_ready"), 1)
                for i in range(2):
                    act.wait_ge(*sg.at("hT_transposed", l, 4 * k + i + 1))
                    for j in range(2):
                        c = 2 * i + j
                        act.activation(hT[:, c, :], b2(4 + i)[:, j, :], ACT.Copy, scale=cols[:, row + c:row + c + 1])\
                            .then_inc(sg.inc("hT_scalar"), 1)

            def ffn(l, which, base):
                done, read = sg.sem("silu_ready"), sg.sem("hid_ready")

                def step(par, s, pos, it=0):
                    n = l * 4 * STEPS + which * 2 * STEPS + 2 * s
                    if isinstance(s, int) and s < 2:
                        act.wait_ge(*sg.at("hT_vector", l, 2 + 6 * which))
                    else:
                        act.wait_ge(read, n - 2)
                    act.wait_ge(sg.sem("first_block_done"), l * 2 * STEPS + which * STEPS + s + 1)
                    act.activation(sil[:, par, 0, :], b2(4 + 2 * par)[:, 0, :], ACT.Silu).then_inc(done, 1)
                    act.wait_ge(*unit_used(pos + 1, l, it))
                    act.activation(sil[:, par, 1, :], b2(5 + 2 * par)[:, 0, :], ACT.Silu).then_inc(done, 1)

                step(0, 0, base)
                step(1, 1, base + 2)
                step(0, 2, base + 5)
                with act.Fori(1, PAIRS) as it:
                    step(1, it * 2 + 1, base + 2, it)
                    step(0, it * 2 + 2, base + 5, it)

            def mixer(l):
                def copy(dst, src, name, func=ACT.Copy, **kw):
                    act.activation(dst, src, func, **kw).then_inc(sg.inc(name), 1)

                act.wait_ge(*sg.at("pads_ready", l))
                for i, u in enumerate((U_GQ, U_GK, U_GV)):
                    act.wait_ge(*unit_used(u, l))
                    copy(z[:, 2 * i:2 * i + 2, 3:3 + S], b2(i), "z_copied")
                act.wait_ge(*sg.at("ab_projected", l))
                copy(ab, bank[3][:, 0:16].rearrange("p (t c) -> p t c", t=NT), "ab_copied")
                act.activation(alog, b_alog, ACT.Exp)
                act.wait_ge(*sg.at("soft_in", l))
                act.activation(ga2, ga2, ACT.Exp)
                link(act.activation(beta, beta, ACT.Exp, scale=-1.0), l)
                copy(ga3, ga2, "soft_ln", ACT.Ln, bias=1.0)
                act.wait_ge(*unit_used(U_Q, l))
                copy(R[:, :, 0:4, :], b2(4).rearrange("p t (h c) -> p t h c", h=4), "q_copied")
                act.wait_ge(*unit_used(U_CKV, l))
                for t in range(NT):
                    copy(cn[:, t, :], b2(5)[:, t, 0:LAT], "msa_ready", ACT.Square, scale=float(LAT) ** -0.5,
                         accum_out=msa[:, t:t + 1])
                copy(R[:, :, 4:6, :], b2(5)[:, :, LAT:256].rearrange("p t (h c) -> p t h c", h=2), "iq0_copied")
                act.wait_ge(*unit_used(U_IQ1, l))
                for t in range(NT):
                    copy(R[:, t, 8, :], b2(6)[:, t, P:P + HD], "msa_ready", ACT.Square, scale=float(HD) ** -0.5,
                         accum_out=msa[:, 2 + t:3 + t])
                copy(R[:, :, 6:8, :], b2(6)[:, :, 0:P].rearrange("p t (h c) -> p t h c", h=2), "iq1_scalar")
                copy(iw, b2(6)[:, :, P + HD:P + HD + H], "iq1_scalar", scale=0.0625)
                for i in range(3):
                    act.wait_ge(*sg.at("conv_v", l) if i == 2 else sg.at("conv_qk", l, 2 * i + 2))
                    copy(cv[:, 2 * i:2 * i + 2, :], cv[:, 2 * i:2 * i + 2, :], "silu_done", ACT.Silu)
                act.wait_ge(*unit_used(U_SGV, l))
                copy(sgv, b2(7), "sgv_gelu", ACT.Gelu_apprx_tanh)
                act.wait_ge(*sg.at("sgv_gelu", l))
                for t in range(NT):
                    copy(sgn[:, t, :], sgv[:, t, :], "mss_ready", ACT.Square, scale=float(GW) ** -0.5,
                         accum_out=mss[:, t:t + 1])
                act.wait_ge(*unit_used(U_SGU, l))
                copy(sgu, b2(6), "sgu_gelu", ACT.Gelu_apprx_tanh)
                for t in range(NT):
                    act.wait_ge(*sg.at("qkv_transposed", l, t + 1))
                    copy(Bm[0][:, t, :, :].rearrange("p h c -> p (h c)"), bank[t][:, :], "qk_squared", ACT.Square)
                act.wait_ge(*sg.at("qkv_transposed", l))
                copy(gv[:, :, :], b2(2), "v_copied")
                act.wait_ge(*sg.at("gates_summed", l))
                copy(gc, bank[3][:, 32:40], "gc_ready")
                copy(ngc, bank[3][:, 32:40], "gc_ready", scale=-1.0)
                act.activation(egl, bank[3][:, 96:112].rearrange("p (c h) -> p c h", c=NCH), ACT.Exp)
                act.activation(egc, bank[3][:, 32:40], ACT.Exp).then_inc(sg.inc("egc_ready"), 1)
                act.wait_ge(*sg.at("ekd_in", l))
                copy(ekd, ekd, "sums_copied", ACT.Exp)
                for t in range(NT):
                    act.wait_ge(*sg.at("kv_up", l, t + 1))
                    copy(dv[:, t, :], b2(4 + t)[:, 1, :], "kv_copied")
                    copy(dk[:, t, :], b2(4 + t)[:, 0, :], "kv_copied")
                act.wait_ge(*unit_used(U_SCC, l))
                copy(scz[:, :, 2:2 + S], b2(7), "scc_copied")
                for t in range(NT):
                    act.wait_ge(*sg.at("ET_in", l, t + 1))
                    for h in range(H):
                        copy(ET[:, t, h, :], ET[:, t, h, :], "ET_ready", ACT.Exp, bias=ngc[:, H * t + h:H * t + h + 1])
                for i, dst in enumerate((kT, kbT, qT, qgT)):
                    act.wait_ge(*sg.at("gT_transposed", l, i + 1))
                    copy(dst, b2(i % 2), "gT_copied")
                act.wait_ge(*unit_used(U_SCH, l))
                copy(sch[:, :, :], b2(6), "sch_copied")
                for i, (dst, src) in enumerate(((dqT[:, :, :], b2(4)), (diqT[:, :, :], b2(5)), (dikT[:, :], bank[4][:, 0:S]),
                                                (dkT[:, :, :], b2(5)))):
                    act.wait_ge(*sg.at("dT_transposed", l, i + 1))
                    copy(dst, src, "dT_copied")
                for t in range(NT):
                    n = 2 * P * (t + 1)
                    for odd in range(2):
                        act.wait_ge(*sg.at("index_scores", l, 2 * t + odd + 1))
                        if t:
                            act.wait_ge(*sg.at("score_added", l))
                        copy(rel[:, n * odd:n * odd + n], bank[4 + odd][:, 0:n], "relu_done", ACT.Relu)
                act.wait_ge(*unit_used(U_SCB, l))
                copy(yT[:, 2:4, :], b2(7), "scb_copied")
                for i in range(1, len(LEVELS)):
                    for t in range(NT):
                        act.wait_ge(*sg.at("U_done", l, NT * i + t + 1))
                        copy(Um[:, t, :, :], b4(2 * t), "U_copied")
                    if i == 1:
                        act.wait_ge(*unit_used(U_GG, l))
                        copy(gate[:, :, :], b2(6), "gate_read", ACT.Silu)
                    else:
                        act.wait_ge(*unit_used(U_XK + i - 2, l))
                        copy(kxT[:, 2 * (i - 2):2 * (i - 2) + 2, :], b2(7 - (i - 2) % 2), "xkv_copied")

                def value_copy(i):
                    act.wait_ge(*unit_used(U_XV + i, l))
                    copy(vx[:, :, 256 * i:256 * i + 256], b2(7 - i % 2), "xkv_copied")

                def read_copy(c):
                    t, r = c // 2, CH * (c % 2)
                    act.wait_ge(*sg.at("vnew_ready", l, 2 * c + 2))
                    for odd in range(2):
                        act.activation(os_[r:r + CH, t, odd:H:2, :],
                                       bank[odd][r:r + CH, P:2 * P].rearrange("p (b c) -> p b c", b=2), ACT.Copy)\
                            .then_inc(sg.inc("qs_copied"), 1)

                value_copy(0)
                act.wait_ge(*sg.at("u_done", l))
                copy(us, b2(0), "uw_copied")
                act.wait_ge(*sg.at("w_done", l))
                copy(wT[:, :, :], b2(1), "uw_copied")
                value_copy(1)

                def dsa_exp(t):
                    act.wait_ge(*sg.at("dmx_ready", l, t + 1))
                    n = P * (t + 1)
                    for h in range(H):
                        copy(Pd[:, n * h:n * h + n], Pd[:, n * h:n * h + n], "dexp_done", ACT.Exp,
                             bias=dmx[:, 4 * t + h:4 * t + h + 1], accum_out=dsum[:, 4 * t + h:4 * t + h + 1])

                read_copy(0)
                dsa_exp(0)
                read_copy(1)
                value_copy(2)
                read_copy(2)
                value_copy(3)
                read_copy(3)
                act.wait_ge(*sg.at("PT_transposed", l, 1))
                copy(PT[:, 0:512], bank[7][:, :], "PT_copied")
                act.wait_ge(*sg.at("sg_transposed", l))
                copy(yT[:, 0:2, :], b2(2), "yT_ready")
                dsa_exp(1)
                act.wait_ge(*sg.at("PT_transposed", l, 2))
                copy(PT[:, 512:1024], bank[5][:, :], "PT_copied")
                act.wait_ge(*sg.at("PT_transposed", l, 3))
                copy(PT[:, 1024:1536], bank[4][:, :], "PT_copied")
                act.wait_ge(*sg.at("dsa_out", l))
                copy(yT[:, 4:6, :], b2(5), "yT_ready")
                act.wait_ge(*sg.at("gdn_transposed", l))
                copy(yT[:, 6:8, :], b2(0), "yT_ready")

            def cross(l):
                def queries(h):
                    act.wait_ge(*unit_used(U_XQ + h, l))
                    act.activation(xqT[:, 2 * h:2 * h + 2, :], b2(4 * (h % 2)), ACT.Copy).then_inc(sg.inc("xq_copied"), 1)

                def exps(h):
                    act.wait_ge(*sg.at("xmax_ready", l, h + 1))
                    if h >= 2:
                        act.wait_ge(*sg.at("xPT", l, h - 1))
                    for t in range(NT):
                        act.activation(xP[:, h % 2, t, :], b2((1, 5, 1, 0)[h])[:, t, :], ACT.Exp, scale=1.0 / 16,
                                       bias=xnb[:, 2 * h + t:2 * h + t + 1], accum_out=xsum[:, 2 * h + t:2 * h + t + 1])\
                            .then_inc(sg.inc("xexp_done"), 1)

                def pt(h):
                    act.wait_ge(*sg.at("xPT", l, h + 1))
                    if h >= 2:
                        act.wait_ge(*sg.at("xvalues", l, h - 1))
                    act.activation(xPT[:, h % 2, :, :], b2(2), ACT.Copy).then_inc(sg.inc("xPT_copied"), 1)

                def outs(h):
                    act.wait_ge(*sg.at("xvalues", l, h + 1))
                    act.activation(oT[:, 2 * h:2 * h + 2, :], b2(3), ACT.Copy).then_inc(sg.inc("oT_copied"), 1)

                queries(0), queries(1), exps(0), queries(2), exps(1), pt(0), queries(3), outs(0)
                exps(2), pt(1), outs(1), exps(3), pt(2), outs(2), pt(3), outs(3)

            with act.Fori(0, DEPTH) as l:
                norm(l, 0, R_FFN1)
                ffn(l, 0, U_FFN1)
                norm(l, 1, R_MIX)
                mixer(l)
                norm(l, 2, R_XA)
                cross(l)
                norm(l, 3, R_FFN2)
                ffn(l, 1, U_FFN2)
            for t in range(NT):
                act.wait_ge(*sg.at("x_updated", DEPTH - 1, 12 + 2 * t + 2))
                act.activation(hn[:, t, :], x[:, t, :], ACT.Square, scale=float(D) ** -0.5,
                               accum_out=ms[:, t:t + 1]).then_inc(sg.sem("final_ms"), 1)

        @block.gpsimd
        def _(pool):
            made = sg.sem("pool_made")
            n_made = [0]

            def step(ins):
                n_made[0] += 1
                ins.then_inc(made, 1)
                pool.wait_ge(made, n_made[0])

            def select(dst, src, op, fill, base, mult, pattern):
                step(pool.affine_select(out=dst, in_=src, compare_op=op, fill=fill, base=base,
                                        channel_multiplier=mult, pattern=pattern))

            step(pool.memset(zeros, 0.0))
            step(pool.memset(onesm[:, :], 1.0))
            select(ident[:, :], zeros, ALU.not_equal, 1.0, 0, 1, [[-1, P]])
            step(pool.memset(mhalf[:, :], -0.5))
            pool.wait_ge(sg.sem("mem_ms"), 2)
            step(pool.tensor_scalar(ms, ms, 1.0, EPS, ALU.mult, ALU.add))
            pool.tensor_tensor(rstd, ms, mhalf[:, 0:2], ALU.pow).then_inc(sg.sem("mem_rstd"), 1)
            for j in range(ROT):
                step(pool.memset(inv[:, j:j + 1],
                                 float(np.float32(THETA) ** np.float32(-j * 2.0 / (2 * ROT)))))
            select(up[:, :], onesm[:, :], ALU.is_ge, 0.0, 0, -1, [[1, P]])
            select(half[:, 0, :], onesm[:, :], ALU.is_ge, 0.0, CH - 1, -1, [[0, P]])
            select(half[:, 1, :], onesm[:, :], ALU.is_ge, 0.0, -CH, 1, [[0, P]])

            def block_diagonal(dst, src, s):
                v = dst.rearrange("p (b c) -> p b c", c=s)
                select(v, src.rearrange("p (b c) -> p b c", c=s), ALU.is_ge, 0.0, 0, 1, [[-s, P // s], [0, s]])
                select(v, v, ALU.is_ge, 0.0, s - 1, -1, [[s, P // s], [0, s]])

            block_diagonal(same[:, :], onesm[:, :], CH)
            block_diagonal(incl[:, :], up[:, :], CH)
            step(pool.tensor_scalar(away[:, :], incl[:, :], -AWAY, AWAY, ALU.mult, ALU.add))
            for n, s in enumerate(LEVELS):
                block_diagonal(lev[:, n, :], up[:, :], 2 * s)
                if s > 1:
                    block_diagonal(Bm[0][:, 0, 0, :], up[:, :], s)
                    step(pool.tensor_tensor(lev[:, n, :], lev[:, n, :], Bm[0][:, 0, 0, :], ALU.subtract))
                else:
                    step(pool.tensor_tensor(lev[:, n, :], lev[:, n, :], ident[:, :], ALU.subtract))
            step(pool.memset(cfill[:, :], 0.0))
            for off in (0, 2 * P):
                select(cfill[:, off:off + P], cfill[:, off:off + P], ALU.is_ge, FILL, 0, 1, [[-1, P]])
            pool.memset(scz[:, :, 0:2], 0.0).then_inc(made, 1)
            pool.wait_ge(made, n_made[0] + 1)
            pool.memset(score[:, :], 0.0).then_inc(consts_done, 1)
            pool.wait_ge(consts_done, 1)

            def link(ins, l):
                ins.then_inc(sg.inc("pool_link"), 1)
                pool.wait_ge(*sg.at("pool_link", l, sg.counts["pool_link"]))

            def rsqrt(dst, src, n, l, name, add=EPS):
                apart(pool)
                link(pool.tensor_scalar(msb[:, 0:n], src, 1.0, add, ALU.mult, ALU.add), l)
                pool.tensor_tensor(dst, msb[:, 0:n], mhalf[:, 0:n], ALU.pow).then_inc(sg.inc(name), 1)
                pool.wait_ge(*sg.at(name, l, sg.counts[name]))

            def norm(l, k):
                for t in range(NT):
                    pool.wait_ge(*sg.at("ms_ready", l, NT * k + t + 1))
                    rsqrt(rstd[:, t:t + 1], ms[:, t:t + 1], 1, l, "rstd_ready")

            def mixer(l):
                apart(pool)
                pool.memset(z[:, :, 0:3], 0.0).then_inc(sg.inc("pads_ready"), 1)
                pool.wait_ge(*sg.at("msa_ready", l))
                rsqrt(rsa, msa, 4, l, "rsa_ready")
                pool.wait_ge(*sg.at("z_copied", l))
                for j in range(4):
                    w = broadcast_last(gcw[:, 4:6, j], S)
                    src = z[:, 4:6, j:j + S]
                    if j == 0:
                        link(pool.tensor_tensor(cv[:, 4:6, :], src, w, ALU.mult), l)
                        continue
                    link(pool.tensor_tensor(sco[:, :, :], src, w, ALU.mult), l)
                    last = pool.tensor_tensor(cv[:, 4:6, :], cv[:, 4:6, :], sco[:, :, :], ALU.add)
                    if j < 3:
                        link(last, l)
                last.then_inc(sg.inc("conv_v"), 1)
                pool.wait_ge(*sg.at("mss_ready", l))
                rsqrt(rss, mss, 2, l, "rss_ready")
                pool.wait_ge(*sg.at("l2_summed", l))
                rsqrt(l2r, l2s, 16, l, "l2_ready")
                pool.wait_ge(mem_loaded, 16 * (l + 1))
                apart(pool)
                for c in range(KC):
                    pool.tensor_scalar(memn[:, c, :], memn[:, c, :], cols[:, R_MEM + c:R_MEM + c + 1], 1.0,
                                       ALU.mult, ALU.mult).then_inc(sg.inc("memn_ready"), 1)
                pool.wait_ge(*sg.at("AE_ready", l))
                pool.wait_ge(*sg.at("l2_read", l))
                for i in range(len(LEVELS)):
                    for t in range(NT):
                        if i >= 2:
                            pool.wait_ge(*sg.at("U_done", l, NT * (i - 2) + t + 1))
                        if i == 2:
                            pool.wait_ge(*sg.at("TS_ready", l, 2 * t + 2))
                        pool.tensor_tensor(Bm[i % 2][:, t, :, :], AE[:, t, :, :],
                                           lev[:, i, :].unsqueeze(1).broadcast_to([P, H, P]), ALU.mult)\
                            .then_inc(sg.inc("B_ready"), 1)
                pool.wait_ge(*sg.at("scc_copied", l))
                pool.wait_ge(*sg.at("sch_copied", l))
                link(pool.tensor_tensor(scz[:, :, 2:2 + S], scz[:, :, 2:2 + S], sch[:, :, :], ALU.mult), l)
                link(pool.tensor_tensor(sco[:, :, :], scz[:, :, 0:S], broadcast_last(scw[:, :, 0], S), ALU.mult), l)
                for j in (1, 2):
                    link(pool.tensor_tensor(sch[:, :, :], scz[:, :, j:j + S], broadcast_last(scw[:, :, j], S), ALU.mult), l)
                    link(pool.tensor_tensor(sco[:, :, :], sco[:, :, :], sch[:, :, :], ALU.add), l)
                pool.wait_ge(*sg.at("scb_copied", l))
                pool.tensor_tensor(yT[:, 2:4, :], sco[:, :, :], yT[:, 2:4, :], ALU.mult).then_inc(sg.inc("sc_out"), 1)
                pool.wait_ge(*sg.at("gos_ready", l))
                rsqrt(gor, gos, 8, l, "gor_ready")

            with pool.Fori(0, DEPTH) as l:
                norm(l, 0)
                norm(l, 1)
                mixer(l)
                norm(l, 2)
                norm(l, 3)
            pool.wait_ge(sg.sem("final_ms"), 2)
            pool.tensor_scalar(msb[:, 0:2], ms, 1.0, EPS, ALU.mult, ALU.add).then_inc(sg.sem("final_eps"), 1)
            pool.wait_ge(sg.sem("final_eps"), 1)
            pool.tensor_tensor(rstd, msb[:, 0:2], mhalf[:, 0:2], ALU.pow).then_inc(sg.sem("final_rstd"), 1)

        @block.vector
        def _(dve):
            def link(ins, l):
                ins.then_inc(sg.inc("vector_link"), 1)
                dve.wait_ge(*sg.at("vector_link", l, sg.counts["vector_link"]))

            for t in range(NT):
                dve.wait_ge(sg.sem("mem_rstd"), 1)
                dve.tensor_scalar(hn[:, t, :], hn[:, t, :], rstd[:, t:t + 1], None, ALU.mult)\
                    .then_inc(sg.sem("mem_hn_ready"), 1)
            dve.wait_ge(rope_loaded, 16)
            dve.wait_ge(consts_done, 1)
            setup = sg.sem("vector_setup")
            n_setup = [0]

            def step(ins):
                n_setup[0] += 1
                ins.then_inc(setup, 1)
                dve.wait_ge(setup, n_setup[0])

            two_pi = 2 * np.pi
            p1 = 6.28125
            p2 = float(np.float32(np.floor((two_pi - p1) * 2.0 ** 21) / 2.0 ** 21))
            p3 = float(np.float32(two_pi - p1 - p2))
            magic = 1.5 * 2.0 ** 23
            pi_in = 3.1415925
            ang, kk, red = rtmp[:, :, 0, 0:ROT], rtmp[:, :, 2, 0:ROT], rtmp[:, :, 3, 0:ROT]
            cosa = rtmp[:, :, 1, 0:ROT]
            step(dve.tensor_copy(posf[:, :], posi[:, :]))
            step(dve.tensor_tensor(ang, broadcast_last(posf[:, :], ROT),
                                   inv[:, :].unsqueeze(1).broadcast_to([P, NT, ROT]), ALU.mult))
            step(dve.tensor_scalar(kk, ang, 1.0 / two_pi, None, ALU.mult))
            step(dve.tensor_scalar(kk, kk, magic, None, ALU.add))
            step(dve.tensor_scalar(kk, kk, -magic, None, ALU.add))
            for part in (p1, p2, p3):
                step(dve.scalar_tensor_tensor(out=ang, in0=kk, scalar=-part, in1=ang, op0=ALU.mult, op1=ALU.add))
            step(dve.tensor_scalar(cosa, ang, np.pi / 2, None, ALU.add))
            step(dve.tensor_scalar(red, cosa, pi_in, -two_pi, ALU.is_gt, ALU.mult))
            step(dve.tensor_tensor(cosa, cosa, red, ALU.add))
            dve.tensor_scalar(cosa, cosa, pi_in, -pi_in, ALU.min, ALU.max).then_inc(sg.sem("angles_ready"), 1)
            dve.tensor_scalar(ang, ang, pi_in, -pi_in, ALU.min, ALU.max).then_inc(sg.sem("angles_ready"), 1)
            dve.wait_ge(sg.sem("trig_done"), 4)

            def gain(row, c):
                return broadcast_last(cols[:, row + c:row + c + 2], S)

            def norm(l, k, row):
                for t in range(NT):
                    dve.wait_ge(*sg.at("rstd_ready", l, NT * k + t + 1))
                    dve.tensor_scalar(hn[:, t, :], x[:, t, :], rstd[:, t:t + 1], None, ALU.mult)\
                        .then_inc(sg.inc("hn_ready"), 1)
                for i in (2, 3):
                    dve.wait_ge(*sg.at("hT_transposed", l, 4 * k + i + 1))
                    dve.tensor_tensor(hT[:, 2 * i:2 * i + 2, :], b2(4 + i), gain(row, 2 * i), ALU.mult)\
                        .then_inc(sg.inc("hT_vector"), 1)

            def add_product(l, bk, scale):
                for t in range(NT):
                    for n in range(2):
                        xs = x[:, t, 512 * n:512 * n + 512]
                        dve.scalar_tensor_tensor(out=xs, in0=bank[bk + 2 * t + n][:, :], scalar=scale, in1=xs,
                                                 op0=ALU.mult, op1=ALU.add).then_inc(sg.inc("x_updated"), 1)

            def ffn(l, which, base):
                done, ready = sg.sem("silu_ready"), sg.sem("hid_ready")

                def step(par, s, read=None):
                    n = l * 4 * STEPS + which * 2 * STEPS + 2 * s
                    if read:
                        dve.wait_ge(*read)
                    for b in range(2):
                        dve.wait_ge(done, n + b + 1)
                        dve.tensor_tensor(hid[:, par, b, :], b2(4 + 2 * par + b)[:, 1, :], sil[:, par, b, :], ALU.mult)\
                            .then_inc(ready, 1)

                step(0, 0)
                step(1, 1)
                step(0, 2, unit_used(base + 4, l))
                with dve.Fori(1, PAIRS) as it:
                    step(1, it * 2 + 1, unit_used(base + 7, l, it - 1))
                    step(0, it * 2 + 2, unit_used(base + 4, l, it))
                dve.wait_ge(*unit_used(base + 2 + 6 * PAIRS, l))
                add_product(l, 0, 0.5)

            def rope(v, heads, l, name):
                t1, t2 = rtmp[:, :, 0:heads, :], rtmp2[:, :, 0:heads, :]
                cb = rc[:, :, :].unsqueeze(2).broadcast_to([P, NT, heads, 2 * ROT])
                sb_ = rs[:, :, :].unsqueeze(2).broadcast_to([P, NT, heads, 2 * ROT])
                dve.tensor_tensor(t1, v[:, :, :, 0:2 * ROT], cb, ALU.mult)
                dve.tensor_tensor(t2[:, :, :, 0:ROT], v[:, :, :, ROT:2 * ROT], sb_[:, :, :, 0:ROT], ALU.mult)
                link(dve.tensor_tensor(t2[:, :, :, ROT:2 * ROT], v[:, :, :, 0:ROT], sb_[:, :, :, ROT:2 * ROT], ALU.mult), l)
                return dve.tensor_tensor(v[:, :, :, 0:2 * ROT], t1, t2, ALU.add)

            def mixer(l):
                def heads(ap):
                    return broadcast_last(ap.rearrange("p (t h) -> p t h", t=NT), HD)

                def by_head(ap):
                    return ap.rearrange("p t (h c) -> p t h c", h=H)

                dve.wait_ge(*sg.at("ab_copied", l))
                link(dve.tensor_tensor(ga1.rearrange("p (t h) -> p t h", t=NT), ab[:, :, 0:4],
                                       b_dt.unsqueeze(1).broadcast_to([P, NT, H]), ALU.add), l)
                dve.tensor_copy(beta.rearrange("p (t h) -> p t h", t=NT), ab[:, :, 4:8])
                link(dve.tensor_scalar(ga2, ga1, -1.0, None, ALU.mult), l)
                dve.tensor_tensor(ga2, ga1, ga2, ALU.min).then_inc(sg.inc("soft_in"), 1)
                for b in range(4):
                    dve.wait_ge(*sg.at("z_copied", l, b // 2 + 1))
                    link(dve.tensor_scalar(cv[:, b, :], z[:, b, 0:S], gcw[:, b, 0:1], None, ALU.mult), l)
                    for j in (1, 2, 3):
                        ins = dve.scalar_tensor_tensor(out=cv[:, b, :], in0=z[:, b, j:j + S], scalar=gcw[:, b, j:j + 1],
                                                       in1=cv[:, b, :], op0=ALU.mult, op1=ALU.add)
                        if j < 3:
                            link(ins, l)
                    ins.then_inc(sg.inc("conv_qk"), 1)
                dve.wait_ge(*sg.at("soft_ln", l))
                dve.tensor_scalar(beta, beta, 1.0, None, ALU.add)
                link(dve.scalar_tensor_tensor(out=ga1, in0=ga1, scalar=0.0, in1=ga3, op0=ALU.max, op1=ALU.add), l)
                dve.reciprocal(beta, beta)
                dve.scalar_tensor_tensor(out=gg_.rearrange("p (t h) -> p t h", t=NT),
                                         in0=ga1.rearrange("p (t h) -> p t h", t=NT), scalar=-1.0,
                                         in1=alog.unsqueeze(1).broadcast_to([P, NT, H]), op0=ALU.mult, op1=ALU.mult)\
                    .then_inc(sg.inc("g_ready"), 1)
                dve.wait_ge(*sg.at("rsa_ready", l))
                dve.wait_ge(*sg.at("iq0_copied", l))
                for t in range(NT):
                    dve.tensor_scalar(cn[:, t, :], b2(5)[:, t, 0:LAT], rsa[:, t:t + 1], None, ALU.mult)\
                        .then_inc(sg.inc("cn_ready"), 1)
                dve.wait_ge(*sg.at("iq1_scalar", l))
                for t in range(NT):
                    for i in (8, 9):
                        last = dve.scalar_tensor_tensor(out=R[:, t, i, :], in0=b2(6)[:, t, P:P + HD],
                                                        scalar=rsa[:, 2 + t:3 + t], in1=b_ikn, op0=ALU.mult, op1=ALU.mult)
                last.then_inc(sg.inc("iq1_copied"), 1)
                dve.wait_ge(*sg.at("g_ready", l))
                for t in range(NT):
                    last = dve.tensor_tensor(Sm[:, t, :, :], incl[:, :].unsqueeze(1).broadcast_to([P, H, P]),
                                             broadcast_last(gg_[:, 4 * t:4 * t + 4], P), ALU.mult)
                last.then_inc(sg.inc("gm_ready"), 1)
                dve.wait_ge(*sg.at("c_transposed", l))
                dve.tensor_scalar(cT[:, :], bank[4][:, 0:S], cols[:, R_KV:R_KV + 1], None, ALU.mult)\
                    .then_inc(sg.inc("cT_ready"), 1)
                dve.wait_ge(*sg.at("gc_ready", l))
                dve.wait_ge(*sg.at("egc_ready", l))
                dve.tensor_tensor(ekd, bank[3][:, 64:72], gc, ALU.subtract).then_inc(sg.inc("ekd_in"), 1)
                dve.wait_ge(*sg.at("iq1_copied", l))
                dve.wait_ge(*sg.at("iq0_copied", l))
                last = rope(R[:, :, 0:9, :], 9, l, "q")
                link(last, l)
                dve.tensor_copy(R[:, :, 9, 0:2 * ROT], R[:, :, 8, 0:2 * ROT]).then_inc(sg.inc("rope_q"), 1)
                for t in range(NT):
                    dve.wait_ge(*sg.at("qk_squared", l, t + 1))
                    last = dve.tensor_reduce(l2s[:, 8 * t:8 * t + 8],
                                             Bm[0][:, t, :, :].rearrange("p a b -> p (a b)").rearrange("p (h c) -> p h c", c=HD),
                                             AX, ALU.add)
                last.then_inc(sg.inc("l2_summed"), 1)
                dve.wait_ge(*sg.at("l2_ready", l))
                l2q = l2r.rearrange("p (t h) -> p t h", t=NT)[:, :, 0:4]
                link(dve.tensor_scalar(l2q, l2q, float(HD) ** -0.5, None, ALU.mult), l)
                for t in range(NT):
                    last = dve.tensor_tensor(qk[:, t, :, :], bank[t][:, :].rearrange("p (h c) -> p h c", c=HD),
                                             broadcast_last(l2r[:, 8 * t:8 * t + 8], HD), ALU.mult)
                    last.then_inc(sg.inc("qk_scaled"), 1)
                dve.wait_ge(*sg.at("qk_scaled", l))
                dve.wait_ge(*sg.at("sums_copied", l))
                dve.tensor_tensor(by_head(kb), qk[:, :, 4:8, :], heads(beta), ALU.mult).then_inc(sg.inc("kb_ready"), 1)
                dve.tensor_tensor(by_head(qg), qk[:, :, 0:4, :], heads(egc), ALU.mult).then_inc(sg.inc("qg_ready"), 1)
                for t in range(NT):
                    dve.wait_ge(*sg.at("gc_rows", l, t + 1))
                    dve.tensor_tensor(ET[:, t, :, :], b4(3 - t), away[:, :].unsqueeze(1).broadcast_to([P, H, P]), ALU.add)\
                        .then_inc(sg.inc("ET_in"), 1)
                dve.wait_ge(*sg.at("v_copied", l))
                dve.tensor_tensor(by_head(vb), by_head(gv[:, :, :]), heads(beta), ALU.mult)
                dve.wait_ge(*sg.at("kb_ready", l))
                dve.tensor_tensor(by_head(kbg), by_head(kb), heads(egc), ALU.mult)
                dve.tensor_tensor(by_head(kd), qk[:, :, 4:8, :], heads(ekd), ALU.mult).then_inc(sg.inc("ET_read"), 1)
                dve.wait_ge(*sg.at("kv_copied", l))
                rope(dk[:, :, :].rearrange("p t (h c) -> p t h c", h=H), H, l, "k").then_inc(sg.inc("rope_k"), 1)
                dve.wait_ge(*sg.at("rss_ready", l))
                for t in range(NT):
                    dve.scalar_tensor_tensor(out=sgn[:, t, :], in0=sgv[:, t, :], scalar=rss[:, t:t + 1], in1=b_sgn,
                                             op0=ALU.mult, op1=ALU.mult).then_inc(sg.inc("sgn_ready"), 1)
                dve.wait_ge(*sg.at("ET_ready", l))
                for t in range(NT):
                    for odd in range(2):
                        dve.wait_ge(*sg.at("kq_done", l, 2 * t + odd + 1))
                        for i, dst in enumerate((AE, AT)):
                            pair = (slice(None), t, slice(odd, H, 2), slice(None))
                            dve.tensor_tensor(dst[pair], b4(2 * t + odd)[:, 2 * i:2 * i + 2, :], ET[pair], ALU.mult)\
                                .then_inc(sg.inc("AE_ready"), 1)
                dve.wait_ge(*sg.at("qk_squared", l))
                dve.memset(state[:, :, :], 0.0).then_inc(sg.inc("l2_read"), 1)

                def weigh(t, h, src):
                    link(dve.scalar_tensor_tensor(out=work[t], in0=src, scalar=iw[:, t, h:h + 1],
                                                  in1=cfills[t] if h == 0 else work[t], op0=ALU.mult, op1=ALU.add), l)

                for t in range(NT):
                    n = P * (t + 1)
                    for i, h in enumerate((0, 2, 1, 3)):
                        if i % 2 == 0:
                            dve.wait_ge(*sg.at("relu_done", l, 2 * t + i // 2 + 1))
                        weigh(t, h, rel[:, n * i:n * i + n])
                    if t == 0:
                        dve.nop().then_inc(sg.inc("score_added"), 1)

                def take(t):
                    apart(dve)
                    link(dve.max(m8[:, t, :], work[t]), l)
                    apart(dve)
                    link(dve.match_replace(out=work[t], in_to_replace=m8[:, t, :], in_values=work[t],
                                           imm_value=TAKEN), l)

                takes = [0] * (TOPK // 8) + [1] * (TOPK // 8)
                for t in range(NT):
                    dve.wait_ge(*sg.at("B_ready", l, t + 1))
                    dve.tensor_tensor(Sm[:, t, :, :], ident[:, :].unsqueeze(1).broadcast_to([P, H, P]), Bm[0][:, t, :, :],
                                      ALU.subtract).then_inc(sg.inc("TS_ready"), 1)
                    dve.wait_ge(*sg.at("U_done", l, t + 1))
                    dve.tensor_tensor(Tm[:, t, :, :], ident[:, :].unsqueeze(1).broadcast_to([P, H, P]), b4(2 * t),
                                      ALU.subtract).then_inc(sg.inc("TS_ready"), 1)
                n = 0
                for i in range(1, len(LEVELS)):
                    for _ in range(3):
                        take(takes[n])
                        n += 1
                    for t in range(NT):
                        last_level = i == len(LEVELS) - 1
                        k = 2 * NT * (i - 1) + (t if last_level else 2 * t)
                        for j, (m, bk) in enumerate([(Tm, 2 * t + 1), (Sm, 2 * t)][last_level:]):
                            dve.wait_ge(*sg.at("TS_done", l, k + j + 1))
                            dve.tensor_tensor(m[:, t, :, :], m[:, t, :, :], b4(bk), ALU.subtract)\
                                .then_inc(sg.inc("TS_ready"), 1)
                take(takes[n])

                def selected(t):
                    link(dve.tensor_scalar(nb[t], work[t], TAKEN_BELOW, -AWAY, ALU.is_lt, ALU.mult), l)
                    link(dve.scalar_tensor_tensor(out=nb[t], in0=nb[t], scalar=AWAY, in1=cfills[t],
                                                  op0=ALU.add, op1=ALU.add), l)

                selected(0)
                selected(1)
                dve.wait_ge(*sg.at("egc_ready", l))
                eg = egl.rearrange("p c (b two) -> p c b two", two=2)
                dve.tensor_copy(egl2[0:HD], eg[0:HD, :, :, 0])
                dve.tensor_copy(egl2[HD:P], eg[HD:P, :, :, 1]).then_inc(sg.inc("state_ready"), 1)

                def chunk_new(c):
                    t, r = c // 2, CH * (c % 2)
                    dve.wait_ge(*sg.at("state_ready", l, c + 1))
                    dve.tensor_tensor(state_d[:, :, :], state[:, :, :], broadcast_last(egl2[:, c, :], HD), ALU.mult)
                    dve.wait_ge(*sg.at("ws_done", l, c + 1))
                    for odd in range(2):
                        pair = (slice(r, r + CH), t, slice(odd, H, 2), slice(None))
                        dve.tensor_tensor(by_head(vnew[:, :, :])[pair], by_head(us)[pair],
                                          bank[odd][r:r + CH, 0:P].rearrange("p (b c) -> p b c", b=2), ALU.subtract)\
                            .then_inc(sg.inc("vnew_ready"), 1)

                def chunk_state(c):
                    dve.wait_ge(*sg.at("kv_done", l, c + 1))
                    dve.tensor_tensor(state[:, :, :], state_d[:, :, :],
                                      bank[2][:, 0:2 * HD].rearrange("p (b c) -> p b c", b=2), ALU.add)\
                        .then_inc(sg.inc("state_ready"), 1)

                def logits(t):
                    dve.wait_ge(*sg.at("logits_done", l, t + 1))
                    n = P * (t + 1)
                    for odd in range(2):
                        dve.scalar_tensor_tensor(
                            out=Pd[:, 2 * n * odd:2 * n * odd + 2 * n].rearrange("p (b s) -> p b s", b=2),
                            in0=bank[4 + odd][:, 0:2 * n].rearrange("p (b s) -> p b s", b=2), scalar=float(HD) ** -0.5,
                            in1=nb[t].unsqueeze(1).broadcast_to([P, 2, n]), op0=ALU.mult, op1=ALU.add)\
                            .then_inc(sg.inc("logits_read"), 1)

                def row_max(t):
                    dst = dmx[:, 4 * t:4 * t + 4]
                    n = 4 * P * (t + 1)
                    dve.tensor_reduce(dst, Pd[:, 0:n].rearrange("p (h s) -> p h s", h=4), AX, ALU.max, negate=True)\
                        .then_inc(sg.inc("dmx_ready"), 1)

                def probs(t):
                    dve.wait_ge(*sg.at("dexp_done", l, 4 * t + 4))
                    d = dsum[:, 4 * t:4 * t + 4]
                    link(dve.reciprocal(d, d), l)
                    n = P * (t + 1)
                    v = Pd[:, 0:4 * n].rearrange("p (h s) -> p h s", h=4)
                    dve.tensor_tensor(v, v, broadcast_last(d, n), ALU.mult).then_inc(sg.inc("probs_ready"), 1)

                chunk_new(0)
                logits(0)
                dve.wait_ge(*sg.at("logits_read", l, 2))
                row_max(0)
                chunk_state(0)
                chunk_new(1)
                probs(0)
                chunk_state(1)
                chunk_new(2)
                chunk_state(2)
                chunk_new(3)
                dve.wait_ge(*sg.at("sgw_transposed", l))
                dve.tensor_tensor(sgwT, b4(7), up[:, :].unsqueeze(1).broadcast_to([P, H, P]), ALU.mult)\
                    .then_inc(sg.inc("sgwT_ready"), 1)
                chunk_state(3)
                dve.wait_ge(*sg.at("o_done", l))
                dve.wait_ge(*sg.at("U_copied", l))
                dve.wait_ge(*sg.at("qs_copied", l))
                link(dve.tensor_tensor(by_head(us), by_head(b2(3)), os_, ALU.add), l)
                link(dve.tensor_tensor(kbg, us, us, ALU.mult), l)
                link(dve.tensor_reduce(gos, by_head(kbg), AX, ALU.add), l)
                dve.tensor_scalar(gos, gos, 1.0 / HD, None, ALU.mult).then_inc(sg.inc("gos_ready"), 1)
                dve.wait_ge(*sg.at("gate_read", l))
                link(dve.tensor_tensor(by_head(gate[:, :, :]), by_head(gate[:, :, :]),
                                       b_gon.unsqueeze(1).unsqueeze(1).broadcast_to([P, NT, H, HD]), ALU.mult), l)
                dve.wait_ge(*sg.at("sg_mixed", l))
                dve.wait_ge(*sg.at("sgu_gelu", l))
                link(dve.tensor_tensor(by_head(sgj), by_head(b2(6)),
                                       broadcast_last(cols[:, R_SGB:R_SGB + H], HD).unsqueeze(1).broadcast_to([P, NT, H, HD]), ALU.add), l)
                dve.tensor_tensor(sgj, sgj, sgu, ALU.mult).then_inc(sg.inc("sg_out"), 1)
                dve.wait_ge(*sg.at("gor_ready", l))
                link(dve.tensor_tensor(by_head(us), by_head(us), heads(gor), ALU.mult), l)
                dve.tensor_tensor(vnew[:, :, :], us, gate[:, :, :], ALU.mult).then_inc(sg.inc("gdn_out"), 1)
                dve.wait_ge(*sg.at("PT_transposed", l, 1))
                logits(1)
                dve.wait_ge(*sg.at("logits_read", l))
                row_max(1)
                probs(1)
                dve.wait_ge(*unit_used(U_OUT + 3, l))
                add_product(l, 4, 1.0)

            def cross(l):
                def maxima(h):
                    dve.wait_ge(*sg.at("xlogits", l, h + 1))
                    m = xmx[:, 2 * h:2 * h + 2]
                    link(dve.tensor_reduce(m, b2((1, 5, 1, 0)[h]), AX, ALU.max), l)
                    dve.tensor_scalar(xnb[:, 2 * h:2 * h + 2], m, -1.0 / 16, None, ALU.mult)\
                        .then_inc(sg.inc("xmax_ready"), 1)

                def probs(h):
                    dve.wait_ge(*sg.at("xexp_done", l, NT * h + NT))
                    s = xsum[:, 2 * h:2 * h + 2]
                    link(dve.reciprocal(s, s), l)
                    v = xP[:, h % 2, :, :]
                    dve.tensor_tensor(v, v, broadcast_last(s, S), ALU.mult).then_inc(sg.inc("xprobs"), 1)

                for h in range(H):
                    maxima(h)
                    probs(h)
                dve.wait_ge(*unit_used(U_XO + 3, l))
                add_product(l, 4, 1.0)

            with dve.Fori(0, DEPTH) as l:
                dve.wait_ge(*sg.at("rows_transposed", l))
                dve.tensor_copy(cols[:, :], bank[7][:, 0:N_ROWS]).then_inc(sg.inc("cols_ready"), 1)
                dve.wait_ge(*sg.at("cols_ready", l))
                norm(l, 0, R_FFN1)
                ffn(l, 0, U_FFN1)
                norm(l, 1, R_MIX)
                mixer(l)
                norm(l, 2, R_XA)
                dve.nop().then_inc(sg.inc("params_used"), 1)
                cross(l)
                norm(l, 3, R_FFN2)
                ffn(l, 1, U_FFN2)
            dve.wait_ge(sg.sem("final_rstd"), 1)
            dve.wait_ge(fgain_loaded, 16)
            for t in range(NT):
                dve.scalar_tensor_tensor(out=hn[:, t, :], in0=x[:, t, :], scalar=rstd[:, t:t + 1], in1=vx[:, 0, :],
                                         op0=ALU.mult, op1=ALU.mult).then_inc(sg.sem("out_ready"), 1)

        return dict(sg.counts)


def kernel(**inputs):
    import concourse.bacc as bacc
    from concourse.bass_utils import run_bass_kernel_spmd

    def program(arrays, per):
        nc = bacc.Bacc("TRN2", target_bir_lowering=False, num_devices=1)
        a = {n: nc.dram_tensor(f"in_{n}", v.shape, mybir.dt.from_np(v.dtype), kind="ExternalInput").ap()
             for n, v in arrays.items()}
        out = nc.dram_tensor("out", (1, S, D), F32, kind="ExternalOutput").ap()
        mem_scratch = nc.dram_tensor("mem_scratch", (P, KC, S), F32, kind="Internal").ap()
        return nc, build(nc, a, out, mem_scratch, per)

    arrays = {n: np.ascontiguousarray(inputs[n]) for n in NAMES}
    _, per = program(arrays, {})
    nc, _ = program(arrays, per)
    r = run_bass_kernel_spmd(nc, [{f"in_{n}": v for n, v in arrays.items()}], core_ids=[0])
    return r.results[0]["out"]
```

```python
from contextlib import ExitStack

import concourse.bass as bass
import numpy as np
from concourse import mybir

F32 = mybir.dt.float32
F32R = mybir.dt.float32r
I32 = mybir.dt.int32
ALU = mybir.AluOpType
ACT = mybir.ActivationFunctionType
AX = mybir.AxisListType.X

P = 128
D = 1024
KC = D // P
S = 256
NT = S // P
DEPTH = 2
D_FF = 2816
STEPS = D_FF // 256
PAIRS = (STEPS - 1) // 2
GW = 256
HD = 64
H = 4
LAT = 128
ROT = 8
THETA = 500000.0
EPS = 1e-6
TOPK = 64
CH = 64
NCH = S // CH
LEVELS = (1, 2, 4, 8, 16, 32)
N_IN = 3020
FILL = -3.0e38
TAKEN = -3.4e38
TAKEN_BELOW = -3.2e38
AWAY = -1.0e30

C_SGU, C_SGV, C_SCB, C_SCC, C_SCH, C_Q, C_CKV, C_IQ1, C_GQKV, C_GA, C_GG = (
    0, 256, 512, 768, 1024, 1280, 1536, 1792, 1988, 2756, 2764)
W_IQ1 = C_GQKV - C_IQ1

RING = 6
FFN_UNITS = 3 * STEPS
SETS = 3
HIGH_WEIGHT, LOW_WEIGHT = [(0, 0), (0, 1)], [(1, 0)]
LAST = None
MIX_COLS = [(C_GQKV, 256), (C_GQKV + 256, 256), (C_GQKV + 512, 256), (C_Q, 256), (C_CKV, 256),
            (C_IQ1, W_IQ1), (C_SGV, 256), (C_SGU, 256), (C_SCC, 256), (C_SCH, 256), (C_SCB, 256),
            (C_GG, 256)]
U_FFN1 = 0
U_MIX = U_FFN1 + FFN_UNITS
(U_GQ, U_GK, U_GV, U_Q, U_CKV, U_IQ1, U_SGV, U_SGU, U_SCC, U_SCH, U_SCB, U_GG) = range(
    U_MIX, U_MIX + len(MIX_COLS))
U_XK = U_GG + 1
U_XV = U_XK + 4
U_OUT = U_XV + 4
U_XQ = U_OUT + 4
U_XO = U_XQ + 4
U_FFN2 = U_XO + 4
N_UNITS = U_FFN2 + FFN_UNITS

N_ROWS = 5 * KC + H + 1
R_FFN1, R_MIX, R_XA, R_MEM, R_FFN2, R_SGB, R_KV = 0, KC, 2 * KC, 3 * KC, 4 * KC, 5 * KC, 5 * KC + H

NAMES = ['x', 'mem', 'positions', 'ffn1_norm', 'ffn1_wg', 'ffn1_wu', 'ffn1_wd', 'mix_norm', 'w_mix_in',
         'w_mix_out', 'sg_norm', 'sg_w', 'sg_b', 'sc_conv', 'kv_norm', 'w_uk', 'w_uv', 'idx_k_norm',
         'gdn_conv', 'gdn_a_log', 'gdn_dt_bias', 'gdn_out_norm', 'xa_norm', 'mem_norm', 'xa_wq', 'xa_wk',
         'xa_wv', 'xa_wo', 'ffn2_norm', 'ffn2_wg', 'ffn2_wu', 'ffn2_wd', 'final_norm']


class Signals:

    def __init__(self, nc, ctx, per):
        self.nc, self.ctx, self.per = nc, ctx, per
        self.sems, self.counts = {}, {}
        self.start = {"x_updated": 4, "params_used": 1}

    def sem(self, name):
        if name not in self.sems:
            self.sems[name] = self.ctx.enter_context(self.nc.semaphore(name))
        return self.sems[name]

    def inc(self, name, times=1):
        self.counts[name] = self.counts.get(name, 0) + times
        return self.sem(name)

    def begin(self, eng, name):
        eng.sem_inc(self.sem(name), self.start[name])

    def at(self, name, layer, k=None):
        per = self.per.get(name, 0)
        return self.sem(name), layer * per + (per if k is None else k) + self.start.get(name, 0)


def broadcast_last(ap, n):
    return ap.unsqueeze(len(ap.shape)).broadcast_to([*ap.shape, n])


def build(nc, a, out, mem_scratch, per):
    with ExitStack() as ctx:
        sg = Signals(nc, ctx, per)

        def sb(name, shape, dt=F32):
            return ctx.enter_context(nc.sbuf_tensor(name, shape, dt))

        x = sb("x", [P, NT, D])
        hT = sb("hT", [P, KC, S])
        hn = sb("hn", [P, NT, D])
        memn = hn[:, :, :].rearrange("p t d -> p (t d)").rearrange("p (c s) -> p c s", c=KC)
        vx = sb("vx", [P, NT, D])
        yT = sb("yT", [P, KC, S])
        ring = [sb(f"ring{i}", [P, 2048]) for i in range(RING)]
        ffn_buf = sb("ffn_buf", [P, 2048])
        sil = ffn_buf[:, 0:1024].rearrange("p (b k s) -> p b k s", b=2, k=2)
        hid = ffn_buf[:, 1024:2048].rearrange("p (b k s) -> p b k s", b=2, k=2)
        sgu = ffn_buf[:, 0:512].rearrange("p (t c) -> p t c", t=NT)
        sgv = ffn_buf[:, 512:1024].rearrange("p (t c) -> p t c", t=NT)
        sgn = ffn_buf[:, 1024:1536].rearrange("p (t c) -> p t c", t=NT)
        sgj = ffn_buf[:, 1536:2048].rearrange("p (t c) -> p t c", t=NT)
        rows = sb("rows", [N_ROWS, P])
        cols = sb("cols", [P, N_ROWS])
        wab = sb("wab", [P, KC, 8])
        w_kv = sb("w_kv", [P, 2, GW])
        sgw = sb("sgw", [P, H, P])
        scw = sb("scw", [P, 2, 3])
        gcw = sb("gcw", [P, 6, 4])
        bc = sb("bc", [P, GW + HD + HD + 2 * H])
        b_sgn, b_ikn, b_gon, b_alog, b_dt = (bc[:, 0:256], bc[:, 256:320], bc[:, 320:384], bc[:, 384:388],
                                             bc[:, 388:392])
        ident = sb("ident", [P, P])
        onesm = sb("onesm", [P, P])
        incl = sb("incl", [P, P])
        away = sb("away", [P, P])
        up = sb("up", [P, P])
        same = sb("same", [P, P])
        half = sb("half", [P, NT, P])
        lev = sb("lev", [P, len(LEVELS), P])
        cfill = sb("cfill", [P, 3 * P])
        cfills = [cfill[:, 0:P], cfill[:, P:3 * P]]
        rc = sb("rc", [P, NT, 2 * ROT])
        rs = sb("rs", [P, NT, 2 * ROT])
        rtmp = sb("rtmp", [P, NT, 9, 2 * ROT])
        rtmp2 = sb("rtmp2", [P, NT, 9, 2 * ROT])
        inv = sb("inv", [P, ROT])
        posi = sb("posi", [P, NT], I32)
        posf = sb("posf", [P, NT])
        mhalf = sb("mhalf", [P, 16])
        sm = sb("sm", [P, 320])
        ms, rstd = sm[:, 268:272], sm[:, 0:2]
        msa, rsa = sm[:, 4:8], sm[:, 8:12]
        mss, rss = sm[:, 12:14], sm[:, 14:16]
        l2s, l2r = sm[:, 16:32], sm[:, 32:48]
        ab = sm[:, 48:64].rearrange("p (t c) -> p t c", t=NT)
        ga1, ga2, ga3 = sm[:, 64:72], sm[:, 72:80], sm[:, 80:88]
        gg_, beta = sm[:, 88:96], sm[:, 96:104]
        gc, glast = sm[:, 104:112], sm[:, 112:120]
        ngc, egc, ekd = sm[:, 120:128], sm[:, 128:136], sm[:, 136:144]
        alog = sm[:, 144:148]
        mean = sm[:, 2:4]
        egl = sm[:, 148:164].rearrange("p (c h) -> p c h", c=NCH)
        egl2 = sm[:, 164:172].rearrange("p (c b) -> p c b", c=NCH)
        iw = sm[:, 172:180].rearrange("p (t h) -> p t h", t=NT)
        m8 = sm[:, 180:196].rearrange("p (t k) -> p t k", t=NT)
        dmx, dsum = sm[:, 196:204], sm[:, 204:212]
        xmx, xnb, xsum = sm[:, 212:220], sm[:, 220:228], sm[:, 228:236]
        gos, gor = sm[:, 236:244], sm[:, 244:252]
        msb = sm[:, 252:268]


        score = sb("score", [P, 3 * P])
        scz = sb("scz", [P, 2, S + 2])
        mixer_only = ExitStack()

        def sb(name, shape, dt=F32):
            return mixer_only.enter_context(nc.sbuf_tensor(name, shape, dt))

        g1 = sb("g1", [P, 2048])
        g2 = sb("g2", [P, 2048])
        kxT = sb("kxT", [P, KC, S])
        arena_a = sb("arena_a", [P, 6 * (S + 3)])
        z = arena_a[:, :].rearrange("p (b s) -> p b s", b=6)
        ET = arena_a[:, 0:1024].rearrange("p (t h c) -> p t h c", t=NT, h=H)
        arena_b = sb("arena_b", [P, 1536])
        cv = arena_b[:, :].rearrange("p (b s) -> p b s", b=6)
        Tm = arena_b[:, 0:1024].rearrange("p (t h c) -> p t h c", t=NT, h=H)
        us = arena_b[:, 1024:1536].rearrange("p (t c) -> p t c", t=NT)
        qk_buf = sb("qk_buf", [P, 1024])
        qk = qk_buf[:, :].rearrange("p (t h c) -> p t h c", t=NT, h=2 * H)
        Um = qk_buf[:, :].rearrange("p (t h c) -> p t h c", t=NT, h=H)
        Sm_buf = sb("Sm_buf", [P, 1024])
        Sm = Sm_buf[:, :].rearrange("p (t h c) -> p t h c", t=NT, h=H)
        Bm = [sb(f"Bm{i}", [P, NT, H, P]) for i in range(2)]
        kb, vb, kbg, kd = (g1[:, 512 * i:512 * i + 512].rearrange("p (t c) -> p t c", t=NT) for i in range(4))
        kT, kbT, qT, qgT = (g2[:, 512 * i:512 * i + 512].rearrange("p (b s) -> p b s", b=2) for i in range(4))
        os_ = kb.rearrange("p t (h c) -> p t h c", h=H)
        PT = g2[:, 0:1536]
        g3 = sb("g3", [P, 2048])
        AE = g3[:, 0:1024].rearrange("p (t h c) -> p t h c", t=NT, h=H)
        AT = g3[:, 1024:2048].rearrange("p (t h c) -> p t h c", t=NT, h=H)
        wT = sb("wT", [P, 2, S])
        qg = wT[:, :, :].rearrange("p b s -> p (b s)").rearrange("p (t c) -> p t c", t=NT)
        vnew = sb("vnew", [P, NT, GW])
        gv = vnew
        state = sb("state", [P, 2, HD])
        state_d = sb("state_d", [P, 2, HD])
        gate = sb("gate", [P, NT, GW])
        R_buf = sb("R_buf", [P, NT * 10 * HD])
        R = R_buf[:, :].rearrange("p (t h c) -> p t h c", t=NT, h=10)
        rel = R_buf[:, 0:1024]
        Pds = [arena_b[:, 0:512], R_buf[:, 0:1024]]
        dk = sb("dk", [P, NT, GW])
        dv = sb("dv", [P, NT, GW])
        dqT = sb("dqT", [P, 2, S])
        diqT = arena_a[:, 1024:1536].rearrange("p (b s) -> p b s", b=2)
        dikT = sb("dikT", [P, S])
        dkT = sb("dkT", [P, 2, S])
        cT = sb("cT", [P, S])
        work = [score[:, 0:P], score[:, P:3 * P]]
        nbias = sb("nbias", [P, 3 * P])
        cn = nbias[:, 0:NT * LAT].rearrange("p (t c) -> p t c", t=NT)
        nb = [nbias[:, 0:P], nbias[:, P:3 * P]]
        sch = sb("sch", [P, 2, S])
        sco = sb("sco", [P, 2, S])
        xP = g1[:, 0:1024].rearrange("p (b t s) -> p b t s", b=2, t=NT)
        xPT = g1[:, 1024:2048].rearrange("p (b k s) -> p b k s", b=2, k=2)
        xqT = g2[:, :].rearrange("p (c s) -> p c s", c=KC)
        oT = yT
        sgwT = arena_a[:, 1024:1536].rearrange("p (h s) -> p h s", h=H)
        zeros, stairs = yT[:, 6, 0:P], yT[:, 7, 0:P]
        mixer_only.close()
        split = [[ctx.enter_context(nc.sbuf_tensor(f"{n}_{part}", shape, F32R)) for part in ("high", "low")]
                 for n, shape in [("xT", [P, KC, S]), ("hidden", [P, 2 * 2 * S])]
                 + [(f"w{i}", [P, 2048]) for i in range(SETS)]]
        xT_parts = split[0]
        hid_parts = [v[:, :].rearrange("p (b k s) -> p b k s", b=2, k=2) for v in split[1]]
        w_parts = split[2:]

        bank = [ctx.enter_context(nc.psum_tensor(f"bank{i}", [P, 512], F32)) for i in range(8)]

        def b2(i):
            return bank[i][:, :].rearrange("p (k s) -> p k s", k=2)

        def norm_bank(k):
            return 4 if k < 2 else 0

        def b4(i):
            return bank[i][:, :].rearrange("p (k s) -> p k s", k=4)

        wide = {n: a[n].rearrange("l (c p) n -> p l c n", p=P)
                for n in ("ffn1_wg", "ffn1_wu", "ffn1_wd", "ffn2_wg", "ffn2_wu", "ffn2_wd", "w_mix_in",
                          "w_mix_out", "xa_wq", "xa_wk", "xa_wv", "xa_wo")}
        x_v = a["x"].rearrange("b (t p) d -> p (b t) d", p=P)
        mem_v = a["mem"].rearrange("b (t p) d -> p (b t) d", p=P)
        out_v = out.rearrange("b (t p) d -> p (b t) d", p=P)

        landed = [sg.sem(f"unit_landed{i}") for i in range(RING)]
        mixer_unit_used = sg.sem("mixer_unit_used")

        def uses(slot):
            return len(range(slot, N_UNITS, RING))

        def unit_landed(pos, layer, it=0):
            s = pos % RING
            return landed[s], (layer * uses(s) + pos // RING + it) * 16 + 16

        def unit_used(pos, layer):
            return mixer_unit_used, layer * (U_FFN2 - U_MIX) + pos - U_MIX + 1

        def as_cols(pos, w=256):
            return ring[pos % RING][:, 0:KC * w].rearrange("p (c n) -> p c n", c=KC)

        def as_rows(pos):
            return ring[pos % RING][:, :].rearrange("p (c n) -> p c n", c=2)

        mem_in, mixer_par_loaded = sg.sem("mem_in"), sg.sem("mixer_par_loaded")
        x_loaded, mem_stored, out_done = sg.sem("x_loaded"), sg.sem("mem_stored"), sg.sem("out_done")
        small_loaded = sg.sem("small_loaded")
        mem_loaded, par_loaded = sg.sem("mem_loaded"), sg.sem("par_loaded")
        N_ROW_LOADS, N_MIXER_LOADS = 7, 11

        high_ready, low_ready, split_used = sg.sem("high_ready"), sg.sem("low_ready"), sg.sem("split_used")

        def nth(l, which, n):
            return (l * 2 + which) * FFN_UNITS + n + 1

        def set_free(l, which, n):
            return split_used, nth(l, which, n)

        def products_done(l, which, n):
            return split_used, nth(l, which, n) + SETS

        def low_done(l, which, n):
            return low_ready, nth(l, which, n) + RING

        def slot_free(pos, l, it=0):
            before = pos - RING
            if not isinstance(it, int):
                which = int(pos >= U_FFN2)
                return low_done(l, which, it * 6 + (before - which * U_FFN2))
            if before < 0:
                return low_done(l - 1, 1, (N_UNITS - 1 - pos) // RING * RING + pos - U_FFN2)
            if U_MIX <= before < U_FFN2:
                return unit_used(before, l)
            return low_done(l, int(before >= U_FFN2), before % U_FFN2)

        def step_of(l, which, s):
            return (l * 2 + which) * STEPS + s + 1

        def blocks_of(l, which, s):
            return (l * 2 + which) * 2 * STEPS + 2 * s + 2 + 4

        def apart(eng):
            eng.sem_inc(sg.sem("waited"), 1)

        block = ctx.enter_context(nc.Block())

        @block.sync
        def _(sp):
            sg.begin(sp, "params_used")
            sp.sem_inc(low_ready, RING)
            sp.dma_start(vx[:, :, :], mem_v).then_inc(mem_in, 16)
            sp.dma_start(posi[:, :], a["positions"].rearrange("b (t p) -> p (b t)", p=P),
                         allow_slow_non_contiguous=True).then_inc(small_loaded, 16)
            sp.dma_start(x[:, :, :], x_v).then_inc(x_loaded, 16)

            def params(l):
                def load(dst, src):
                    sp.dma_start(dst, src).then_inc(par_loaded, 16)
                sp.wait_ge(*sg.at("params_used", l, 0))
                apart(sp)
                for r, n in ((R_FFN1, "ffn1_norm"), (R_MIX, "mix_norm"), (R_XA, "xa_norm"), (R_MEM, "mem_norm"),
                             (R_FFN2, "ffn2_norm")):
                    load(rows[r:r + KC, :], a[n].rearrange("l (c p) -> c l p", p=P)[:, l, :])
                load(rows[R_SGB:R_SGB + H, :], a["sg_b"].rearrange("l h t -> h l t")[:, l, :])
                load(rows[R_KV:R_KV + 1, :], a["kv_norm"][bass.ds(l, 1), :])

            def mixer_params(l):
                def load(dst, src):
                    sp.dma_start(dst, src).then_inc(mixer_par_loaded, 16)
                load(wab[:, :, :], wide["w_mix_in"][:, l, :, C_GA:C_GA + 8])
                load(w_kv[:, 0, :], a["w_uk"].rearrange("l p n -> p l n")[:, l, :])
                load(w_kv[:, 1, :], a["w_uv"].rearrange("l p n -> p l n")[:, l, :])
                load(sgw[:, :, :], a["sg_w"].rearrange("l h t s -> t l h s")[:, l, :, :])
                load(scw[:, :, :], a["sc_conv"].rearrange("l (b p) j -> p l b j", p=P)[:, l, :, :])
                load(gcw[:, :, :], a["gdn_conv"].rearrange("l (b p) j -> p l b j", p=P)[:, l, :, :])
                for dst, n, w in ((b_sgn, "sg_norm", GW), (b_ikn, "idx_k_norm", HD), (b_gon, "gdn_out_norm", HD),
                                  (b_alog, "gdn_a_log", H), (b_dt, "gdn_dt_bias", H)):
                    load(dst, a[n][bass.ds(l, 1), :].broadcast_to([P, w]))

            def unit(dst, src, pos, l, it=0):
                sp.wait_ge(*slot_free(pos, l, it))
                apart(sp)
                sp.dma_start(dst, src).then_inc(landed[pos % RING], 16)

            def ffn_units(l, n, base):
                def gate_up(pos, c0, it=0):
                    for i, w in enumerate(("wg", "wu")):
                        unit(as_cols(pos + i), wide[f"{n}_{w}"][:, l, :, c0], pos + i, l, it)

                def down(pos, r0, it=0):
                    unit(as_rows(pos), wide[f"{n}_wd"][:, l, r0, :], pos, l, it)

                def pair(it):
                    gate_up(base + 2, bass.ds(it * 512 + 256, 256), it)
                    down(base + 4, bass.ds(it * 4, 2), it)
                    gate_up(base + 5, bass.ds(it * 512 + 512, 256), it)
                    down(base + 7, bass.ds(it * 4 + 2, 2), it)

                gate_up(base, slice(0, 256))
                gate_up(base + 2, slice(256, 512))
                down(base + 4, slice(0, 2))
                gate_up(base + 5, slice(512, 768))
                down(base + 7, slice(2, 4))
                if n == "ffn1":
                    mixer_params(l)
                with sp.Fori(1, PAIRS) as it:
                    pair(it)
                down(base + 2 + 6 * PAIRS, slice(2 * STEPS - 2, 2 * STEPS))

            with sp.Fori(0, DEPTH) as l:
                params(l)
                ffn_units(l, "ffn1", U_FFN1)
                for i, (c, w) in enumerate(MIX_COLS):
                    unit(as_cols(U_MIX + i, w), wide["w_mix_in"][:, l, :, c:c + w], U_MIX + i, l)
                    if i == 5:
                        sp.wait_ge(*sg.at("hT_transposed", l, 8))
                        sp.wait_ge(mem_stored, 16)
                        sp.dma_start(memn, mem_scratch).then_inc(mem_loaded, 16)
                for u, n in ((U_XK, "xa_wk"), (U_XV, "xa_wv")):
                    for i in range(4):
                        unit(as_cols(u + i), wide[n][:, l, :, 256 * i:256 * i + 256], u + i, l)
                for i in range(4):
                    unit(as_rows(U_OUT + i), wide["w_mix_out"][:, l, 2 * i:2 * i + 2, :], U_OUT + i, l)
                for i in range(4):
                    unit(as_cols(U_XQ + i), wide["xa_wq"][:, l, :, 256 * i:256 * i + 256], U_XQ + i, l)
                for i in range(4):
                    unit(as_rows(U_XO + i), wide["xa_wo"][:, l, 2 * i:2 * i + 2, :], U_XO + i, l)
                ffn_units(l, "ffn2", U_FFN2)
            sp.wait_ge(*sg.at("x_updated", DEPTH - 1))
            sp.dma_start(vx[:, 0, :], a["final_norm"].rearrange("(o d) -> o d", o=1).broadcast_to([P, D]))\
                .then_inc(small_loaded, 16)
            for t in range(NT):
                sp.wait_ge(sg.sem("out_ready"), t + 1)
                sp.dma_start(out_v[:, t, :], hn[:, t, :]).then_inc(out_done, 16)
            sp.wait_ge(out_done, 16 * NT)

        @block.tensor
        def _(pe):
            def norm_transposes(ready, src=hn, bk=4):
                for t in range(NT):
                    pe.wait_ge(*ready(t))
                    for c in range(KC):
                        tr = pe.transpose(b2(bk + c // 2)[:, c % 2, t * P:t * P + P],
                                          src[:, t, c * P:c * P + P], ident[:, :])
                        if t == NT - 1 and c % 2:
                            yield tr

            def norm(l, k):
                for tr in norm_transposes(lambda t: sg.at("hn_ready", l, NT * k + t + 1), bk=norm_bank(k)):
                    tr.then_inc(sg.inc("hT_transposed"), 1)

            def hT_chunk(l, k, c):
                if c // 2 % 2:
                    pe.wait_ge(*sg.at("hT_vector", l, 2 * k + c // 4 + 1))
                else:
                    pe.wait_ge(*sg.at("hT_scalar", l, 4 * k + 2 * (c // 4) + c % 2 + 1))

            pe.sem_inc(split_used, SETS)
            pe.wait_ge(sg.sem("ident_ready"), 1)
            for tr in norm_transposes(lambda t: (sg.sem("mem_hn_ready"), t + 1), src=vx, bk=0):
                tr.then_inc(sg.sem("mem_transposed"), 1)

            def feature_major(pos, bk, src, l, norm_k=None):
                pe.wait_ge(*unit_landed(pos, l))
                w = as_cols(pos)
                for b in range(2):
                    for c in range(KC):
                        if norm_k is not None and b == 0 and c % 2 == 0:
                            hT_chunk(l, norm_k, c)
                            hT_chunk(l, norm_k, c + 1)
                        mm = pe.matmul(b2(bk)[:, b, :], w[:, c, b * P:b * P + P], src[:, c, :],
                                       start=(c == 0), stop=(c == KC - 1))
                mm.then_inc(mixer_unit_used, 1)

            def token_major(pos, bk, src, l, w=256):
                pe.wait_ge(*unit_landed(pos, l))
                wt = as_cols(pos, w)
                for t in range(NT):
                    for c in range(KC):
                        mm = pe.matmul(b2(bk)[:, t, 0:w], src[:, c, t * P:t * P + P], wt[:, c, :],
                                       start=(c == 0), stop=(c == KC - 1))
                mm.then_inc(mixer_unit_used, 1)

            def rows_product(pos, src, c0, bk, l, first, last, it=0):
                pe.wait_ge(*unit_landed(pos, l, it))
                w = as_rows(pos)
                for t in range(NT):
                    for n in range(2):
                        for c in range(2):
                            mm = pe.matmul(bank[bk + 2 * t + n][:, :], src[:, c0 + c, t * P:t * P + P],
                                           w[:, c, 512 * n:512 * n + 512],
                                           start=(first and c == 0), stop=(last and c == 1),
                                           skip_group_check=True)
                        if last and (t, n) != (NT - 1, 1):
                            mm.then_inc(sg.inc("bank_summed"), 1)
                mm.then_inc(mixer_unit_used, 1)

            def ffn(l, which):
                def gate_or_up(k, n, par, s):
                    w_hl = [v[:, :].rearrange("p (c n) -> p c n", c=KC) for v in w_parts[n[1]]]
                    n = n[0]
                    opening = isinstance(n, int) and n == 0
                    if k == 0:
                        pe.wait_ge(sg.sem("hid_ready"), blocks_of(l, which, s - 2))
                    def products(b, pairs, first=True, last=True):
                        for c in range(KC):
                            if opening and b == 0 and first and c % 2 == 0:
                                pe.wait_ge(*sg.at("xT_low_ready", l, 4 * which + c // 2 + 1))
                            for i, (wp, xp) in enumerate(pairs):
                                mm = pe.matmul(b2(4 + 2 * par + b)[:, k, :], w_hl[wp][:, c, b * P:b * P + P],
                                               xT_parts[xp][:, c, :], start=(first and c == 0 and i == 0),
                                               stop=(last and c == KC - 1 and i == len(pairs) - 1),
                                               skip_group_check=opening)
                        return mm

                    if opening:
                        pe.wait_ge(high_ready, nth(l, which, n))
                        for b in range(2):
                            products(b, HIGH_WEIGHT, last=False)
                        pe.wait_ge(*low_done(l, which, n))
                        for b in range(2):
                            mm = products(b, LOW_WEIGHT, first=False)
                    else:
                        pe.wait_ge(*low_done(l, which, n))
                        mm = products(0, HIGH_WEIGHT + LOW_WEIGHT)
                        if k == 1:
                            mm.then_inc(sg.sem("first_block_done"), 1)
                        mm = products(1, HIGH_WEIGHT + LOW_WEIGHT)
                    mm.then_inc(split_used, 1)

                def down(n, par, s, first=False, last=False):
                    w_hl = [v[:, :].rearrange("p (c n) -> p c n", c=2) for v in w_parts[n[1]]]
                    n = n[0]
                    pe.wait_ge(sg.sem("hid_low_ready"), step_of(l, which, s))
                    pe.wait_ge(*low_done(l, which, n))
                    for t in range(NT):
                        for half_ in range(2):
                            for c in range(2):
                                for i, (wp, xp) in enumerate(HIGH_WEIGHT + LOW_WEIGHT):
                                    mm = pe.matmul(bank[2 * t + half_][:, :], hid_parts[xp][:, par, c, t * P:t * P + P],
                                                   w_hl[wp][:, c, 512 * half_:512 * half_ + 512],
                                                   start=(first and c == 0 and i == 0), stop=(last and c == 1 and i == 2),
                                                   skip_group_check=True)
                            if last and (t, half_) != (NT - 1, 1):
                                mm.then_inc(sg.inc("bank_summed"), 1)
                    mm.then_inc(split_used, 1)

                def pair(s, first=False):
                    n = 3 * s + 2
                    for par in (1, 0):
                        gate_or_up(0, (n, 2), par, s + 1)
                        gate_or_up(1, (n + 1, 0), par, s + 1)
                        down((n + 2, 1), 1 - par, s, first=first and par == 1)
                        s, n = s + 1, n + 3

                gate_or_up(0, (0, 0), 0, 0)
                gate_or_up(1, (1, 1), 0, 0)
                pair(0, first=True)
                with pe.Fori(1, PAIRS) as it:
                    pair(it * 2)
                down((FFN_UNITS - 1, (FFN_UNITS - 1) % SETS), 0, STEPS - 1, last=True)

            def hs(h):
                return slice(HD * (h % 2), HD * (h % 2) + HD)

            def mixer(l):
                feature_major(U_GQ, 0, hT, l, norm_k=1)
                feature_major(U_GK, 1, hT, l)
                feature_major(U_GV, 2, hT, l)
                for t in range(NT):
                    for c in range(KC):
                        mm = pe.matmul(bank[3][:, 8 * t:8 * t + 8], hT[:, c, t * P:t * P + P], wab[:, c, :],
                                       start=(c == 0), stop=(c == KC - 1))
                mm.then_inc(sg.inc("ab_projected"), 1)
                token_major(U_Q, 4, hT, l)
                token_major(U_CKV, 5, hT, l)
                token_major(U_IQ1, 6, hT, l, W_IQ1)
                pe.wait_ge(*sg.at("g_ready", l))
                pe.matmul(bank[3][:, 32:40], incl[:, :], gg_, start=True, stop=True)
                pe.matmul(bank[3][:, 64:72], same[:, :], gg_, start=True, stop=True)
                for c in range(NCH):
                    mm = pe.matmul(bank[3][:, 96 + 4 * c:100 + 4 * c], half[:, c % 2, :],
                                   gg_[:, 4 * (c // 2):4 * (c // 2) + 4], start=True, stop=True)
                mm.then_inc(sg.inc("gates_summed"), 1)
                token_major(U_SGV, 7, hT, l)
                pe.wait_ge(*sg.at("silu_done", l))
                for t in range(NT):
                    for b in range(4):
                        tr = pe.transpose(b4(t)[:, b, :], cv[:, b, t * P:t * P + P], ident[:, :])
                    tr.then_inc(sg.inc("qkv_transposed"), 1)
                for t in range(NT):
                    for b in range(2):
                        tr = pe.transpose(b4(2)[:, 2 * t + b, :], cv[:, 4 + b, t * P:t * P + P], ident[:, :])
                tr.then_inc(sg.inc("qkv_transposed"), 1)
                pe.wait_ge(*sg.at("cn_ready", l))
                pe.wait_ge(*sg.at("q_copied", l))
                for t in range(NT):
                    tr = pe.transpose(bank[4][:, t * P:t * P + P], cn[:, t, :], ident[:, :])
                tr.then_inc(sg.inc("c_transposed"), 1)
                pe.wait_ge(*sg.at("iq1_copied", l))
                token_major(U_SGU, 6, hT, l)
                pe.wait_ge(*sg.at("cT_ready", l))
                for t in range(NT):
                    pe.matmul(bank[4 + t][:, :], cT[:, t * P:t * P + P],
                              w_kv[:, :, :].rearrange("p i n -> p (i n)"), start=True, stop=True)\
                        .then_inc(sg.inc("kv_up"), 1)
                pe.wait_ge(*sg.at("gm_ready", l))
                pe.wait_ge(*sg.at("sums_copied", l))
                pe.matmul(bank[3][:, :], onesm[:, :], Sm_buf[:, 0:512], start=True, stop=True)\
                    .then_inc(sg.inc("gc_rows"), 1)
                pe.wait_ge(*sg.at("v_copied", l))
                pe.matmul(bank[2][:, :], onesm[:, :], Sm_buf[:, 512:1024], start=True, stop=True)\
                    .then_inc(sg.inc("gc_rows"), 1)
                pe.wait_ge(*sg.at("sgv_gelu", l))
                feature_major(U_SCC, 7, hT, l)
                for i, (src, bk, ev) in enumerate(((lambda t, b: qk[:, t, 4 + 2 * b:6 + 2 * b, :].rearrange("p h c -> p (h c)"), 0, "qk_scaled"),
                                                   (lambda t, b: kb[:, t, b * P:b * P + P], 1, "kb_ready"),
                                                   (lambda t, b: qk[:, t, 2 * b:2 * b + 2, :].rearrange("p h c -> p (h c)"), 0, "qk_scaled"),
                                                   (lambda t, b: qg[:, t, b * P:b * P + P], 1, "qg_ready"))):
                    pe.wait_ge(*sg.at(ev, l))
                    if i >= 2:
                        pe.wait_ge(*sg.at("gT_copied", l, i - 1))
                    for b in range(2):
                        for t in range(NT):
                            tr = pe.transpose(b2(bk)[:, b, t * P:t * P + P], src(t, b), ident[:, :])
                    tr.then_inc(sg.inc("gT_transposed"), 1)
                pe.wait_ge(*sg.at("sgu_gelu", l))
                feature_major(U_SCH, 6, hT, l)
                pe.wait_ge(*sg.at("rope_q", l))
                pe.wait_ge(*sg.at("kv_copied", l))
                for bk, s0, n in ((4, 0, 2), (5, 4, 2), (4, 8, 1), (5, -1, 2)):
                    if (bk, s0) == (4, 8):
                        pe.wait_ge(*sg.at("dT_copied", l, 1))
                    if s0 < 0:
                        pe.wait_ge(*sg.at("dT_copied", l, 2))
                        pe.wait_ge(*sg.at("rope_k", l))
                    for b in range(n):
                        for t in range(NT):
                            src = (dk[:, t, b * P:b * P + P] if s0 < 0 else
                                   R[:, t, s0 + 2 * b:s0 + 2 * b + 2, :].rearrange("p h c -> p (h c)"))
                            tr = pe.transpose(b2(bk)[:, b, t * P:t * P + P], src, ident[:, :])
                    tr.then_inc(sg.inc("dT_transposed"), 1)
                pe.wait_ge(*sg.at("gT_copied", l))
                pe.wait_ge(*sg.at("ET_read", l))
                for t in range(NT):
                    for odd in range(2):
                        for i, src in enumerate((kbT, qT)):
                            for b in range(2):
                                h = 2 * b + odd
                                mm = pe.matmul(b4(2 * t + odd)[:, 2 * i + b, :], kT[hs(h), b, t * P:t * P + P],
                                               src[hs(h), b, t * P:t * P + P], start=True, stop=True)
                        mm.then_inc(sg.inc("kq_done"), 1)
                pe.wait_ge(*sg.at("dT_copied", l))
                for t in range(NT):
                    n = P * (t + 1)
                    for odd in range(2):
                        if t:
                            pe.wait_ge(*sg.at("relu_done", l, odd + 1))
                        for b in range(2):
                            h = 2 * b + odd
                            mm = pe.matmul(bank[4 + odd][:, n * b:n * b + n], diqT[hs(h), b, t * P:t * P + P],
                                           dikT[hs(h), 0:n], start=True, stop=True)
                        mm.then_inc(sg.inc("index_scores"), 1)
                pe.wait_ge(*sg.at("scc_copied", l))
                feature_major(U_SCB, 7, hT, l)

                def level_u(i, t):
                    pe.wait_ge(*sg.at("B_ready", l, NT * i + t + 1))
                    if i:
                        pe.wait_ge(*sg.at("TS_ready", l, 2 * (NT * (i - 1) + t) + 2))
                    else:
                        pe.wait_ge(*sg.at("AE_ready", l))
                    for h in range(H):
                        mm = pe.matmul(b4(2 * t)[:, h, :], Bm[i % 2][:, t, h, :],
                                       ident[:, :] if i == 0 else Tm[:, t, h, :], start=True, stop=True)
                    mm.then_inc(sg.inc("U_done"), 1)

                def level_ts(i, t):
                    pe.wait_ge(*sg.at("U_copied", l, NT * (i - 1) + t + 1))
                    if i < len(LEVELS) - 1:
                        for h in range(H):
                            mm = pe.matmul(b4(2 * t + 1)[:, h, :], Sm[:, t, h, :], Um[:, t, h, :], start=True, stop=True)
                        mm.then_inc(sg.inc("TS_done"), 1)
                    for h in range(H):
                        mm = pe.matmul(b4(2 * t)[:, h, :], Um[:, t, h, :], Sm[:, t, h, :], start=True, stop=True)
                    mm.then_inc(sg.inc("TS_done"), 1)

                fillers = {1: lambda: (pe.wait_ge(*sg.at("sch_copied", l)), token_major(U_GG, 6, hT, l)),
                           2: lambda: xa_key(0), 3: lambda: xa_key(1), 4: lambda: xa_key(2), 5: lambda: xa_key(3)}

                def xa_bank(i):
                    if i == 0:
                        pe.wait_ge(*sg.at("scb_copied", l))
                        pe.wait_ge(*sg.at("memn_ready", l))
                    elif i == 1:
                        pe.wait_ge(*sg.at("gate_read", l))
                    else:
                        pe.wait_ge(*sg.at("xkv_copied", l, i - 1))
                    return 7 - i % 2

                def xa_key(i):
                    feature_major(U_XK + i, xa_bank(i), memn, l)

                def xa_value(i):
                    token_major(U_XV + i, xa_bank(4 + i), memn, l)

                for t in range(NT):
                    level_u(0, t)
                for i in range(1, len(LEVELS)):
                    for t in range(NT):
                        level_u(i, t)
                    fillers[i]()
                    for t in range(NT):
                        level_ts(i, t)
                xa_value(0)
                pe.wait_ge(*sg.at("TS_ready", l))
                for t in range(NT):
                    for h in range(H):
                        mm = pe.matmul(b2(0)[:, t, HD * h:HD * h + HD], Sm[:, t, h, :],
                                       vb[:, t, HD * h:HD * h + HD], start=True, stop=True)
                mm.then_inc(sg.inc("u_done"), 1)
                for t in range(NT):
                    for h in range(H):
                        mm = pe.matmul(b2(1)[hs(h), h // 2, t * P:t * P + P], kbg[:, t, HD * h:HD * h + HD],
                                       Sm[:, t, h, :], start=True, stop=True)
                mm.then_inc(sg.inc("w_done"), 1)
                xa_value(1)
                def chunk_read(c):
                    t, r = c // 2, CH * (c % 2)
                    pe.wait_ge(*sg.at("uw_copied", l))
                    pe.wait_ge(*sg.at("state_ready", l, c + 1))
                    if c:
                        pe.wait_ge(*sg.at("qs_copied", l, 2 * c))
                    apart(pe)
                    for odd in range(2):
                        for i, src in enumerate((wT, qgT)):
                            for b in range(2):
                                rows_ = slice(HD * odd, HD * odd + HD)
                                mm = pe.matmul(bank[odd][r:r + CH, P * i + HD * b:P * i + HD * b + HD],
                                               src[rows_, b, t * P + r:t * P + r + CH], state[rows_, b, :],
                                               start=True, stop=True)
                    mm.then_inc(sg.inc("ws_done"), 1)

                def chunk_write(c):
                    t, r = c // 2, CH * (c % 2)
                    pe.wait_ge(*sg.at("vnew_ready", l, 2 * c + 2))
                    apart(pe)
                    for h in range(H):
                        mm = pe.matmul(bank[2][hs(h), HD * (h // 2):HD * (h // 2) + HD], kd[r:r + CH, t, HD * h:HD * h + HD],
                                       vnew[r:r + CH, t, HD * h:HD * h + HD], start=True, stop=True)
                    mm.then_inc(sg.inc("kv_done"), 1)
                    for h in range(H):
                        mm = pe.matmul(b2(3)[r:r + CH, t, HD * h:HD * h + HD], AT[r:r + CH, t, h, r:r + CH],
                                       vnew[r:r + CH, t, HD * h:HD * h + HD], start=True, stop=True)
                    mm.then_inc(sg.inc("o_done"), 1)

                def dsa_logits(t):
                    pe.wait_ge(*(sg.at("logits_read", l, 2) if t else sg.at("relu_done", l)))
                    n = P * (t + 1)
                    for odd in range(2):
                        for b in range(2):
                            h = 2 * b + odd
                            mm = pe.matmul(bank[4 + odd][:, n * b:n * b + n], dqT[hs(h), b, t * P:t * P + P],
                                           dkT[hs(h), b, 0:n], start=True, stop=True)
                    mm.then_inc(sg.inc("logits_done"), 1)

                def dsa_transposes(i):
                    if i == 0:
                        pe.wait_ge(*sg.at("probs_ready", l, 1))
                        for h in range(H):
                            tr = pe.transpose(b4(7)[:, h, :], Pds[0][:, P * h:P * h + P], ident[:, :])
                    else:
                        pe.wait_ge(*sg.at("probs_ready", l, 2))
                        pe.wait_ge(*sg.at("logits_read", l))
                        for h in range(H):
                            tr = pe.transpose(b4(5 if i == 1 else 4)[:, h, :],
                                              Pds[1][:, 2 * P * h + P * (i - 1):2 * P * h + P * i], ident[:, :])
                    tr.then_inc(sg.inc("PT_transposed"), 1)

                def dsa_values():
                    pe.wait_ge(*sg.at("PT_copied", l))
                    for i, h in enumerate((0, 2, 1, 3)):
                        pe.matmul(b2(5)[hs(h), h // 2, 0:P], dv[:, 0, HD * h:HD * h + HD], PT[:, P * i:P * i + P],
                                  start=True, stop=True)
                        for k in range(2):
                            mm = pe.matmul(b2(5)[hs(h), h // 2, P:2 * P], dv[:, k, HD * h:HD * h + HD],
                                           PT[:, 512 * (k + 1) + P * i:512 * (k + 1) + P * i + P],
                                           start=(k == 0), stop=(k == 1))
                    mm.then_inc(sg.inc("dsa_out"), 1)

                chunk_read(0)
                dsa_logits(0)
                chunk_write(0)
                chunk_read(1)
                dsa_logits(1)
                xa_value(2)
                chunk_write(1)
                chunk_read(2)
                xa_value(3)
                chunk_write(2)
                chunk_read(3)
                pe.wait_ge(*sg.at("xkv_copied", l, 7))
                for h in range(H):
                    tr = pe.transpose(b4(7)[:, h, :], sgw[:, h, :], ident[:, :])
                tr.then_inc(sg.inc("sgw_transposed"), 1)
                chunk_write(3)
                pe.wait_ge(*sg.at("xkv_copied", l))
                pe.wait_ge(*sg.at("sgwT_ready", l))
                pe.wait_ge(*sg.at("sgn_ready", l))
                for t in range(NT):
                    for h in range(H):
                        mm = pe.matmul(b2(6)[:, t, HD * h:HD * h + HD], sgwT[:, h, :], sgn[:, t, HD * h:HD * h + HD],
                                       start=True, stop=True)
                mm.then_inc(sg.inc("sg_mixed"), 1)
                dsa_transposes(0)
                pe.wait_ge(*sg.at("sg_out", l))
                for b in range(2):
                    for t in range(NT):
                        tr = pe.transpose(b2(2)[:, b, t * P:t * P + P], sgj[:, t, b * P:b * P + P], ident[:, :])
                tr.then_inc(sg.inc("sg_transposed"), 1)
                dsa_transposes(1)
                dsa_transposes(2)
                dsa_values()
                pe.wait_ge(*sg.at("gdn_out", l))
                for b in range(2):
                    for t in range(NT):
                        tr = pe.transpose(b2(0)[:, b, t * P:t * P + P], vnew[:, t, b * P:b * P + P], ident[:, :])
                tr.then_inc(sg.inc("gdn_transposed"), 1)
                pe.wait_ge(*sg.at("yT_ready", l, 3))
                pe.wait_ge(*sg.at("sc_out", l))
                rows_product(U_OUT, yT, 0, 4, l, True, False)
                rows_product(U_OUT + 1, yT, 2, 4, l, False, False)
                rows_product(U_OUT + 2, yT, 4, 4, l, False, False)
                rows_product(U_OUT + 3, yT, 6, 4, l, False, True)

            def cross(l):
                def queries(h):
                    feature_major(U_XQ + h, 4 * (h % 2), hT, l, norm_k=None if h else 2)

                def logits(h):
                    pe.wait_ge(*sg.at("xq_copied", l, h + 1))
                    bk = (1, 5, 1, 0)[h]
                    if h == 2:
                        pe.wait_ge(*sg.at("xexp_done", l, NT))
                    for t in range(NT):
                        for b in range(2):
                            mm = pe.matmul(b2(bk)[:, t, :], xqT[:, 2 * h + b, t * P:t * P + P], kxT[:, 2 * h + b, :],
                                           start=(b == 0), stop=(b == 1))
                    mm.then_inc(sg.inc("xlogits"), 1)

                def transposes(h):
                    pe.wait_ge(*sg.at("xprobs", l, h + 1))
                    if h:
                        pe.wait_ge(*sg.at("xPT_copied", l, h))
                    for k in range(2):
                        for t in range(NT):
                            tr = pe.transpose(b2(2)[:, k, t * P:t * P + P], xP[:, h % 2, t, k * P:k * P + P], ident[:, :])
                    tr.then_inc(sg.inc("xPT"), 1)

                def values(h):
                    pe.wait_ge(*sg.at("xPT_copied", l, h + 1))
                    if h:
                        pe.wait_ge(*sg.at("oT_copied", l, h))
                    for b in range(2):
                        for k in range(2):
                            mm = pe.matmul(b2(3)[:, b, :], vx[:, k, 256 * h + b * P:256 * h + b * P + P],
                                           xPT[:, h % 2, k, :], start=(k == 0), stop=(k == 1))
                    mm.then_inc(sg.inc("xvalues"), 1)

                def project(h):
                    pe.wait_ge(*sg.at("oT_copied", l, h + 1))
                    if h == 0:
                        pe.wait_ge(*sg.at("xq_copied", l))
                        pe.wait_ge(*sg.at("xexp_done", l, 2 * NT))
                    rows_product(U_XO + h, oT, 2 * h, 4, l, h == 0, h == H - 1)

                queries(0), queries(1), logits(0), queries(2), logits(1), transposes(0), queries(3), values(0)
                logits(2), transposes(1), project(0), values(1), logits(3), transposes(2), project(1)
                values(2), transposes(3), project(2), values(3), project(3)

            with pe.Fori(0, DEPTH) as l:
                pe.wait_ge(par_loaded, (l + 1) * N_ROW_LOADS * 16)
                pe.wait_ge(sg.sem("memT_copied"), 4)
                pe.wait_ge(sg.sem("hid_ready"), blocks_of(l, 0, -1))
                apart(pe)
                pe.transpose(bank[7][:, 0:N_ROWS], rows[:, :], ident[0:N_ROWS, 0:N_ROWS])\
                    .then_inc(sg.inc("rows_transposed"), 1)
                pe.wait_ge(*sg.at("cols_ready", l))
                norm(l, 0)
                ffn(l, 0)
                norm(l, 1)
                pe.wait_ge(mixer_par_loaded, (l + 1) * N_MIXER_LOADS * 16)
                mixer(l)
                norm(l, 2)
                cross(l)
                norm(l, 3)
                ffn(l, 1)

        @block.scalar
        def _(act):
            def mean_squares(l, k, signal):
                for t in range(NT):
                    for n in range(2):
                        act.wait_ge(*sg.at("x_updated", l, 4 * k - 4 + 2 * t + n + 1) if k else
                                    sg.at("x_updated", l, 2 * t + n + 1 - 4))
                        part = slice(512 * n, 512 * n + 512)
                        act.activation(hn[:, t, part], x[:, t, part], ACT.Square, scale=float(D) ** -0.5,
                                       accum_out=ms[:, 2 * t + n:2 * t + n + 1]).then_inc(signal(), 1)

            def link(ins, l):
                ins.then_inc(sg.inc("scalar_link"), 1)
                act.wait_ge(*sg.at("scalar_link", l, sg.counts["scalar_link"]))

            act.wait_ge(mem_in, 16)
            for t in range(NT):
                act.activation(yT[:, 0:4, :].rearrange("p c s -> p (c s)"), vx[:, t, :], ACT.Square,
                               scale=float(D) ** -0.5, accum_out=msb[:, 2 + t:3 + t]).then_inc(sg.sem("mem_ms"), 1)
                act.wait_ge(sg.sem("mem_ms"), t + 1)
            act.wait_ge(sg.sem("angles_ready"), 2)
            act.activation(rs[:, :, ROT:2 * ROT], rtmp[:, :, 0, 0:ROT], ACT.Sin).then_inc(sg.sem("trig_done"), 1)
            act.activation(rc[:, :, 0:ROT], rtmp[:, :, 1, 0:ROT], ACT.Sin).then_inc(sg.sem("trig_done"), 1)
            act.wait_ge(sg.sem("trig_done"), 2)
            act.activation(rs[:, :, 0:ROT], rs[:, :, ROT:2 * ROT], ACT.Copy, scale=-1.0).then_inc(sg.sem("trig_done"), 1)
            act.activation(rc[:, :, ROT:2 * ROT], rc[:, :, 0:ROT], ACT.Copy).then_inc(sg.sem("trig_done"), 1)
            act.wait_ge(sg.sem("mem_transposed"), 4)
            for i in range(4):
                act.activation(vx[:, :, :].rearrange("p t d -> p (t d)")[:, 512 * i:512 * i + 512], bank[i][:, :], ACT.Copy)\
                    .then_inc(sg.sem("memT_copied"), 1)
            act.wait_ge(sg.sem("memT_copied"), 4)
            act.dma_start(mem_scratch.rearrange("p c s -> p (c s)"), vx[:, :, :].rearrange("p t d -> p (t d)"))\
                .then_inc(mem_stored, 16)

            def norm(l, k, row):
                if k == 0:
                    act.wait_ge(x_loaded, 16)
                if k in (0, 3):
                    high(l, k // 3, (U_FFN1, U_FFN2)[k // 3], 0)
                    high(l, k // 3, (U_FFN1, U_FFN2)[k // 3], 1)
                mean_squares(l, k, lambda: sg.inc("ms_ready"))
                for i in range(4):
                    if i % 2 == 0:
                        act.wait_ge(*sg.at("hT_transposed", l, 4 * k + i + 1))
                        for c in (2 * i, 2 * i + 1):
                            act.activation(hT[:, c, :], b2(norm_bank(k) + i)[:, c % 2, :], ACT.Copy, scale=cols[:, row + c:row + c + 1])\
                                .then_inc(sg.inc("hT_scalar"), 1)
                    if k in (0, 3):
                        act.wait_ge(*(sg.at("hT_vector", l, 2 * k + i // 2 + 1) if i % 2 else
                                      sg.at("hT_scalar", l, 4 * k + i + 2)))
                        act.activation(xT_parts[0][:, 2 * i:2 * i + 2, :], hT[:, 2 * i:2 * i + 2, :], ACT.Copy)\
                            .then_inc(sg.inc("xT_high_ready"), 1)

            def high(l, which, base, n, it=0):
                act.wait_ge(*unit_landed(base + n, l, it))
                act.wait_ge(*set_free(l, which, it * 6 + n))
                act.activation(w_parts[n % SETS][0][:, :], ring[(base + n) % RING][:, :], ACT.Copy)\
                    .then_inc(high_ready, 1)

            def ffn(l, which):
                base = (U_FFN1, U_FFN2)[which]

                def step(par, s, it=0):
                    n = 3 * par + 2
                    split_next = s is not LAST
                    if split_next:
                        high(l, which, base, n, it)
                    else:
                        s = STEPS - 1
                    act.wait_ge(sg.sem("first_block_done"), step_of(l, which, s))
                    act.activation(sil[:, par, 0, :], b2(4 + 2 * par)[:, 0, :], ACT.Silu).then_inc(sg.sem("silu_ready"), 1)
                    act.wait_ge(*products_done(l, which, s * 3 + (1 if isinstance(s, int) and s == 0 else 0)))
                    act.activation(sil[:, par, 1, :], b2(5 + 2 * par)[:, 0, :], ACT.Silu).then_inc(sg.sem("silu_ready"), 1)
                    if split_next:
                        high(l, which, base, n + 1, it)
                    act.wait_ge(sg.sem("hid_ready"), blocks_of(l, which, s))
                    act.activation(hid_parts[0][:, par, :, :], hid[:, par, :, :], ACT.Copy)\
                        .then_inc(sg.sem("hid_high_ready"), 1)
                    if split_next:
                        high(l, which, base, n + 2, it)
                    else:
                        high(l, which, base, FFN_UNITS - 1)

                step(0, 0)
                step(1, 1)
                with act.Fori(1, PAIRS) as it:
                    step(0, it * 2, it)
                    step(1, it * 2 + 1, it)
                step(0, LAST)

            def mixer(l):
                def copy(dst, src, name, func=ACT.Copy, **kw):
                    act.activation(dst, src, func, **kw).then_inc(sg.inc(name), 1)

                act.wait_ge(*sg.at("pads_ready", l))
                for i, u in enumerate((U_GQ, U_GK, U_GV)):
                    act.wait_ge(*unit_used(u, l))
                    copy(z[:, 2 * i:2 * i + 2, 3:3 + S], b2(i), "z_copied")
                act.wait_ge(*sg.at("ab_projected", l))
                copy(ab, bank[3][:, 0:16].rearrange("p (t c) -> p t c", t=NT), "ab_copied")
                act.activation(alog, b_alog, ACT.Exp)
                act.wait_ge(*sg.at("soft_in", l))
                act.activation(ga2, ga2, ACT.Exp)
                link(act.activation(beta, beta, ACT.Exp, scale=-1.0), l)
                copy(ga3, ga2, "soft_ln", ACT.Ln, bias=1.0)
                act.wait_ge(*unit_used(U_Q, l))
                copy(R[:, :, 0:4, :], b2(4).rearrange("p t (h c) -> p t h c", h=4), "q_copied")
                act.wait_ge(*unit_used(U_CKV, l))
                for t in range(NT):
                    copy(cn[:, t, :], b2(5)[:, t, 0:LAT], "msa_ready", ACT.Square, scale=float(LAT) ** -0.5,
                         accum_out=msa[:, t:t + 1])
                copy(R[:, :, 4:6, :], b2(5)[:, :, LAT:256].rearrange("p t (h c) -> p t h c", h=2), "iq0_copied")
                act.wait_ge(*unit_used(U_IQ1, l))
                for t in range(NT):
                    copy(R[:, t, 8, :], b2(6)[:, t, P:P + HD], "msa_ready", ACT.Square, scale=float(HD) ** -0.5,
                         accum_out=msa[:, 2 + t:3 + t])
                copy(R[:, :, 6:8, :], b2(6)[:, :, 0:P].rearrange("p t (h c) -> p t h c", h=2), "iq1_scalar")
                copy(iw, b2(6)[:, :, P + HD:P + HD + H], "iq1_scalar", scale=0.0625)
                for i in range(3):
                    act.wait_ge(*sg.at("conv_v", l) if i == 2 else sg.at("conv_qk", l, 2 * i + 2))
                    copy(cv[:, 2 * i:2 * i + 2, :], cv[:, 2 * i:2 * i + 2, :], "silu_done", ACT.Silu)
                act.wait_ge(*unit_used(U_SGV, l))
                copy(sgv, b2(7), "sgv_gelu", ACT.Gelu_apprx_tanh)
                act.wait_ge(*sg.at("sgv_gelu", l))
                for t in range(NT):
                    copy(sgn[:, t, :], sgv[:, t, :], "mss_ready", ACT.Square, scale=float(GW) ** -0.5,
                         accum_out=mss[:, t:t + 1])
                act.wait_ge(*unit_used(U_SGU, l))
                copy(sgu, b2(6), "sgu_gelu", ACT.Gelu_apprx_tanh)
                for t in range(NT):
                    act.wait_ge(*sg.at("qkv_transposed", l, t + 1))
                    copy(Bm[0][:, t, :, :].rearrange("p h c -> p (h c)"), bank[t][:, :], "qk_squared", ACT.Square)
                act.wait_ge(*sg.at("qkv_transposed", l))
                copy(gv[:, :, :], b2(2), "v_copied")
                act.wait_ge(*sg.at("gates_summed", l))
                copy(gc, bank[3][:, 32:40], "gc_ready")
                copy(ngc, bank[3][:, 32:40], "gc_ready", scale=-1.0)
                act.activation(egl, bank[3][:, 96:112].rearrange("p (c h) -> p c h", c=NCH), ACT.Exp)
                act.activation(egc, bank[3][:, 32:40], ACT.Exp).then_inc(sg.inc("egc_ready"), 1)
                act.wait_ge(*sg.at("ekd_in", l))
                copy(ekd, ekd, "sums_copied", ACT.Exp)
                for t in range(NT):
                    act.wait_ge(*sg.at("kv_up", l, t + 1))
                    copy(dv[:, t, :], b2(4 + t)[:, 1, :], "kv_copied")
                    copy(dk[:, t, :], b2(4 + t)[:, 0, :], "kv_copied")
                act.wait_ge(*unit_used(U_SCC, l))
                copy(scz[:, :, 2:2 + S], b2(7), "scc_copied")
                for t in range(NT):
                    act.wait_ge(*sg.at("ET_in", l, t + 1))
                    for h in range(H):
                        copy(ET[:, t, h, :], ET[:, t, h, :], "ET_ready", ACT.Exp, bias=ngc[:, H * t + h:H * t + h + 1])
                for i, dst in enumerate((kT, kbT, qT, qgT)):
                    act.wait_ge(*sg.at("gT_transposed", l, i + 1))
                    copy(dst, b2(i % 2), "gT_copied")
                act.wait_ge(*unit_used(U_SCH, l))
                copy(sch[:, :, :], b2(6), "sch_copied")
                for i, (dst, src) in enumerate(((dqT[:, :, :], b2(4)), (diqT[:, :, :], b2(5)), (dikT[:, :], bank[4][:, 0:S]),
                                                (dkT[:, :, :], b2(5)))):
                    act.wait_ge(*sg.at("dT_transposed", l, i + 1))
                    copy(dst, src, "dT_copied")
                for t in range(NT):
                    n = 2 * P * (t + 1)
                    for odd in range(2):
                        act.wait_ge(*sg.at("index_scores", l, 2 * t + odd + 1))
                        if t:
                            act.wait_ge(*sg.at("score_added", l))
                        copy(rel[:, n * odd:n * odd + n], bank[4 + odd][:, 0:n], "relu_done", ACT.Relu)
                act.wait_ge(*unit_used(U_SCB, l))
                copy(yT[:, 2:4, :], b2(7), "scb_copied")
                for i in range(1, len(LEVELS)):
                    for t in range(NT):
                        act.wait_ge(*sg.at("U_done", l, NT * i + t + 1))
                        copy(Um[:, t, :, :], b4(2 * t), "U_copied")
                    if i == 1:
                        act.wait_ge(*unit_used(U_GG, l))
                        copy(gate[:, :, :], b2(6), "gate_read", ACT.Silu)
                    else:
                        act.wait_ge(*unit_used(U_XK + i - 2, l))
                        copy(kxT[:, 2 * (i - 2):2 * (i - 2) + 2, :], b2(7 - (i - 2) % 2), "xkv_copied")

                def value_copy(i):
                    act.wait_ge(*unit_used(U_XV + i, l))
                    copy(vx[:, :, 256 * i:256 * i + 256], b2(7 - i % 2), "xkv_copied")

                def read_copy(c):
                    t, r = c // 2, CH * (c % 2)
                    act.wait_ge(*sg.at("vnew_ready", l, 2 * c + 2))
                    for odd in range(2):
                        act.activation(os_[r:r + CH, t, odd:H:2, :],
                                       bank[odd][r:r + CH, P:2 * P].rearrange("p (b c) -> p b c", b=2), ACT.Copy)\
                            .then_inc(sg.inc("qs_copied"), 1)

                value_copy(0)
                act.wait_ge(*sg.at("u_done", l))
                copy(us, b2(0), "uw_copied")
                act.wait_ge(*sg.at("w_done", l))
                copy(wT[:, :, :], b2(1), "uw_copied")
                value_copy(1)

                def dsa_exp(t):
                    act.wait_ge(*sg.at("dmx_ready", l, t + 1))
                    n, Pd = P * (t + 1), Pds[t]
                    for h in range(H):
                        copy(Pd[:, n * h:n * h + n], Pd[:, n * h:n * h + n], "dexp_done", ACT.Exp,
                             bias=dmx[:, 4 * t + h:4 * t + h + 1], accum_out=dsum[:, 4 * t + h:4 * t + h + 1])

                read_copy(0)
                dsa_exp(0)
                read_copy(1)
                value_copy(2)
                read_copy(2)
                value_copy(3)
                read_copy(3)
                dsa_exp(1)
                act.wait_ge(*sg.at("PT_transposed", l, 1))
                copy(PT[:, 0:512], bank[7][:, :], "PT_copied")
                act.wait_ge(*sg.at("sg_transposed", l))
                copy(yT[:, 0:2, :], b2(2), "yT_ready")
                act.wait_ge(*sg.at("PT_transposed", l, 2))
                copy(PT[:, 512:1024], bank[5][:, :], "PT_copied")
                act.wait_ge(*sg.at("PT_transposed", l, 3))
                copy(PT[:, 1024:1536], bank[4][:, :], "PT_copied")
                act.wait_ge(*sg.at("dsa_out", l))
                copy(yT[:, 4:6, :], b2(5), "yT_ready")
                act.wait_ge(*sg.at("gdn_transposed", l))
                copy(yT[:, 6:8, :], b2(0), "yT_ready")

            def cross(l):
                def queries(h):
                    act.wait_ge(*unit_used(U_XQ + h, l))
                    act.activation(xqT[:, 2 * h:2 * h + 2, :], b2(4 * (h % 2)), ACT.Copy).then_inc(sg.inc("xq_copied"), 1)

                def exps(h):
                    act.wait_ge(*sg.at("xmax_ready", l, h + 1))
                    if h >= 2:
                        act.wait_ge(*sg.at("xPT", l, h - 1))
                    for t in range(NT):
                        act.activation(xP[:, h % 2, t, :], b2((1, 5, 1, 0)[h])[:, t, :], ACT.Exp, scale=1.0 / 16,
                                       bias=xnb[:, 2 * h + t:2 * h + t + 1], accum_out=xsum[:, 2 * h + t:2 * h + t + 1])\
                            .then_inc(sg.inc("xexp_done"), 1)

                def pt(h):
                    act.wait_ge(*sg.at("xPT", l, h + 1))
                    if h >= 2:
                        act.wait_ge(*sg.at("xvalues", l, h - 1))
                    act.activation(xPT[:, h % 2, :, :], b2(2), ACT.Copy).then_inc(sg.inc("xPT_copied"), 1)

                def outs(h):
                    act.wait_ge(*sg.at("xvalues", l, h + 1))
                    act.activation(oT[:, 2 * h:2 * h + 2, :], b2(3), ACT.Copy).then_inc(sg.inc("oT_copied"), 1)

                queries(0), queries(1), exps(0), queries(2), exps(1), pt(0), queries(3), outs(0)
                exps(2), pt(1), outs(1), exps(3), pt(2), outs(2), pt(3), outs(3)

            with act.Fori(0, DEPTH) as l:
                norm(l, 0, R_FFN1)
                ffn(l, 0)
                norm(l, 1, R_MIX)
                mixer(l)
                norm(l, 2, R_XA)
                cross(l)
                norm(l, 3, R_FFN2)
                ffn(l, 1)
            mean_squares(DEPTH, 0, lambda: sg.sem("ms_ready"))

        @block.gpsimd
        def _(pool):
            made = sg.sem("pool_made")
            n_made = [0]

            def step(ins):
                n_made[0] += 1
                ins.then_inc(made, 1)
                pool.wait_ge(made, n_made[0])

            def select(dst, src, op, fill, base, mult, pattern):
                step(pool.affine_select(out=dst, in_=src, compare_op=op, fill=fill, base=base,
                                        channel_multiplier=mult, pattern=pattern))

            step(pool.memset(zeros, 0.0))
            step(pool.memset(onesm[:, :], 1.0))
            select(ident[:, :], zeros, ALU.not_equal, 1.0, 0, 1, [[-1, P]])
            pool.memset(mhalf[:, :], -0.5).then_inc(sg.sem("ident_ready"), 1)
            pool.wait_ge(sg.sem("ident_ready"), 1)
            pool.wait_ge(sg.sem("mem_ms"), 2)
            step(pool.tensor_scalar(msb[:, 0:2], msb[:, 2:4], 1.0, EPS, ALU.mult, ALU.add))
            pool.tensor_tensor(msb[:, 4:6], msb[:, 0:2], mhalf[:, 0:2], ALU.pow).then_inc(sg.sem("mem_rstd"), 1)
            def norm(l, k, signal=sg.inc):
                for t in range(NT):
                    pool.wait_ge(*sg.at("ms_ready", l, 4 * k + 2 * t + 2))
                    if not isinstance(l, int):
                        apart(pool)
                    pool.tensor_scalar(mean[:, t:t + 1], ms[:, 2 * t:2 * t + 1], ms[:, 2 * t + 1:2 * t + 2], EPS,
                                       ALU.add, ALU.add).then_inc(signal("mean_ready"), 1)
                    pool.wait_ge(*sg.at("mean_ready", l, NT * k + t + 1))
                    pool.tensor_tensor(rstd[:, t:t + 1], mean[:, t:t + 1], mhalf[:, 0:1], ALU.pow)\
                        .then_inc(signal("rstd_ready"), 1)

            norm(0, 0, sg.sem)
            select(up[:, :], onesm[:, :], ALU.is_ge, 0.0, 0, -1, [[1, P]])
            select(half[:, 0, :], onesm[:, :], ALU.is_ge, 0.0, CH - 1, -1, [[0, P]])
            select(half[:, 1, :], onesm[:, :], ALU.is_ge, 0.0, -CH, 1, [[0, P]])

            def block_diagonal(dst, src, s):
                v = dst.rearrange("p (b c) -> p b c", c=s)
                select(v, src.rearrange("p (b c) -> p b c", c=s), ALU.is_ge, 0.0, 0, 1, [[-s, P // s], [0, s]])
                select(v, v, ALU.is_ge, 0.0, s - 1, -1, [[s, P // s], [0, s]])

            block_diagonal(same[:, :], onesm[:, :], CH)
            block_diagonal(incl[:, :], up[:, :], CH)
            step(pool.tensor_scalar(away[:, :], incl[:, :], -AWAY, AWAY, ALU.mult, ALU.add))
            for n, s in enumerate(LEVELS):
                block_diagonal(lev[:, n, :], up[:, :], 2 * s)
                if s > 1:
                    block_diagonal(stairs, up[:, :], s)
                    step(pool.tensor_tensor(lev[:, n, :], lev[:, n, :], stairs, ALU.subtract))
                else:
                    step(pool.tensor_tensor(lev[:, n, :], lev[:, n, :], ident[:, :], ALU.subtract))
            step(pool.memset(cfill[:, :], 0.0))
            for off in (0, 2 * P):
                select(cfill[:, off:off + P], cfill[:, off:off + P], ALU.is_ge, FILL, 0, 1, [[-1, P]])
            pool.memset(scz[:, :, 0:2], 0.0).then_inc(made, 1)
            pool.wait_ge(made, n_made[0] + 1)
            pool.memset(score[:, :], 0.0).then_inc(made, 1)
            pool.wait_ge(made, n_made[0] + 2)

            def link(ins, l):
                ins.then_inc(sg.inc("pool_link"), 1)
                pool.wait_ge(*sg.at("pool_link", l, sg.counts["pool_link"]))

            def rsqrt(dst, src, n, l, name, add=EPS):
                apart(pool)
                link(pool.tensor_scalar(msb[:, 0:n], src, 1.0, add, ALU.mult, ALU.add), l)
                pool.tensor_tensor(dst, msb[:, 0:n], mhalf[:, 0:n], ALU.pow).then_inc(sg.inc(name), 1)
                pool.wait_ge(*sg.at(name, l, sg.counts[name]))

            def mixer(l):
                apart(pool)
                pool.memset(z[:, :, 0:3], 0.0).then_inc(sg.inc("pads_ready"), 1)
                pool.wait_ge(*sg.at("msa_ready", l))
                rsqrt(rsa, msa, 4, l, "rsa_ready")
                pool.wait_ge(*sg.at("z_copied", l))
                for j in range(4):
                    w = broadcast_last(gcw[:, 4:6, j], S)
                    src = z[:, 4:6, j:j + S]
                    if j == 0:
                        link(pool.tensor_tensor(cv[:, 4:6, :], src, w, ALU.mult), l)
                        continue
                    link(pool.tensor_tensor(sco[:, :, :], src, w, ALU.mult), l)
                    last = pool.tensor_tensor(cv[:, 4:6, :], cv[:, 4:6, :], sco[:, :, :], ALU.add)
                    if j < 3:
                        link(last, l)
                last.then_inc(sg.inc("conv_v"), 1)
                pool.wait_ge(*sg.at("mss_ready", l))
                rsqrt(rss, mss, 2, l, "rss_ready")
                pool.wait_ge(*sg.at("l2_summed", l))
                rsqrt(l2r, l2s, 16, l, "l2_ready")
                pool.wait_ge(mem_loaded, 16 * (l + 1))
                apart(pool)
                for c in range(KC):
                    pool.tensor_scalar(memn[:, c, :], memn[:, c, :], cols[:, R_MEM + c:R_MEM + c + 1], 1.0,
                                       ALU.mult, ALU.mult).then_inc(sg.inc("memn_ready"), 1)
                pool.wait_ge(*sg.at("AE_ready", l))
                pool.wait_ge(*sg.at("l2_read", l))
                for i in range(len(LEVELS)):
                    for t in range(NT):
                        if i >= 2:
                            pool.wait_ge(*sg.at("U_done", l, NT * (i - 2) + t + 1))
                        if i == 2:
                            pool.wait_ge(*sg.at("TS_ready", l, 2 * t + 2))
                        pool.tensor_tensor(Bm[i % 2][:, t, :, :], AE[:, t, :, :],
                                           lev[:, i, :].unsqueeze(1).broadcast_to([P, H, P]), ALU.mult)\
                            .then_inc(sg.inc("B_ready"), 1)
                pool.wait_ge(*sg.at("scc_copied", l))
                pool.wait_ge(*sg.at("sch_copied", l))
                link(pool.tensor_tensor(scz[:, :, 2:2 + S], scz[:, :, 2:2 + S], sch[:, :, :], ALU.mult), l)
                link(pool.tensor_tensor(sco[:, :, :], scz[:, :, 0:S], broadcast_last(scw[:, :, 0], S), ALU.mult), l)
                for j in (1, 2):
                    link(pool.tensor_tensor(sch[:, :, :], scz[:, :, j:j + S], broadcast_last(scw[:, :, j], S), ALU.mult), l)
                    link(pool.tensor_tensor(sco[:, :, :], sco[:, :, :], sch[:, :, :], ALU.add), l)
                pool.wait_ge(*sg.at("scb_copied", l))
                pool.tensor_tensor(yT[:, 2:4, :], sco[:, :, :], yT[:, 2:4, :], ALU.mult).then_inc(sg.inc("sc_out"), 1)
                pool.wait_ge(*sg.at("gos_ready", l))
                rsqrt(gor, gos, 8, l, "gor_ready")

            with pool.Fori(0, DEPTH) as l:
                norm(l, 1)
                mixer(l)
                norm(l, 2)
                norm(l, 3)
                norm(l + 1, 0)

        @block.vector
        def _(dve):
            def link(ins, l):
                ins.then_inc(sg.inc("vector_link"), 1)
                dve.wait_ge(*sg.at("vector_link", l, sg.counts["vector_link"]))

            sg.begin(dve, "x_updated")
            dve.sem_inc(sg.sem("hid_ready"), 4)
            setup = sg.sem("vector_setup")
            n_setup = [0]

            def step(ins):
                n_setup[0] += 1
                ins.then_inc(setup, 1)
                dve.wait_ge(setup, n_setup[0])

            two_pi = 2 * np.pi
            p1 = 6.28125
            p2 = float(np.float32(np.floor((two_pi - p1) * 2.0 ** 21) / 2.0 ** 21))
            p3 = float(np.float32(two_pi - p1 - p2))
            magic = 1.5 * 2.0 ** 23
            pi_in = 3.1415925
            ang, kk, red = rtmp[:, :, 0, 0:ROT], rtmp[:, :, 2, 0:ROT], rtmp[:, :, 3, 0:ROT]
            cosa = rtmp[:, :, 1, 0:ROT]
            for j in range(ROT):
                step(dve.memset(inv[:, j:j + 1], float(np.float32(THETA) ** np.float32(-j * 2.0 / (2 * ROT)))))
            dve.wait_ge(small_loaded, 16)
            step(dve.tensor_copy(posf[:, :], posi[:, :]))
            step(dve.tensor_tensor(ang, broadcast_last(posf[:, :], ROT),
                                   inv[:, :].unsqueeze(1).broadcast_to([P, NT, ROT]), ALU.mult))
            step(dve.tensor_scalar(kk, ang, 1.0 / two_pi, None, ALU.mult))
            step(dve.tensor_scalar(kk, kk, magic, None, ALU.add))
            step(dve.tensor_scalar(kk, kk, -magic, None, ALU.add))
            for part in (p1, p2, p3):
                step(dve.scalar_tensor_tensor(out=ang, in0=kk, scalar=-part, in1=ang, op0=ALU.mult, op1=ALU.add))
            step(dve.tensor_scalar(cosa, ang, np.pi / 2, None, ALU.add))
            step(dve.tensor_scalar(red, cosa, pi_in, -two_pi, ALU.is_gt, ALU.mult))
            step(dve.tensor_tensor(cosa, cosa, red, ALU.add))
            dve.tensor_scalar(cosa, cosa, pi_in, -pi_in, ALU.min, ALU.max).then_inc(sg.sem("angles_ready"), 1)
            dve.tensor_scalar(ang, ang, pi_in, -pi_in, ALU.min, ALU.max).then_inc(sg.sem("angles_ready"), 1)
            dve.wait_ge(sg.sem("mem_rstd"), 1)
            for t in range(NT):
                dve.tensor_scalar(vx[:, t, :], vx[:, t, :], msb[:, 4 + t:5 + t], None, ALU.mult)\
                    .then_inc(sg.sem("mem_hn_ready"), 1)
            dve.wait_ge(sg.sem("trig_done"), 4)

            def gain(row, c):
                return broadcast_last(cols[:, row + c:row + c + 2], S)

            def norm(l, k, row):
                base = (U_FFN1, U_FFN2)[k // 3]
                for t in range(NT):
                    dve.wait_ge(*sg.at("rstd_ready", l, NT * k + t + 1))
                    dve.tensor_scalar(hn[:, t, :], x[:, t, :], rstd[:, t:t + 1], None, ALU.mult)\
                        .then_inc(sg.inc("hn_ready"), 1)

                def low_xT(i):
                    dve.wait_ge(*sg.at("xT_high_ready", l, 4 * (k // 3) + i + 1))
                    part = slice(2 * i, 2 * i + 2)
                    dve.tensor_tensor(xT_parts[1][:, part, :], hT[:, part, :], xT_parts[0][:, part, :], ALU.subtract)\
                        .then_inc(sg.inc("xT_low_ready"), 1)

                for i in (1, 3):
                    dve.wait_ge(*sg.at("hT_transposed", l, 4 * k + i + 1))
                    dve.tensor_tensor(hT[:, 2 * i:2 * i + 2, :], b2(norm_bank(k) + i), gain(row, 2 * i), ALU.mult)\
                        .then_inc(sg.inc("hT_vector"), 1)
                    if k in (0, 3) and i == 1:
                        low_xT(0)
                if k in (0, 3):
                    for i in (1, 2, 3):
                        low_xT(i)
                    low(l, k // 3, base, 0)
                    low(l, k // 3, base, 1)

            def low(l, which, base, n, it=0):
                dve.wait_ge(high_ready, nth(l, which, it * 6 + n))
                dve.tensor_tensor(w_parts[n % SETS][1][:, :], ring[(base + n) % RING][:, :], w_parts[n % SETS][0][:, :],
                                  ALU.subtract).then_inc(low_ready, 1)

            def add_product(l, k, bk, scale, all_done):
                for t in range(NT):
                    for n in range(2):
                        dve.wait_ge(*(all_done if (t, n) == (NT - 1, 1) else
                                      sg.at("bank_summed", l, 3 * k + 2 * t + n + 1)))
                        xs = x[:, t, 512 * n:512 * n + 512]
                        dve.scalar_tensor_tensor(out=xs, in0=bank[bk + 2 * t + n][:, :], scalar=scale, in1=xs,
                                                 op0=ALU.mult, op1=ALU.add).then_inc(sg.inc("x_updated"), 1)

            def ffn(l, which):
                base = (U_FFN1, U_FFN2)[which]

                def step(par, s, it=0):
                    n = 3 * par + 2
                    split_next = s is not LAST
                    if split_next:
                        low(l, which, base, n, it)
                    else:
                        s = STEPS - 1
                    if not (isinstance(s, int) and s < 2):
                        dve.wait_ge(sg.sem("hid_low_ready"), step_of(l, which, s - 2))
                    for b in range(2):
                        dve.wait_ge(sg.sem("silu_ready"), (l * 2 + which) * 2 * STEPS + s * 2 + b + 1)
                        dve.tensor_tensor(hid[:, par, b, :], b2(4 + 2 * par + b)[:, 1, :], sil[:, par, b, :], ALU.mult)\
                            .then_inc(sg.sem("hid_ready"), 1)
                    if split_next:
                        low(l, which, base, n + 1, it)
                    dve.wait_ge(sg.sem("hid_high_ready"), step_of(l, which, s))
                    dve.tensor_tensor(hid_parts[1][:, par, :, :], hid[:, par, :, :], hid_parts[0][:, par, :, :], ALU.subtract)\
                        .then_inc(sg.sem("hid_low_ready"), 1)
                    if split_next:
                        low(l, which, base, n + 2, it)
                    else:
                        low(l, which, base, FFN_UNITS - 1)

                step(0, 0)
                step(1, 1)
                with dve.Fori(1, PAIRS) as it:
                    step(0, it * 2, it)
                    step(1, it * 2 + 1, it)
                step(0, LAST)
                add_product(l, 3 * which, 0, 0.5, products_done(l, which, FFN_UNITS - 1))

            def rope(v, heads, l, name):
                t1, t2 = rtmp[:, :, 0:heads, :], rtmp2[:, :, 0:heads, :]
                cb = rc[:, :, :].unsqueeze(2).broadcast_to([P, NT, heads, 2 * ROT])
                sb_ = rs[:, :, :].unsqueeze(2).broadcast_to([P, NT, heads, 2 * ROT])
                dve.tensor_tensor(t1, v[:, :, :, 0:2 * ROT], cb, ALU.mult)
                dve.tensor_tensor(t2[:, :, :, 0:ROT], v[:, :, :, ROT:2 * ROT], sb_[:, :, :, 0:ROT], ALU.mult)
                link(dve.tensor_tensor(t2[:, :, :, ROT:2 * ROT], v[:, :, :, 0:ROT], sb_[:, :, :, ROT:2 * ROT], ALU.mult), l)
                return dve.tensor_tensor(v[:, :, :, 0:2 * ROT], t1, t2, ALU.add)

            def mixer(l):
                def heads(ap):
                    return broadcast_last(ap.rearrange("p (t h) -> p t h", t=NT), HD)

                def by_head(ap):
                    return ap.rearrange("p t (h c) -> p t h c", h=H)

                dve.wait_ge(*sg.at("ab_copied", l))
                link(dve.tensor_tensor(ga1.rearrange("p (t h) -> p t h", t=NT), ab[:, :, 0:4],
                                       b_dt.unsqueeze(1).broadcast_to([P, NT, H]), ALU.add), l)
                dve.tensor_copy(beta.rearrange("p (t h) -> p t h", t=NT), ab[:, :, 4:8])
                link(dve.tensor_scalar(ga2, ga1, -1.0, None, ALU.mult), l)
                dve.tensor_tensor(ga2, ga1, ga2, ALU.min).then_inc(sg.inc("soft_in"), 1)
                for b in range(4):
                    dve.wait_ge(*sg.at("z_copied", l, b // 2 + 1))
                    link(dve.tensor_scalar(cv[:, b, :], z[:, b, 0:S], gcw[:, b, 0:1], None, ALU.mult), l)
                    for j in (1, 2, 3):
                        ins = dve.scalar_tensor_tensor(out=cv[:, b, :], in0=z[:, b, j:j + S], scalar=gcw[:, b, j:j + 1],
                                                       in1=cv[:, b, :], op0=ALU.mult, op1=ALU.add)
                        if j < 3:
                            link(ins, l)
                    ins.then_inc(sg.inc("conv_qk"), 1)
                dve.wait_ge(*sg.at("soft_ln", l))
                dve.tensor_scalar(beta, beta, 1.0, None, ALU.add)
                link(dve.scalar_tensor_tensor(out=ga1, in0=ga1, scalar=0.0, in1=ga3, op0=ALU.max, op1=ALU.add), l)
                dve.reciprocal(beta, beta)
                dve.scalar_tensor_tensor(out=gg_.rearrange("p (t h) -> p t h", t=NT),
                                         in0=ga1.rearrange("p (t h) -> p t h", t=NT), scalar=-1.0,
                                         in1=alog.unsqueeze(1).broadcast_to([P, NT, H]), op0=ALU.mult, op1=ALU.mult)\
                    .then_inc(sg.inc("g_ready"), 1)
                dve.wait_ge(*sg.at("rsa_ready", l))
                dve.wait_ge(*sg.at("iq0_copied", l))
                for t in range(NT):
                    dve.tensor_scalar(cn[:, t, :], b2(5)[:, t, 0:LAT], rsa[:, t:t + 1], None, ALU.mult)\
                        .then_inc(sg.inc("cn_ready"), 1)
                dve.wait_ge(*sg.at("iq1_scalar", l))
                for t in range(NT):
                    for i in (8, 9):
                        last = dve.scalar_tensor_tensor(out=R[:, t, i, :], in0=b2(6)[:, t, P:P + HD],
                                                        scalar=rsa[:, 2 + t:3 + t], in1=b_ikn, op0=ALU.mult, op1=ALU.mult)
                last.then_inc(sg.inc("iq1_copied"), 1)
                dve.wait_ge(*sg.at("g_ready", l))
                for t in range(NT):
                    last = dve.tensor_tensor(Sm[:, t, :, :], incl[:, :].unsqueeze(1).broadcast_to([P, H, P]),
                                             broadcast_last(gg_[:, 4 * t:4 * t + 4], P), ALU.mult)
                last.then_inc(sg.inc("gm_ready"), 1)
                dve.wait_ge(*sg.at("c_transposed", l))
                dve.tensor_scalar(cT[:, :], bank[4][:, 0:S], cols[:, R_KV:R_KV + 1], None, ALU.mult)\
                    .then_inc(sg.inc("cT_ready"), 1)
                dve.wait_ge(*sg.at("gc_ready", l))
                dve.wait_ge(*sg.at("egc_ready", l))
                dve.tensor_tensor(ekd, bank[3][:, 64:72], gc, ALU.subtract).then_inc(sg.inc("ekd_in"), 1)
                dve.wait_ge(*sg.at("iq1_copied", l))
                dve.wait_ge(*sg.at("iq0_copied", l))
                last = rope(R[:, :, 0:9, :], 9, l, "q")
                link(last, l)
                dve.tensor_copy(R[:, :, 9, 0:2 * ROT], R[:, :, 8, 0:2 * ROT]).then_inc(sg.inc("rope_q"), 1)
                for t in range(NT):
                    dve.wait_ge(*sg.at("qk_squared", l, t + 1))
                    last = dve.tensor_reduce(l2s[:, 8 * t:8 * t + 8],
                                             Bm[0][:, t, :, :].rearrange("p a b -> p (a b)").rearrange("p (h c) -> p h c", c=HD),
                                             AX, ALU.add)
                last.then_inc(sg.inc("l2_summed"), 1)
                dve.wait_ge(*sg.at("l2_ready", l))
                l2q = l2r.rearrange("p (t h) -> p t h", t=NT)[:, :, 0:4]
                link(dve.tensor_scalar(l2q, l2q, float(HD) ** -0.5, None, ALU.mult), l)
                for t in range(NT):
                    last = dve.tensor_tensor(qk[:, t, :, :], bank[t][:, :].rearrange("p (h c) -> p h c", c=HD),
                                             broadcast_last(l2r[:, 8 * t:8 * t + 8], HD), ALU.mult)
                    last.then_inc(sg.inc("qk_scaled"), 1)
                dve.wait_ge(*sg.at("qk_scaled", l))
                dve.wait_ge(*sg.at("sums_copied", l))
                dve.tensor_tensor(by_head(kb), qk[:, :, 4:8, :], heads(beta), ALU.mult).then_inc(sg.inc("kb_ready"), 1)
                dve.tensor_tensor(by_head(qg), qk[:, :, 0:4, :], heads(egc), ALU.mult).then_inc(sg.inc("qg_ready"), 1)
                for t in range(NT):
                    dve.wait_ge(*sg.at("gc_rows", l, t + 1))
                    dve.tensor_tensor(ET[:, t, :, :], b4(3 - t), away[:, :].unsqueeze(1).broadcast_to([P, H, P]), ALU.add)\
                        .then_inc(sg.inc("ET_in"), 1)
                dve.wait_ge(*sg.at("v_copied", l))
                dve.tensor_tensor(by_head(vb), by_head(gv[:, :, :]), heads(beta), ALU.mult)
                dve.wait_ge(*sg.at("kb_ready", l))
                dve.tensor_tensor(by_head(kbg), by_head(kb), heads(egc), ALU.mult)
                dve.tensor_tensor(by_head(kd), qk[:, :, 4:8, :], heads(ekd), ALU.mult).then_inc(sg.inc("ET_read"), 1)
                dve.wait_ge(*sg.at("kv_copied", l))
                rope(dk[:, :, :].rearrange("p t (h c) -> p t h c", h=H), H, l, "k").then_inc(sg.inc("rope_k"), 1)
                dve.wait_ge(*sg.at("rss_ready", l))
                for t in range(NT):
                    dve.scalar_tensor_tensor(out=sgn[:, t, :], in0=sgv[:, t, :], scalar=rss[:, t:t + 1], in1=b_sgn,
                                             op0=ALU.mult, op1=ALU.mult).then_inc(sg.inc("sgn_ready"), 1)
                dve.wait_ge(*sg.at("ET_ready", l))
                for t in range(NT):
                    for odd in range(2):
                        dve.wait_ge(*sg.at("kq_done", l, 2 * t + odd + 1))
                        for i, dst in enumerate((AE, AT)):
                            pair = (slice(None), t, slice(odd, H, 2), slice(None))
                            dve.tensor_tensor(dst[pair], b4(2 * t + odd)[:, 2 * i:2 * i + 2, :], ET[pair], ALU.mult)\
                                .then_inc(sg.inc("AE_ready"), 1)
                dve.wait_ge(*sg.at("qk_squared", l))
                dve.memset(state[:, :, :], 0.0).then_inc(sg.inc("l2_read"), 1)

                def weigh(t, h, src):
                    link(dve.scalar_tensor_tensor(out=work[t], in0=src, scalar=iw[:, t, h:h + 1],
                                                  in1=cfills[t] if h == 0 else work[t], op0=ALU.mult, op1=ALU.add), l)

                for t in range(NT):
                    n = P * (t + 1)
                    for i, h in enumerate((0, 2, 1, 3)):
                        if i % 2 == 0:
                            dve.wait_ge(*sg.at("relu_done", l, 2 * t + i // 2 + 1))
                        weigh(t, h, rel[:, n * i:n * i + n])
                    if t == 0:
                        dve.nop().then_inc(sg.inc("score_added"), 1)

                def take(t):
                    apart(dve)
                    link(dve.max(m8[:, t, :], work[t]), l)
                    apart(dve)
                    link(dve.match_replace(out=work[t], in_to_replace=m8[:, t, :], in_values=work[t],
                                           imm_value=TAKEN), l)

                takes = [0] * (TOPK // 8) + [1] * (TOPK // 8)
                for t in range(NT):
                    dve.wait_ge(*sg.at("B_ready", l, t + 1))
                    dve.tensor_tensor(Sm[:, t, :, :], ident[:, :].unsqueeze(1).broadcast_to([P, H, P]), Bm[0][:, t, :, :],
                                      ALU.subtract).then_inc(sg.inc("TS_ready"), 1)
                    dve.wait_ge(*sg.at("U_done", l, t + 1))
                    dve.tensor_tensor(Tm[:, t, :, :], ident[:, :].unsqueeze(1).broadcast_to([P, H, P]), b4(2 * t),
                                      ALU.subtract).then_inc(sg.inc("TS_ready"), 1)
                n = 0
                for i in range(1, len(LEVELS)):
                    for _ in range(3):
                        take(takes[n])
                        n += 1
                    for t in range(NT):
                        last_level = i == len(LEVELS) - 1
                        k = 2 * NT * (i - 1) + (t if last_level else 2 * t)
                        for j, (m, bk) in enumerate([(Tm, 2 * t + 1), (Sm, 2 * t)][last_level:]):
                            dve.wait_ge(*sg.at("TS_done", l, k + j + 1))
                            dve.tensor_tensor(m[:, t, :, :], m[:, t, :, :], b4(bk), ALU.subtract)\
                                .then_inc(sg.inc("TS_ready"), 1)
                take(takes[n])

                def selected(t):
                    link(dve.tensor_scalar(nb[t], work[t], TAKEN_BELOW, -AWAY, ALU.is_lt, ALU.mult), l)
                    link(dve.scalar_tensor_tensor(out=nb[t], in0=nb[t], scalar=AWAY, in1=cfills[t],
                                                  op0=ALU.add, op1=ALU.add), l)

                selected(0)
                selected(1)
                dve.wait_ge(*sg.at("egc_ready", l))
                eg = egl.rearrange("p c (b two) -> p c b two", two=2)
                dve.tensor_copy(egl2[0:HD], eg[0:HD, :, :, 0])
                dve.tensor_copy(egl2[HD:P], eg[HD:P, :, :, 1]).then_inc(sg.inc("state_ready"), 1)

                def chunk_new(c):
                    t, r = c // 2, CH * (c % 2)
                    dve.wait_ge(*sg.at("state_ready", l, c + 1))
                    dve.tensor_tensor(state_d[:, :, :], state[:, :, :], broadcast_last(egl2[:, c, :], HD), ALU.mult)
                    dve.wait_ge(*sg.at("ws_done", l, c + 1))
                    for odd in range(2):
                        pair = (slice(r, r + CH), t, slice(odd, H, 2), slice(None))
                        dve.tensor_tensor(by_head(vnew[:, :, :])[pair], by_head(us)[pair],
                                          bank[odd][r:r + CH, 0:P].rearrange("p (b c) -> p b c", b=2), ALU.subtract)\
                            .then_inc(sg.inc("vnew_ready"), 1)

                def chunk_state(c):
                    dve.wait_ge(*sg.at("kv_done", l, c + 1))
                    dve.tensor_tensor(state[:, :, :], state_d[:, :, :],
                                      bank[2][:, 0:2 * HD].rearrange("p (b c) -> p b c", b=2), ALU.add)\
                        .then_inc(sg.inc("state_ready"), 1)

                def logits(t):
                    dve.wait_ge(*sg.at("logits_done", l, t + 1))
                    n = P * (t + 1)
                    for odd in range(2):
                        dve.scalar_tensor_tensor(
                            out=Pds[t][:, 2 * n * odd:2 * n * odd + 2 * n].rearrange("p (b s) -> p b s", b=2),
                            in0=bank[4 + odd][:, 0:2 * n].rearrange("p (b s) -> p b s", b=2), scalar=float(HD) ** -0.5,
                            in1=nb[t].unsqueeze(1).broadcast_to([P, 2, n]), op0=ALU.mult, op1=ALU.add)\
                            .then_inc(sg.inc("logits_read"), 1)

                def row_max(t):
                    dst = dmx[:, 4 * t:4 * t + 4]
                    n = 4 * P * (t + 1)
                    dve.tensor_reduce(dst, Pds[t][:, 0:n].rearrange("p (h s) -> p h s", h=4), AX, ALU.max, negate=True)\
                        .then_inc(sg.inc("dmx_ready"), 1)

                def probs(t):
                    dve.wait_ge(*sg.at("dexp_done", l, 4 * t + 4))
                    d = dsum[:, 4 * t:4 * t + 4]
                    link(dve.reciprocal(d, d), l)
                    n = P * (t + 1)
                    v = Pds[t][:, 0:4 * n].rearrange("p (h s) -> p h s", h=4)
                    dve.tensor_tensor(v, v, broadcast_last(d, n), ALU.mult).then_inc(sg.inc("probs_ready"), 1)

                chunk_new(0)
                logits(0)
                dve.wait_ge(*sg.at("logits_read", l, 2))
                row_max(0)
                chunk_state(0)
                chunk_new(1)
                probs(0)
                chunk_state(1)
                chunk_new(2)
                logits(1)
                chunk_state(2)
                chunk_new(3)
                dve.wait_ge(*sg.at("logits_read", l))
                row_max(1)
                dve.wait_ge(*sg.at("sgw_transposed", l))
                dve.tensor_tensor(sgwT, b4(7), up[:, :].unsqueeze(1).broadcast_to([P, H, P]), ALU.mult)\
                    .then_inc(sg.inc("sgwT_ready"), 1)
                chunk_state(3)
                dve.wait_ge(*sg.at("o_done", l))
                dve.wait_ge(*sg.at("U_copied", l))
                dve.wait_ge(*sg.at("qs_copied", l))
                link(dve.tensor_tensor(by_head(us), by_head(b2(3)), os_, ALU.add), l)
                link(dve.tensor_tensor(kbg, us, us, ALU.mult), l)
                link(dve.tensor_reduce(gos, by_head(kbg), AX, ALU.add), l)
                dve.tensor_scalar(gos, gos, 1.0 / HD, None, ALU.mult).then_inc(sg.inc("gos_ready"), 1)
                probs(1)
                dve.wait_ge(*sg.at("gate_read", l))
                link(dve.tensor_tensor(by_head(gate[:, :, :]), by_head(gate[:, :, :]),
                                       b_gon.unsqueeze(1).unsqueeze(1).broadcast_to([P, NT, H, HD]), ALU.mult), l)
                dve.wait_ge(*sg.at("sg_mixed", l))
                dve.wait_ge(*sg.at("sgu_gelu", l))
                link(dve.tensor_tensor(by_head(sgj), by_head(b2(6)),
                                       broadcast_last(cols[:, R_SGB:R_SGB + H], HD).unsqueeze(1).broadcast_to([P, NT, H, HD]), ALU.add), l)
                dve.tensor_tensor(sgj, sgj, sgu, ALU.mult).then_inc(sg.inc("sg_out"), 1)
                dve.wait_ge(*sg.at("gor_ready", l))
                link(dve.tensor_tensor(by_head(us), by_head(us), heads(gor), ALU.mult), l)
                dve.tensor_tensor(vnew[:, :, :], us, gate[:, :, :], ALU.mult).then_inc(sg.inc("gdn_out"), 1)
                add_product(l, 1, 4, 1.0, unit_used(U_OUT + 3, l))

            def cross(l):
                def maxima(h):
                    dve.wait_ge(*sg.at("xlogits", l, h + 1))
                    m = xmx[:, 2 * h:2 * h + 2]
                    link(dve.tensor_reduce(m, b2((1, 5, 1, 0)[h]), AX, ALU.max), l)
                    dve.tensor_scalar(xnb[:, 2 * h:2 * h + 2], m, -1.0 / 16, None, ALU.mult)\
                        .then_inc(sg.inc("xmax_ready"), 1)

                def probs(h):
                    dve.wait_ge(*sg.at("xexp_done", l, NT * h + NT))
                    s = xsum[:, 2 * h:2 * h + 2]
                    link(dve.reciprocal(s, s), l)
                    v = xP[:, h % 2, :, :]
                    dve.tensor_tensor(v, v, broadcast_last(s, S), ALU.mult).then_inc(sg.inc("xprobs"), 1)

                for h in range(H):
                    maxima(h)
                    probs(h)
                add_product(l, 2, 4, 1.0, unit_used(U_XO + 3, l))

            with dve.Fori(0, DEPTH) as l:
                dve.wait_ge(*sg.at("rows_transposed", l))
                dve.tensor_copy(cols[:, :], bank[7][:, 0:N_ROWS]).then_inc(sg.inc("cols_ready"), 1)
                dve.wait_ge(*sg.at("cols_ready", l))
                norm(l, 0, R_FFN1)
                ffn(l, 0)
                norm(l, 1, R_MIX)
                mixer(l)
                norm(l, 2, R_XA)
                dve.nop().then_inc(sg.inc("params_used"), 1)
                cross(l)
                norm(l, 3, R_FFN2)
                ffn(l, 1)
            dve.wait_ge(small_loaded, 32)
            for t in range(NT):
                dve.wait_ge(*sg.at("rstd_ready", DEPTH, t + 1))
                dve.scalar_tensor_tensor(out=hn[:, t, :], in0=x[:, t, :], scalar=rstd[:, t:t + 1], in1=vx[:, 0, :],
                                         op0=ALU.mult, op1=ALU.mult).then_inc(sg.sem("out_ready"), 1)

        return dict(sg.counts)


def kernel(**inputs):
    import concourse.bacc as bacc
    from concourse.bass_utils import run_bass_kernel_spmd

    def program(arrays, per):
        nc = bacc.Bacc("TRN2", target_bir_lowering=False, num_devices=1)
        a = {n: nc.dram_tensor(f"in_{n}", v.shape, mybir.dt.from_np(v.dtype), kind="ExternalInput").ap()
             for n, v in arrays.items()}
        out = nc.dram_tensor("out", (1, S, D), F32, kind="ExternalOutput").ap()
        mem_scratch = nc.dram_tensor("mem_scratch", (P, KC, S), F32, kind="Internal").ap()
        return nc, build(nc, a, out, mem_scratch, per)

    arrays = {n: np.ascontiguousarray(inputs[n]) for n in NAMES}
    _, per = program(arrays, {})
    nc, _ = program(arrays, per)
    r = run_bass_kernel_spmd(nc, [{f"in_{n}": v for n, v in arrays.items()}], core_ids=[0])
    return r.results[0]["out"]
```

```python
from contextlib import ExitStack

import concourse.bass as bass
import numpy as np
from concourse import mybir

F32 = mybir.dt.float32
F32R = mybir.dt.float32r
I32 = mybir.dt.int32
ALU = mybir.AluOpType
ACT = mybir.ActivationFunctionType
AX = mybir.AxisListType.X

P = 128
D = 1024
KC = D // P
S = 256
NT = S // P
DEPTH = 2
D_FF = 2816
STEPS = D_FF // 256
PAIRS = (STEPS - 1) // 2
GW = 256
HD = 64
H = 4
LAT = 128
ROT = 8
THETA = 500000.0
EPS = 1e-6
TOPK = 64
CH = 64
NCH = S // CH
LEVELS = (1, 2, 4, 8, 16, 32)
FILL = -3.0e38
TAKEN = -3.4e38
TAKEN_BELOW = -3.2e38
AWAY = -1.0e30

C_SGU, C_SGV, C_SCB, C_SCC, C_SCH, C_Q, C_CKV, C_IQ1, C_GQKV, C_GA, C_GG = (
    0, 256, 512, 768, 1024, 1280, 1536, 1792, 1988, 2756, 2764)
W_IQ1 = C_GQKV - C_IQ1

RING = 6
FFN_UNITS = 3 * STEPS
SETS = 3
MIX_SPLITS = 9
VALUE_UNIT_BANK = (7, 6, 7, 7)
VALUES_BANK = (3, 3, 3, 1)
HIGH_WEIGHT, LOW_WEIGHT = [(0, 0), (0, 1)], [(1, 0)]
LAST = None
MIX_COLS = [(C_GQKV, 256), (C_GQKV + 256, 256), (C_GQKV + 512, 256), (C_Q, 256), (C_CKV, 256),
            (C_IQ1, W_IQ1), (C_SGV, 256), (C_SGU, 256), (C_SCC, 256), (C_SCH, 256), (C_SCB, 256),
            (C_GG, 256)]
U_FFN1 = 0
U_MIX = U_FFN1 + FFN_UNITS + 1
(U_GQ, U_GK, U_GV, U_Q, U_CKV, U_IQ1, U_SGV, U_SGU, U_SCC, U_SCH, U_SCB, U_GG) = range(
    U_MIX, U_MIX + len(MIX_COLS))
U_XK = U_GG + 1 + 1
U_XV = U_XK + 4 + 1
U_OUT = U_XV + 4 + 1
U_XQ = U_OUT + 4
U_XO = U_XQ + 4
U_FFN2 = U_XO + 4
N_UNITS = U_FFN2 + FFN_UNITS
assert N_UNITS % RING == 0
WHOLE = [*range(U_MIX + MIX_SPLITS, U_GG + 1), *range(U_XK, U_XK + 4), *range(U_XV, U_XV + 4), *range(U_OUT, U_OUT + 3)]
UNITS = sorted([*range(U_MIX - 1), *range(U_MIX, U_MIX + MIX_SPLITS), *WHOLE, *range(U_OUT + 3, N_UNITS)])
Q_MIX = FFN_UNITS
Q_OUT3 = Q_MIX + MIX_SPLITS
Q_XQ = Q_OUT3 + 1
Q_XO = Q_XQ + 4
Q_FFN = (0, Q_XO + 4)
N_SPLITS = Q_FFN[1] + FFN_UNITS

N_ROWS = 5 * KC + H + 1
R_FFN1, R_MIX, R_XA, R_MEM, R_FFN2, R_SGB, R_KV = 0, KC, 2 * KC, 3 * KC, 4 * KC, 5 * KC, 5 * KC + H

NAMES = ['x', 'mem', 'positions', 'ffn1_norm', 'ffn1_wg', 'ffn1_wu', 'ffn1_wd', 'mix_norm', 'w_mix_in',
         'w_mix_out', 'sg_norm', 'sg_w', 'sg_b', 'sc_conv', 'kv_norm', 'w_uk', 'w_uv', 'idx_k_norm',
         'gdn_conv', 'gdn_a_log', 'gdn_dt_bias', 'gdn_out_norm', 'xa_norm', 'mem_norm', 'xa_wq', 'xa_wk',
         'xa_wv', 'xa_wo', 'ffn2_norm', 'ffn2_wg', 'ffn2_wu', 'ffn2_wd', 'final_norm']


class Signals:

    def __init__(self, nc, ctx, per):
        self.nc, self.ctx, self.per = nc, ctx, per
        self.sems, self.counts = {}, {}
        self.start = {"x_updated": 4, "params_used": 1}

    def sem(self, name):
        if name not in self.sems:
            self.sems[name] = self.ctx.enter_context(self.nc.semaphore(name))
        return self.sems[name]

    def inc(self, name, times=1):
        self.counts[name] = self.counts.get(name, 0) + times
        return self.sem(name)

    def begin(self, eng, name):
        eng.sem_inc(self.sem(name), self.start[name])

    def at(self, name, layer, k=None):
        per = self.per.get(name, 0)
        return self.sem(name), layer * per + (per if k is None else k) + self.start.get(name, 0)


def broadcast_last(ap, n):
    return ap.unsqueeze(len(ap.shape)).broadcast_to([*ap.shape, n])


def build(nc, a, out, mem_scratch, per):
    with ExitStack() as ctx:
        sg = Signals(nc, ctx, per)

        def sb(name, shape, dt=F32):
            return ctx.enter_context(nc.sbuf_tensor(name, shape, dt))

        x = sb("x", [P, NT, D])
        hT = sb("hT", [P, KC, S])
        hn = sb("hn", [P, NT, D])
        memn = hn[:, :, :].rearrange("p t d -> p (t d)").rearrange("p (c s) -> p c s", c=KC)
        ring = [sb(f"ring{i}", [P, 2048]) for i in range(RING)]
        ffn_buf = sb("ffn_buf", [P, 2048])
        sil = ffn_buf[:, 0:1024].rearrange("p (b k s) -> p b k s", b=2, k=2)
        hid = ffn_buf[:, 1024:2048].rearrange("p (b k s) -> p b k s", b=2, k=2)
        sgu = ffn_buf[:, 0:512].rearrange("p (t c) -> p t c", t=NT)
        sgv = ffn_buf[:, 512:1024].rearrange("p (t c) -> p t c", t=NT)
        sgn = ffn_buf[:, 1024:1536].rearrange("p (t c) -> p t c", t=NT)
        sgj = ffn_buf[:, 1536:2048].rearrange("p (t c) -> p t c", t=NT)

        rows = sb("rows", [N_ROWS, P])
        cols = sb("cols", [P, N_ROWS])
        wab = sb("wab", [P, KC, 8])
        w_kv = sb("w_kv", [P, 2, GW])
        sgw = sb("sgw", [P, H, P])
        scw = sb("scw", [P, 2, 3])
        gcw = sb("gcw", [P, 6, 4])
        bc = sb("bc", [P, GW + HD + HD + 2 * H])
        b_sgn, b_ikn, b_gon, b_alog, b_dt = (bc[:, 0:256], bc[:, 256:320], bc[:, 320:384], bc[:, 384:388],
                                             bc[:, 388:392])
        ident = sb("ident", [P, P])
        onesm = sb("onesm", [P, P])
        incl = sb("incl", [P, P])
        away = sb("away", [P, P])
        up = sb("up", [P, P])
        same = sb("same", [P, P])
        half = sb("half", [P, NT, P])
        lev = sb("lev", [P, len(LEVELS), P])
        cfill = sb("cfill", [P, 3 * P])
        cfills = [cfill[:, 0:P], cfill[:, P:3 * P]]
        rc = sb("rc", [P, NT, 2 * ROT])
        rs = sb("rs", [P, NT, 2 * ROT])
        rtmp = sb("rtmp", [P, NT, 9, 2 * ROT])
        rtmp2 = sb("rtmp2", [P, NT, 9, 2 * ROT])
        inv = sb("inv", [P, ROT])
        posi = sb("posi", [P, NT], I32)
        posf = sb("posf", [P, NT])
        mhalf = sb("mhalf", [P, 16])
        sm = sb("sm", [P, 320])
        ms, rstd = sm[:, 268:272], sm[:, 0:2]
        msa, rsa = sm[:, 4:8], sm[:, 8:12]
        mss, rss = sm[:, 12:14], sm[:, 14:16]
        l2s, l2r = sm[:, 16:32], sm[:, 32:48]
        ab = sm[:, 48:64].rearrange("p (t c) -> p t c", t=NT)
        ga1, ga2, ga3 = sm[:, 64:72], sm[:, 72:80], sm[:, 80:88]
        gg_, beta = sm[:, 88:96], sm[:, 96:104]
        gc, glast = sm[:, 104:112], sm[:, 112:120]
        ngc, egc, ekd = sm[:, 120:128], sm[:, 128:136], sm[:, 136:144]
        alog = sm[:, 144:148]
        mean = sm[:, 2:4]
        egl = sm[:, 148:164].rearrange("p (c h) -> p c h", c=NCH)
        egl2 = sm[:, 164:172].rearrange("p (c b) -> p c b", c=NCH)
        iw = sm[:, 172:180].rearrange("p (t h) -> p t h", t=NT)
        m8 = sm[:, 180:196].rearrange("p (t k) -> p t k", t=NT)
        dmx, dsum = sm[:, 196:204], sm[:, 204:212]
        xmx, xnb, xsum = sm[:, 212:220], sm[:, 220:228], sm[:, 228:236]
        gos, gor = sm[:, 236:244], sm[:, 244:252]
        msb = sm[:, 252:268]


        score = sb("score", [P, 3 * P])
        scz = sb("scz", [P, 2, S + 2])
        mixer_only = ExitStack()

        sizes = []

        def sb(name, shape, dt=F32):
            sizes.append((name, int(np.prod(shape[1:]))))
            return mixer_only.enter_context(nc.sbuf_tensor(name, shape, dt))

        vx = sb("vx", [P, NT, D])
        yT = sb("yT", [P, KC, S])
        g1 = sb("g1", [P, 2048])
        g2 = sb("g2", [P, 2048])
        kxT = sb("kxT", [P, KC, S])
        arena_a = sb("arena_a", [P, 6 * (S + 3)])
        z = arena_a[:, :].rearrange("p (b s) -> p b s", b=6)
        ET = arena_a[:, 0:1024].rearrange("p (t h c) -> p t h c", t=NT, h=H)
        arena_b = sb("arena_b", [P, 1536])
        cv = arena_b[:, :].rearrange("p (b s) -> p b s", b=6)
        Tm = arena_b[:, 0:1024].rearrange("p (t h c) -> p t h c", t=NT, h=H)
        us = arena_b[:, 1024:1536].rearrange("p (t c) -> p t c", t=NT)
        qk_buf = sb("qk_buf", [P, 1024])
        qk = qk_buf[:, :].rearrange("p (t h c) -> p t h c", t=NT, h=2 * H)
        Um = qk_buf[:, :].rearrange("p (t h c) -> p t h c", t=NT, h=H)
        Sm_buf = sb("Sm_buf", [P, 1024])
        Sm = Sm_buf[:, :].rearrange("p (t h c) -> p t h c", t=NT, h=H)
        Bm = [sb(f"Bm{i}", [P, NT, H, P]) for i in range(2)]
        kb, vb, kbg, kd = (g1[:, 512 * i:512 * i + 512].rearrange("p (t c) -> p t c", t=NT) for i in range(4))
        kT, kbT, qT, qgT = (g2[:, 512 * i:512 * i + 512].rearrange("p (b s) -> p b s", b=2) for i in range(4))
        os_ = kb.rearrange("p t (h c) -> p t h c", h=H)
        PT = g2[:, 0:1536]
        g3 = sb("g3", [P, 2048])
        AE = g3[:, 0:1024].rearrange("p (t h c) -> p t h c", t=NT, h=H)
        AT = g3[:, 1024:2048].rearrange("p (t h c) -> p t h c", t=NT, h=H)
        wT = sb("wT", [P, 2, S])
        qg = wT[:, :, :].rearrange("p b s -> p (b s)").rearrange("p (t c) -> p t c", t=NT)
        vnew = sb("vnew", [P, NT, GW])
        gv = vnew
        state = sb("state", [P, 2, HD])
        state_d = sb("state_d", [P, 2, HD])
        gate = sb("gate", [P, NT, GW])
        R_buf = sb("R_buf", [P, NT * 10 * HD])
        R = R_buf[:, :].rearrange("p (t h c) -> p t h c", t=NT, h=10)
        rel = R_buf[:, 0:1024]
        Pds = [arena_b[:, 0:512], R_buf[:, 0:1024]]
        dk = sb("dk", [P, NT, GW])
        dv = sb("dv", [P, NT, GW])
        dqT = sb("dqT", [P, 2, S])
        diqT = arena_a[:, 1024:1536].rearrange("p (b s) -> p b s", b=2)
        dikT = sb("dikT", [P, S])
        dkT = sb("dkT", [P, 2, S])
        cT = sb("cT", [P, S])
        work = [score[:, 0:P], score[:, P:3 * P]]
        nbias = sb("nbias", [P, 3 * P])
        cn = nbias[:, 0:NT * LAT].rearrange("p (t c) -> p t c", t=NT)
        nb = [nbias[:, 0:P], nbias[:, P:3 * P]]
        sch = sb("sch", [P, 2, S])
        sco = sb("sco", [P, 2, S])
        xP = g1[:, 0:1024].rearrange("p (b t s) -> p b t s", b=2, t=NT)
        xPT = g1[:, 1024:2048].rearrange("p (b k s) -> p b k s", b=2, k=2)
        xqT = g2[:, :].rearrange("p (c s) -> p c s", c=KC)
        sgwT = arena_a[:, 1024:1536].rearrange("p (h s) -> p h s", h=H)
        zeros, stairs = yT[:, 6, 0:P], yT[:, 7, 0:P]
        mixer_only.close()

        def words(first, end):
            names = [n for n, _ in sizes]
            return sum(w for _, w in sizes[names.index(first):names.index(end)])

        over = ExitStack()

        def part(name, shape, dt=F32R, stack=over):
            return stack.enter_context(nc.sbuf_tensor(name, shape, dt))

        mix_w1_high = part("mix_w1_high", [P, 2048])
        xm_high = part("xm_high", [P, KC, S])
        part("over_g1", [P, words("g1", "g2")], F32)
        mix_w0_high, mix_w0_low = part("mix_w0_high", [P, 2048]), part("mix_w0_low", [P, 2048])
        part("over_arena_a_on", [P, words("arena_a", "g3")], F32)
        xm_low = part("xm_low", [P, KC, S])
        part("over_wT_on", [P, words("wT", "dk")], F32)
        mix_w1_low = part("mix_w1_low", [P, 2048])
        assert words("dk", "cT") >= 2048
        over.close()
        mix_parts = [(mix_w0_high, mix_w0_low), (mix_w1_high, mix_w1_low)]
        part("over_vx", [P, words("vx", "yT")], F32, ctx)
        split = [[part(f"{n}_{hl}", shape, stack=ctx) for hl in ("high", "low")]
                 for n, shape in [("out", [P, 2 * 2 * S]), ("hidden", [P, 2 * 2 * S])]]
        part("over_g2_and_kxT", [P, words("g2", "arena_a")], F32, ctx)
        split += [[part(f"{n}_{hl}", shape, stack=ctx) for hl in ("high", "low")]
                  for n, shape in [("xT", [P, KC, S])] + [(f"w{i}", [P, 2048]) for i in range(SETS)]]
        oT_parts = [v[:, :].rearrange("p (b k s) -> p b k s", b=2, k=2) for v in split[0]]
        xT_parts, xm_parts = split[2], [xm_high, xm_low]
        hid_parts = [v[:, :].rearrange("p (b k s) -> p b k s", b=2, k=2) for v in split[1]]
        w_parts = split[3:]

        bank = [ctx.enter_context(nc.psum_tensor(f"bank{i}", [P, 512], F32)) for i in range(8)]

        def b2(i):
            return bank[i][:, :].rearrange("p (k s) -> p k s", k=2)

        def norm_bank(k):
            return 4 if k < 2 else 0

        def piece(ap, j):
            return ap[:, 4 * (j % 2):4 * (j % 2) + 4, P * (j // 2):P * (j // 2) + P]

        def b4(i):
            return bank[i][:, :].rearrange("p (k s) -> p k s", k=4)

        wide = {n: a[n].rearrange("l (c p) n -> p l c n", p=P)
                for n in ("ffn1_wg", "ffn1_wu", "ffn1_wd", "ffn2_wg", "ffn2_wu", "ffn2_wd", "w_mix_in",
                          "w_mix_out", "xa_wq", "xa_wk", "xa_wv", "xa_wo")}
        x_v = a["x"].rearrange("b (t p) d -> p (b t) d", p=P)
        mem_v = a["mem"].rearrange("b (t p) d -> p (b t) d", p=P)
        out_v = out.rearrange("b (t p) d -> p (b t) d", p=P)

        landed = [sg.sem(f"unit_landed{i}") for i in range(RING)]
        mixer_unit_used = sg.sem("mixer_unit_used")

        def unit_landed(pos, layer, it=0):
            slot = [u for u in UNITS if u % RING == pos % RING]
            return landed[pos % RING], (layer * len(slot) + slot.index(pos) + it) * 16 + 16

        def unit_used(pos, layer):
            return mixer_unit_used, layer * len(WHOLE) + WHOLE.index(pos) + 1

        def as_cols(pos, w=256):
            return ring[pos % RING][:, 0:KC * w].rearrange("p (c n) -> p c n", c=KC)

        def as_rows(pos):
            return ring[pos % RING][:, :].rearrange("p (c n) -> p c n", c=2)

        mem_in, mixer_par_loaded = sg.sem("mem_in"), sg.sem("mixer_par_loaded")
        x_loaded, mem_stored, out_done = sg.sem("x_loaded"), sg.sem("mem_stored"), sg.sem("out_done")
        small_loaded = sg.sem("small_loaded")
        mem_loaded, par_loaded = sg.sem("mem_loaded"), sg.sem("par_loaded")
        N_ROW_LOADS, N_MIXER_LOADS = 7, 11

        high_ready, low_ready, split_used = sg.sem("high_ready"), sg.sem("low_ready"), sg.sem("split_used")

        def nth(l, q):
            return l * N_SPLITS + q + 1

        def set_free(l, q):
            if isinstance(q, int) and Q_MIX < q < Q_OUT3:
                return split_used, nth(l, q) + SETS - 2
            if isinstance(q, int) and q == Q_MIX:
                return split_used, nth(l, q) - 2
            return split_used, nth(l, q)

        def products_done(l, q):
            return split_used, nth(l, q) + SETS

        def low_done(l, q):
            return low_ready, nth(l, q) + RING

        def number(pos):
            if pos < U_MIX - 1:
                return pos
            return pos - U_MIX + Q_MIX if pos < U_MIX + MIX_SPLITS else pos - U_XQ + Q_XQ

        def position(q):
            return q if q < Q_MIX else q - Q_MIX + U_MIX if q < Q_OUT3 else q - Q_XQ + U_XQ

        def parts_of(q):
            if Q_MIX <= q < Q_OUT3:
                return mix_parts[(q - Q_MIX) % 2], KC * MIX_COLS[q - Q_MIX][1]
            return w_parts[q % SETS], 2048

        assert N_SPLITS % SETS == 0

        def slot_free(pos, l, it=0):
            before = pos - RING
            if not isinstance(it, int):
                return low_done(l, it * 6 + (number(pos) - RING))
            if before < 0:
                return low_done(l - 1, number(before + N_UNITS))
            if before not in UNITS:
                before -= RING
            if before in WHOLE:
                return unit_used(before, l)
            return low_done(l, number(before))

        def split_set(q, as_=None):
            parts, n = parts_of(q)
            return [v[:, 0:n].rearrange("p (c n) -> p c n", c=as_) for v in parts]

        def step_of(l, which, s):
            return (l * 2 + which) * STEPS + s + 1

        def blocks_of(l, which, s):
            return (l * 2 + which) * 2 * STEPS + 2 * s + 2 + 4

        def apart(eng):
            eng.sem_inc(sg.sem("waited"), 1)

        block = ctx.enter_context(nc.Block())

        @block.sync
        def _(sp):
            sg.begin(sp, "params_used")
            sp.sem_inc(low_ready, RING)
            sp.dma_start(vx[:, :, :], mem_v).then_inc(mem_in, 16)
            sp.dma_start(posi[:, :], a["positions"].rearrange("b (t p) -> p (b t)", p=P),
                         allow_slow_non_contiguous=True).then_inc(small_loaded, 16)
            sp.dma_start(x[:, :, :], x_v).then_inc(x_loaded, 16)

            def params(l):
                def load(dst, src):
                    sp.dma_start(dst, src).then_inc(par_loaded, 16)
                sp.wait_ge(*sg.at("params_used", l, 0))
                apart(sp)
                for r, n in ((R_FFN1, "ffn1_norm"), (R_MIX, "mix_norm"), (R_XA, "xa_norm"), (R_MEM, "mem_norm"),
                             (R_FFN2, "ffn2_norm")):
                    load(rows[r:r + KC, :], a[n].rearrange("l (c p) -> c l p", p=P)[:, l, :])
                load(rows[R_SGB:R_SGB + H, :], a["sg_b"].rearrange("l h t -> h l t")[:, l, :])
                load(rows[R_KV:R_KV + 1, :], a["kv_norm"][bass.ds(l, 1), :])

            def mixer_params(l):
                def load(dst, src):
                    sp.dma_start(dst, src).then_inc(mixer_par_loaded, 16)
                load(wab[:, :, :], wide["w_mix_in"][:, l, :, C_GA:C_GA + 8])
                load(w_kv[:, 0, :], a["w_uk"].rearrange("l p n -> p l n")[:, l, :])
                load(w_kv[:, 1, :], a["w_uv"].rearrange("l p n -> p l n")[:, l, :])
                load(sgw[:, :, :], a["sg_w"].rearrange("l h t s -> t l h s")[:, l, :, :])
                load(scw[:, :, :], a["sc_conv"].rearrange("l (b p) j -> p l b j", p=P)[:, l, :, :])
                load(gcw[:, :, :], a["gdn_conv"].rearrange("l (b p) j -> p l b j", p=P)[:, l, :, :])
                for dst, n, w in ((b_sgn, "sg_norm", GW), (b_ikn, "idx_k_norm", HD), (b_gon, "gdn_out_norm", HD),
                                  (b_alog, "gdn_a_log", H), (b_dt, "gdn_dt_bias", H)):
                    load(dst, a[n][bass.ds(l, 1), :].broadcast_to([P, w]))

            def unit(dst, src, pos, l, it=0):
                sp.wait_ge(*slot_free(pos, l, it))
                apart(sp)
                sp.dma_start(dst, src).then_inc(landed[pos % RING], 16)

            def ffn_units(l, n, base):
                def gate_up(pos, c0, it=0):
                    for i, w in enumerate(("wg", "wu")):
                        unit(as_cols(pos + i), wide[f"{n}_{w}"][:, l, :, c0], pos + i, l, it)

                def down(pos, r0, it=0):
                    unit(as_rows(pos), wide[f"{n}_wd"][:, l, r0, :], pos, l, it)

                def pair(it):
                    gate_up(base + 2, bass.ds(it * 512 + 256, 256), it)
                    down(base + 4, bass.ds(it * 4, 2), it)
                    gate_up(base + 5, bass.ds(it * 512 + 512, 256), it)
                    down(base + 7, bass.ds(it * 4 + 2, 2), it)

                gate_up(base, slice(0, 256))
                gate_up(base + 2, slice(256, 512))
                down(base + 4, slice(0, 2))
                gate_up(base + 5, slice(512, 768))
                down(base + 7, slice(2, 4))
                if n == "ffn1":
                    mixer_params(l)
                with sp.Fori(1, PAIRS) as it:
                    pair(it)
                down(base + 2 + 6 * PAIRS, slice(2 * STEPS - 2, 2 * STEPS))

            with sp.Fori(0, DEPTH) as l:
                params(l)
                ffn_units(l, "ffn1", U_FFN1)
                for i, (c, w) in enumerate(MIX_COLS):
                    unit(as_cols(U_MIX + i, w), wide["w_mix_in"][:, l, :, c:c + w], U_MIX + i, l)
                    if i == 5:
                        sp.wait_ge(*sg.at("hT_transposed", l, 8))
                        sp.wait_ge(mem_stored, 16)
                        sp.dma_start(memn, mem_scratch).then_inc(mem_loaded, 16)
                for u, n in ((U_XK, "xa_wk"), (U_XV, "xa_wv")):
                    for i in range(4):
                        unit(as_cols(u + i), wide[n][:, l, :, 256 * i:256 * i + 256], u + i, l)
                for i in range(4):
                    unit(as_rows(U_OUT + i), wide["w_mix_out"][:, l, 2 * i:2 * i + 2, :], U_OUT + i, l)
                for i in range(4):
                    unit(as_cols(U_XQ + i), wide["xa_wq"][:, l, :, 256 * i:256 * i + 256], U_XQ + i, l)
                for i in range(4):
                    unit(as_rows(U_XO + i), wide["xa_wo"][:, l, 2 * i:2 * i + 2, :], U_XO + i, l)
                ffn_units(l, "ffn2", U_FFN2)
            sp.wait_ge(*sg.at("x_updated", DEPTH - 1))
            sp.dma_start(vx[:, 0, :], a["final_norm"].rearrange("(o d) -> o d", o=1).broadcast_to([P, D]))\
                .then_inc(small_loaded, 16)
            for t in range(NT):
                sp.wait_ge(sg.sem("out_ready"), t + 1)
                sp.dma_start(out_v[:, t, :], hn[:, t, :]).then_inc(out_done, 16)
            sp.wait_ge(out_done, 16 * NT)

        @block.tensor
        def _(pe):
            def norm_transposes(ready, src=hn, bk=4):
                for t in range(NT):
                    pe.wait_ge(*ready(t))
                    for c in range(KC):
                        tr = pe.transpose(b4(bk + 2 * t + c // 4)[:, c % 4, :], src[:, t, c * P:c * P + P], ident[:, :])
                        if c % 4 == 3:
                            yield tr

            def norm(l, k):
                def ready(t):
                    if k == 0 and t == 1:
                        pe.wait_ge(*sg.at("cols_ready", l))
                    return sg.at("hn_ready", l, NT * k + t + 1)

                for tr in norm_transposes(ready, bk=norm_bank(k)):
                    tr.then_inc(sg.inc("hT_transposed"), 1)

            pe.sem_inc(split_used, SETS)
            pe.wait_ge(sg.sem("ident_ready"), 1)
            for tr in norm_transposes(lambda t: (sg.sem("set_up_vector"), 2 + t + 1), src=vx, bk=0):
                tr.then_inc(sg.sem("mem_transposed"), 1)

            def feature_major(pos, bk, src, l):
                pe.wait_ge(*unit_landed(pos, l))
                w = as_cols(pos)
                for b in range(2):
                    for c in range(KC):
                        mm = pe.matmul(b2(bk)[:, b, :], w[:, c, b * P:b * P + P], src[:, c, :],
                                       start=(c == 0), stop=(c == KC - 1))
                mm.then_inc(mixer_unit_used, 1)

            def token_major(pos, bk, src, l, w=256):
                pe.wait_ge(*unit_landed(pos, l))
                wt = as_cols(pos, w)
                for t in range(NT):
                    for c in range(KC):
                        mm = pe.matmul(b2(bk)[:, t, 0:w], src[:, c, t * P:t * P + P], wt[:, c, :],
                                       start=(c == 0), stop=(c == KC - 1))
                mm.then_inc(mixer_unit_used, 1)

            def rows_product(pos, src, c0, bk, l, first, last, it=0):
                pe.wait_ge(*unit_landed(pos, l, it))
                w = as_rows(pos)
                for t in range(NT):
                    for n in range(2):
                        for c in range(2):
                            mm = pe.matmul(bank[bk + 2 * t + n][:, :], src[:, c0 + c, t * P:t * P + P],
                                           w[:, c, 512 * n:512 * n + 512],
                                           start=(first and c == 0), stop=(last and c == 1),
                                           skip_group_check=True)
                        if last and (t, n) != (NT - 1, 1):
                            mm.then_inc(sg.inc("bank_summed"), 1)
                mm.then_inc(mixer_unit_used, 1)

            def split_columns(l, q, set_, out, after_norm=None, block_done=None, two_banks=True, src=xT_parts):
                w_hl = split_set(set_, KC)

                def products(b, pairs, first=True, last=True, start=True):
                    for c in range(KC):
                        if after_norm is not None and b == 0 and first and c % 4 == 0:
                            part = "xT_low_ready" if (0, 1) in pairs else "xT_high_ready"
                            pe.wait_ge(*sg.at(part, l, 4 * after_norm + 2 + c // 4 + 1))
                        for i, (wp, xp) in enumerate(pairs):
                            mm = pe.matmul(out(b), w_hl[wp][:, c, b * P:b * P + P], src[xp][:, c, :],
                                           start=(first and start and c == 0 and i == 0),
                                           stop=(last and c == KC - 1 and i == len(pairs) - 1),
                                           skip_group_check=after_norm is not None)
                    return mm

                if after_norm is not None:
                    pe.wait_ge(high_ready, nth(l, q))
                    for blocks in ((0, 1),) if two_banks else ((0,), (1,)):
                        for b in blocks:
                            products(b, HIGH_WEIGHT[:1], last=False)
                        for b in blocks:
                            products(b, HIGH_WEIGHT[1:], start=False, last=False)
                        pe.wait_ge(*low_done(l, q))
                        for b in blocks:
                            mm = products(b, LOW_WEIGHT, first=False)
                else:
                    pe.wait_ge(*low_done(l, q))
                    mm = products(0, HIGH_WEIGHT + LOW_WEIGHT)
                    if block_done:
                        mm.then_inc(block_done, 1)
                    mm = products(1, HIGH_WEIGHT + LOW_WEIGHT)
                mm.then_inc(split_used, 1)

            def split_tokens(l, q, bk, src, w=256):
                w_hl = split_set(q, KC)
                pe.wait_ge(*low_done(l, q))
                for t in range(NT):
                    for c in range(KC):
                        for i, (wp, xp) in enumerate(HIGH_WEIGHT + LOW_WEIGHT):
                            mm = pe.matmul(b2(bk)[:, t, 0:w], src[xp][:, c, t * P:t * P + P], w_hl[wp][:, c, :],
                                           start=(c == 0 and i == 0), stop=(c == KC - 1 and i == 2))
                mm.then_inc(split_used, 1)

            def split_rows(l, q, set_, src, bk, first, last):
                w_hl = split_set(set_, 2)
                pe.wait_ge(*low_done(l, q))
                for t in range(NT):
                    for n in range(2):
                        for c in range(2):
                            for i, (wp, xp) in enumerate(HIGH_WEIGHT + LOW_WEIGHT):
                                mm = pe.matmul(bank[bk + 2 * t + n][:, :], src(xp)[:, c, t * P:t * P + P],
                                               w_hl[wp][:, c, 512 * n:512 * n + 512],
                                               start=(first and c == 0 and i == 0), stop=(last and c == 1 and i == 2),
                                               skip_group_check=True)
                        if last and (t, n) != (NT - 1, 1):
                            mm.then_inc(sg.inc("bank_summed"), 1)
                mm.then_inc(split_used, 1)

            def ffn(l, which):
                q0 = Q_FFN[which]

                def gate_and_up(n, set_, par, s, after_norm=None):
                    pe.wait_ge(sg.sem("hid_ready"), blocks_of(l, which, s - 2))
                    for k in range(2):
                        split_columns(l, q0 + n + k, q0 + set_ + k, lambda b: b2(4 + 2 * par + b)[:, k, :],
                                      None if k else after_norm, sg.sem("first_block_done") if k else None)

                def down(n, set_, par, s, first=False, last=False):
                    pe.wait_ge(sg.sem("hid_low_ready"), step_of(l, which, s))
                    split_rows(l, q0 + n, q0 + set_, lambda part: hid_parts[part][:, par], 0, first, last)

                def pair(s, first=False):
                    for i, par in enumerate((1, 0)):
                        n = 3 * (s + i) + 2
                        gate_and_up(n, 2, par, s + i + 1)
                        down(n + 2, 4, 1 - par, s + i, first=first and i == 0)

                gate_and_up(0, 0, 0, 0, after_norm=3 * which)
                pair(0, first=True)
                with pe.Fori(1, PAIRS) as it:
                    pair(it * 2)
                down(FFN_UNITS - 1, FFN_UNITS - 1, 0, STEPS - 1, last=True)

            def hs(h):
                return slice(HD * (h % 2), HD * (h % 2) + HD)

            def mixer(l):
                for i in range(3):
                    split_columns(l, Q_MIX + i, Q_MIX + i, lambda b: b2(i)[:, b, :], None if i else 1,
                                  two_banks=False, src=xm_parts)
                for t in range(NT):
                    for c in range(KC):
                        mm = pe.matmul(bank[3][:, 8 * t:8 * t + 8], hT[:, c, t * P:t * P + P], wab[:, c, :],
                                       start=(c == 0), stop=(c == KC - 1))
                mm.then_inc(sg.inc("ab_projected"), 1)
                split_tokens(l, Q_MIX + 3, 4, xm_parts)
                split_tokens(l, Q_MIX + 4, 5, xm_parts)
                pe.wait_ge(*sg.at("silu_done", l, 2))
                for t in range(NT):
                    for b in range(4):
                        tr = pe.transpose(b4(t)[:, b, :], cv[:, b, t * P:t * P + P], ident[:, :])
                    tr.then_inc(sg.inc("qkv_transposed"), 1)
                split_tokens(l, Q_MIX + 5, 6, xm_parts, W_IQ1)
                pe.wait_ge(*sg.at("g_ready", l))
                pe.matmul(bank[3][:, 32:40], incl[:, :], gg_, start=True, stop=True)
                pe.matmul(bank[3][:, 64:72], same[:, :], gg_, start=True, stop=True)
                for c in range(NCH):
                    mm = pe.matmul(bank[3][:, 96 + 4 * c:100 + 4 * c], half[:, c % 2, :],
                                   gg_[:, 4 * (c // 2):4 * (c // 2) + 4], start=True, stop=True)
                mm.then_inc(sg.inc("gates_summed"), 1)
                split_tokens(l, Q_MIX + 6, 7, xm_parts)
                pe.wait_ge(*sg.at("silu_done", l))
                for t in range(NT):
                    for b in range(2):
                        tr = pe.transpose(b4(2)[:, 2 * t + b, :], cv[:, 4 + b, t * P:t * P + P], ident[:, :])
                tr.then_inc(sg.inc("qkv_transposed"), 1)
                pe.wait_ge(*sg.at("cn_ready", l))
                pe.wait_ge(*sg.at("q_copied", l))
                for t in range(NT):
                    tr = pe.transpose(bank[4][:, t * P:t * P + P], cn[:, t, :], ident[:, :])
                tr.then_inc(sg.inc("c_transposed"), 1)
                pe.wait_ge(*sg.at("iq1_copied", l))
                split_tokens(l, Q_MIX + 7, 6, xm_parts)
                pe.wait_ge(*sg.at("cT_ready", l))
                for t in range(NT):
                    pe.matmul(bank[4 + t][:, :], cT[:, t * P:t * P + P],
                              w_kv[:, :, :].rearrange("p i n -> p (i n)"), start=True, stop=True)\
                        .then_inc(sg.inc("kv_up"), 1)
                pe.wait_ge(*sg.at("gm_ready", l))
                pe.wait_ge(*sg.at("sums_copied", l))
                pe.matmul(bank[3][:, :], onesm[:, :], Sm_buf[:, 0:512], start=True, stop=True)\
                    .then_inc(sg.inc("gc_rows"), 1)
                pe.wait_ge(*sg.at("v_copied", l))
                pe.matmul(bank[2][:, :], onesm[:, :], Sm_buf[:, 512:1024], start=True, stop=True)\
                    .then_inc(sg.inc("gc_rows"), 1)
                pe.wait_ge(*sg.at("sgv_gelu", l))
                split_columns(l, Q_MIX + 8, Q_MIX + 8, lambda b: b2(7)[:, b, :], src=xm_parts)
                def pair_of(v, first):
                    return lambda t, b: v[:, t, first + 2 * b:first + 2 * b + 2, :].rearrange("p h c -> p (h c)")

                def block_of(v):
                    return lambda t, b: v[:, t, b * P:b * P + P]

                for i, (src, bk, ev) in enumerate(((pair_of(qk, 4), 0, "qk_scaled"), (block_of(kb), 1, "kb_ready"),
                                                   (pair_of(qk, 0), 0, "qk_scaled"), (block_of(qg), 1, "qg_ready"))):
                    pe.wait_ge(*sg.at(ev, l))
                    if i >= 2:
                        pe.wait_ge(*sg.at("gT_copied", l, i - 1))
                    for b in range(2):
                        for t in range(NT):
                            tr = pe.transpose(b2(bk)[:, b, t * P:t * P + P], src(t, b), ident[:, :])
                    tr.then_inc(sg.inc("gT_transposed"), 1)
                pe.wait_ge(*sg.at("sgu_gelu", l))
                feature_major(U_SCH, 6, hT, l)
                pe.wait_ge(*sg.at("rope_q", l))
                pe.wait_ge(*sg.at("kv_copied", l))
                for bk, s0, n in ((4, 0, 2), (5, 4, 2), (4, 8, 1), (5, -1, 2)):
                    if (bk, s0) == (4, 8):
                        pe.wait_ge(*sg.at("dT_copied", l, 1))
                    if s0 < 0:
                        pe.wait_ge(*sg.at("dT_copied", l, 2))
                        pe.wait_ge(*sg.at("rope_k", l))
                    for b in range(n):
                        for t in range(NT):
                            src = (dk[:, t, b * P:b * P + P] if s0 < 0 else
                                   R[:, t, s0 + 2 * b:s0 + 2 * b + 2, :].rearrange("p h c -> p (h c)"))
                            tr = pe.transpose(b2(bk)[:, b, t * P:t * P + P], src, ident[:, :])
                    tr.then_inc(sg.inc("dT_transposed"), 1)
                pe.wait_ge(*sg.at("gT_copied", l))
                pe.wait_ge(*sg.at("ET_read", l))
                for t in range(NT):
                    for odd in range(2):
                        for i, src in enumerate((kbT, qT)):
                            for b in range(2):
                                h = 2 * b + odd
                                mm = pe.matmul(b4(2 * t + odd)[:, 2 * i + b, :], kT[hs(h), b, t * P:t * P + P],
                                               src[hs(h), b, t * P:t * P + P], start=True, stop=True)
                        mm.then_inc(sg.inc("kq_done"), 1)
                pe.wait_ge(*sg.at("dT_copied", l))
                for t in range(NT):
                    n = P * (t + 1)
                    for odd in range(2):
                        if t:
                            pe.wait_ge(*sg.at("relu_done", l, odd + 1))
                        for b in range(2):
                            h = 2 * b + odd
                            mm = pe.matmul(bank[4 + odd][:, n * b:n * b + n], diqT[hs(h), b, t * P:t * P + P],
                                           dikT[hs(h), 0:n], start=True, stop=True)
                        mm.then_inc(sg.inc("index_scores"), 1)
                pe.wait_ge(*sg.at("scc_copied", l))
                feature_major(U_SCB, 7, hT, l)

                def level_u(i, t):
                    pe.wait_ge(*sg.at("B_ready", l, NT * i + t + 1))
                    if i:
                        pe.wait_ge(*sg.at("TS_ready", l, 2 * (NT * (i - 1) + t) + 2))
                    else:
                        pe.wait_ge(*sg.at("AE_ready", l))
                    for h in range(H):
                        mm = pe.matmul(b4(2 * t)[:, h, :], Bm[i % 2][:, t, h, :],
                                       ident[:, :] if i == 0 else Tm[:, t, h, :], start=True, stop=True)
                    mm.then_inc(sg.inc("U_done"), 1)

                def level_ts(i, t):
                    pe.wait_ge(*sg.at("U_copied", l, NT * (i - 1) + t + 1))
                    if i < len(LEVELS) - 1:
                        for h in range(H):
                            mm = pe.matmul(b4(2 * t + 1)[:, h, :], Sm[:, t, h, :], Um[:, t, h, :], start=True, stop=True)
                        mm.then_inc(sg.inc("TS_done"), 1)
                    for h in range(H):
                        mm = pe.matmul(b4(2 * t)[:, h, :], Um[:, t, h, :], Sm[:, t, h, :], start=True, stop=True)
                    mm.then_inc(sg.inc("TS_done"), 1)

                fillers = {1: lambda: (pe.wait_ge(*sg.at("sch_copied", l)), token_major(U_GG, 6, hT, l)),
                           2: lambda: xa_key(0), 3: lambda: xa_key(1), 4: lambda: xa_key(2), 5: lambda: xa_key(3)}

                def xa_bank(i):
                    if i == 0:
                        pe.wait_ge(*sg.at("scb_copied", l))
                        pe.wait_ge(*sg.at("memn_ready", l))
                    elif i == 1:
                        pe.wait_ge(*sg.at("gate_read", l))
                    else:
                        pe.wait_ge(*sg.at("xkv_copied", l, i - 1))
                    return 7 - i % 2

                def xa_key(i):
                    feature_major(U_XK + i, xa_bank(i), memn, l)

                def xa_value(i):
                    if i >= 2:
                        pe.wait_ge(*(sg.at("sgwT_ready", l) if i == 2 else sg.at("xkv_copied", l, 7)))
                    token_major(U_XV + i, VALUE_UNIT_BANK[i] if i >= 2 else xa_bank(4 + i), memn, l)

                for t in range(NT):
                    level_u(0, t)
                for i in range(1, len(LEVELS)):
                    for t in range(NT):
                        level_u(i, t)
                    fillers[i]()
                    for t in range(NT):
                        level_ts(i, t)
                xa_value(0)
                pe.wait_ge(*sg.at("TS_ready", l))
                for t in range(NT):
                    for h in range(H):
                        mm = pe.matmul(b2(0)[:, t, HD * h:HD * h + HD], Sm[:, t, h, :],
                                       vb[:, t, HD * h:HD * h + HD], start=True, stop=True)
                mm.then_inc(sg.inc("u_done"), 1)
                for t in range(NT):
                    for h in range(H):
                        mm = pe.matmul(b2(1)[hs(h), h // 2, t * P:t * P + P], kbg[:, t, HD * h:HD * h + HD],
                                       Sm[:, t, h, :], start=True, stop=True)
                mm.then_inc(sg.inc("w_done"), 1)
                xa_value(1)
                def chunk_read(c):
                    t, r = c // 2, CH * (c % 2)
                    pe.wait_ge(*sg.at("uw_copied", l))
                    pe.wait_ge(*sg.at("state_ready", l, c + 1))
                    if c:
                        pe.wait_ge(*sg.at("qs_copied", l, 2 * c))
                    apart(pe)
                    for odd in range(2):
                        for i, src in enumerate((wT, qgT)):
                            for b in range(2):
                                rows_ = slice(HD * odd, HD * odd + HD)
                                mm = pe.matmul(bank[odd][r:r + CH, P * i + HD * b:P * i + HD * b + HD],
                                               src[rows_, b, t * P + r:t * P + r + CH], state[rows_, b, :],
                                               start=True, stop=True)
                    mm.then_inc(sg.inc("ws_done"), 1)

                def chunk_write(c):
                    t, r = c // 2, CH * (c % 2)
                    pe.wait_ge(*sg.at("vnew_ready", l, 2 * c + 2))
                    apart(pe)
                    for h in range(H):
                        mm = pe.matmul(bank[2][hs(h), HD * (h // 2):HD * (h // 2) + HD], kd[r:r + CH, t, HD * h:HD * h + HD],
                                       vnew[r:r + CH, t, HD * h:HD * h + HD], start=True, stop=True)
                    mm.then_inc(sg.inc("kv_done"), 1)
                    for h in range(H):
                        mm = pe.matmul(b2(3)[r:r + CH, t, HD * h:HD * h + HD], AT[r:r + CH, t, h, r:r + CH],
                                       vnew[r:r + CH, t, HD * h:HD * h + HD], start=True, stop=True)
                    mm.then_inc(sg.inc("o_done"), 1)

                def dsa_logits(t):
                    pe.wait_ge(*(sg.at("logits_read", l, 2) if t else sg.at("relu_done", l)))
                    n = P * (t + 1)
                    for odd in range(2):
                        for b in range(2):
                            h = 2 * b + odd
                            mm = pe.matmul(bank[4 + odd][:, n * b:n * b + n], dqT[hs(h), b, t * P:t * P + P],
                                           dkT[hs(h), b, 0:n], start=True, stop=True)
                    mm.then_inc(sg.inc("logits_done"), 1)

                def dsa_transposes(i):
                    if i == 0:
                        pe.wait_ge(*sg.at("probs_ready", l, 1))
                        for h in range(H):
                            tr = pe.transpose(b4(7)[:, h, :], Pds[0][:, P * h:P * h + P], ident[:, :])
                    else:
                        pe.wait_ge(*sg.at("probs_ready", l, 2))
                        pe.wait_ge(*sg.at("logits_read", l))
                        for h in range(H):
                            tr = pe.transpose(b4(5 if i == 1 else 4)[:, h, :],
                                              Pds[1][:, 2 * P * h + P * (i - 1):2 * P * h + P * i], ident[:, :])
                    tr.then_inc(sg.inc("PT_transposed"), 1)

                def dsa_values():
                    pe.wait_ge(*sg.at("PT_copied", l))
                    for i, h in enumerate((0, 2, 1, 3)):
                        pe.matmul(b2(5)[hs(h), h // 2, 0:P], dv[:, 0, HD * h:HD * h + HD], PT[:, P * i:P * i + P],
                                  start=True, stop=True)
                        for k in range(2):
                            mm = pe.matmul(b2(5)[hs(h), h // 2, P:2 * P], dv[:, k, HD * h:HD * h + HD],
                                           PT[:, 512 * (k + 1) + P * i:512 * (k + 1) + P * i + P],
                                           start=(k == 0), stop=(k == 1))
                    mm.then_inc(sg.inc("dsa_out"), 1)

                chunk_read(0)
                dsa_logits(0)
                pe.wait_ge(*sg.at("xkv_copied", l, 5))
                for h in range(H):
                    tr = pe.transpose(b4(7)[:, h, :], sgw[:, h, :], ident[:, :])
                tr.then_inc(sg.inc("sgw_transposed"), 1)
                chunk_write(0)
                chunk_read(1)
                dsa_logits(1)
                xa_value(2)
                chunk_write(1)
                pe.wait_ge(*sg.at("xkv_copied", l, 6))
                pe.wait_ge(*sg.at("sgwT_ready", l))
                pe.wait_ge(*sg.at("sgn_ready", l))
                for t in range(NT):
                    for h in range(H):
                        mm = pe.matmul(b2(6)[:, t, HD * h:HD * h + HD], sgwT[:, h, :], sgn[:, t, HD * h:HD * h + HD],
                                       start=True, stop=True)
                mm.then_inc(sg.inc("sg_mixed"), 1)
                chunk_read(2)
                xa_value(3)
                chunk_write(2)
                chunk_read(3)
                pe.wait_ge(*sg.at("sg_out", l))
                for b in range(2):
                    for t in range(NT):
                        tr = pe.transpose(b2(6)[:, b, t * P:t * P + P], sgj[:, t, b * P:b * P + P], ident[:, :])
                tr.then_inc(sg.inc("sg_transposed"), 1)
                chunk_write(3)
                pe.wait_ge(*sg.at("xkv_copied", l))
                dsa_transposes(0)
                dsa_transposes(1)
                dsa_transposes(2)
                dsa_values()
                pe.wait_ge(*sg.at("yT_ready", l, 2))
                rows_product(U_OUT, yT, 0, 4, l, True, False)
                pe.wait_ge(*sg.at("gdn_out", l))
                for b in range(2):
                    for t in range(NT):
                        tr = pe.transpose(b2(0)[:, b, t * P:t * P + P], vnew[:, t, b * P:b * P + P], ident[:, :])
                tr.then_inc(sg.inc("gdn_transposed"), 1)
                pe.wait_ge(*sg.at("sc_out", l))
                rows_product(U_OUT + 1, yT, 2, 4, l, False, False)
                rows_product(U_OUT + 2, yT, 4, 4, l, False, False)
                pe.wait_ge(*sg.at("y_low", l))
                split_rows(l, Q_OUT3, Q_OUT3, lambda part: hid_parts[part][:, 0], 4, False, True)

            def cross(l):
                def queries(h):
                    split_columns(l, Q_XQ + h, Q_XQ + h, lambda b: b2(4 * (h % 2))[:, b, :], None if h else 2,
                                  two_banks=False)

                def logits(h):
                    pe.wait_ge(*sg.at("xq_copied", l, h + 1))
                    bk = (1, 5, 1, 0)[h]
                    if h == 2:
                        pe.wait_ge(*sg.at("xexp_done", l, NT))
                    for t in range(NT):
                        for b in range(2):
                            mm = pe.matmul(b2(bk)[:, t, :], xqT[:, 2 * h + b, t * P:t * P + P], kxT[:, 2 * h + b, :],
                                           start=(b == 0), stop=(b == 1))
                    mm.then_inc(sg.inc("xlogits"), 1)

                def transposes(h):
                    pe.wait_ge(*sg.at("xprobs", l, h + 1))
                    if h:
                        pe.wait_ge(*sg.at("xPT_copied", l, h))
                    for k in range(2):
                        for t in range(NT):
                            tr = pe.transpose(b2(2)[:, k, t * P:t * P + P], xP[:, h % 2, t, k * P:k * P + P], ident[:, :])
                    tr.then_inc(sg.inc("xPT"), 1)

                def values(h):
                    pe.wait_ge(*sg.at("xPT_copied", l, h + 1))
                    if h == H - 1:
                        pe.wait_ge(*sg.at("xexp_done", l, NT * (H - 1)))
                    elif h:
                        pe.wait_ge(*sg.at("oT_low", l, h))
                    for b in range(2):
                        for k in range(2):
                            mm = pe.matmul(b2(VALUES_BANK[h])[:, b, :], vx[:, k, 256 * h + b * P:256 * h + b * P + P],
                                           xPT[:, h % 2, k, :], start=(k == 0), stop=(k == 1))
                    mm.then_inc(sg.inc("xvalues"), 1)

                def project(h):
                    pe.wait_ge(*sg.at("oT_low", l, h + 1))
                    if h == 0:
                        pe.wait_ge(*sg.at("xq_copied", l))
                        pe.wait_ge(*sg.at("xexp_done", l, 2 * NT))
                    split_rows(l, Q_XO + h, Q_XO + h, lambda part: oT_parts[part][:, h % 2], 4, h == 0, h == H - 1)

                queries(0), queries(1), logits(0), queries(2), logits(1), transposes(0), queries(3), values(0)
                logits(2), transposes(1), project(0), values(1), transposes(2), logits(3), values(2), project(1)
                transposes(3), values(3), project(2), project(3)

            with pe.Fori(0, DEPTH) as l:
                pe.wait_ge(par_loaded, (l + 1) * N_ROW_LOADS * 16)
                pe.wait_ge(sg.sem("memT_copied"), 4)
                pe.wait_ge(sg.sem("hid_ready"), blocks_of(l, 0, -1))
                apart(pe)
                pe.transpose(bank[7][:, 0:N_ROWS], rows[:, :], ident[0:N_ROWS, 0:N_ROWS])\
                    .then_inc(sg.inc("rows_transposed"), 1)
                norm(l, 0)
                ffn(l, 0)
                norm(l, 1)
                pe.wait_ge(mixer_par_loaded, (l + 1) * N_MIXER_LOADS * 16)
                mixer(l)
                norm(l, 2)
                cross(l)
                norm(l, 3)
                ffn(l, 1)

        @block.scalar
        def _(act):
            def mean_squares(l, k, signal):
                for t in range(NT):
                    for n in range(2):
                        act.wait_ge(*sg.at("x_updated", l, 4 * k - 4 + 2 * t + n + 1) if k else
                                    sg.at("x_updated", l, 2 * t + n + 1 - 4))
                        part = slice(512 * n, 512 * n + 512)
                        act.activation(hn[:, t, part], x[:, t, part], ACT.Square, scale=float(D) ** -0.5,
                                       accum_out=ms[:, 2 * t + n:2 * t + n + 1]).then_inc(signal(), 1)

            def link(ins, l):
                ins.then_inc(sg.inc("scalar_link"), 1)
                act.wait_ge(*sg.at("scalar_link", l, sg.counts["scalar_link"]))

            act.wait_ge(mem_in, 16)
            for t in range(NT):
                act.activation(yT[:, 0:4, :].rearrange("p c s -> p (c s)"), vx[:, t, :], ACT.Square,
                               scale=float(D) ** -0.5, accum_out=msb[:, 2 + t:3 + t]).then_inc(sg.sem("mem_ms"), 1)
                act.wait_ge(sg.sem("mem_ms"), t + 1)
            act.wait_ge(sg.sem("set_up_vector"), 2)
            act.activation(rs[:, :, ROT:2 * ROT], rtmp[:, :, 0, 0:ROT], ACT.Sin).then_inc(sg.sem("trig_done"), 1)
            act.activation(rc[:, :, 0:ROT], rtmp[:, :, 1, 0:ROT], ACT.Sin).then_inc(sg.sem("trig_done"), 1)
            act.wait_ge(sg.sem("trig_done"), 2)
            act.activation(rs[:, :, 0:ROT], rs[:, :, ROT:2 * ROT], ACT.Copy, scale=-1.0).then_inc(sg.sem("trig_done"), 1)
            act.activation(rc[:, :, ROT:2 * ROT], rc[:, :, 0:ROT], ACT.Copy).then_inc(sg.sem("trig_done"), 1)
            act.wait_ge(sg.sem("mem_transposed"), 4)
            for i in range(4):
                act.activation(piece(vx[:, :, :].rearrange("p t d -> p (t d)").rearrange("p (c s) -> p c s", c=KC), i),
                               b4(i), ACT.Copy)\
                    .then_inc(sg.sem("memT_copied"), 1)
            act.wait_ge(sg.sem("memT_copied"), 4)
            act.dma_start(mem_scratch.rearrange("p c s -> p (c s)"), vx[:, :, :].rearrange("p t d -> p (t d)"))\
                .then_inc(mem_stored, 16)

            def norm(l, k, row):
                act.wait_ge(x_loaded, 16)
                if k == 2:
                    high(l, Q_XQ + 1)
                mean_squares(l, k, lambda: sg.inc("ms_ready"))
                if k == 0:
                    high(l, 0)
                if k == 1:
                    act.wait_ge(mem_stored, 16)
                    high(l, Q_MIX + 1)
                for j in range(4):
                    act.wait_ge(*sg.at("hT_ready", l, 4 * k + j + 1))
                    act.activation(piece((xm_parts if k == 1 else xT_parts)[0], j), piece(hT, j), ACT.Copy)\
                        .then_inc(sg.inc("xT_high_ready"), 1)
                if k == 0:
                    high(l, 1)

            def high(l, q, it=0):
                pos, ((high_, low_), n) = position(q), parts_of(q)
                act.wait_ge(*unit_landed(pos, l, it))
                act.wait_ge(*set_free(l, it * 6 + q))
                act.activation(high_[:, 0:n], ring[pos % RING][:, 0:n], ACT.Copy).then_inc(high_ready, 1)

            def ffn(l, which):
                q0 = Q_FFN[which]

                def step(par, s, it=0):
                    q = q0 + 3 * par + 2
                    split_next = s is not LAST
                    if split_next:
                        high(l, q, it)
                    else:
                        s = STEPS - 1
                    act.wait_ge(sg.sem("first_block_done"), step_of(l, which, s))
                    act.activation(sil[:, par, 0, :], b2(4 + 2 * par)[:, 0, :], ACT.Silu).then_inc(sg.sem("silu_ready"), 1)
                    if not split_next:
                        high(l, q0 + FFN_UNITS - 1)
                    act.wait_ge(*products_done(l, s * 3 + q0 + (1 if isinstance(s, int) and s == 0 else 0)))
                    act.activation(sil[:, par, 1, :], b2(5 + 2 * par)[:, 0, :], ACT.Silu).then_inc(sg.sem("silu_ready"), 1)
                    if split_next:
                        high(l, q + 1, it)
                    act.wait_ge(sg.sem("hid_ready"), blocks_of(l, which, s))
                    act.activation(hid_parts[0][:, par, :, :], hid[:, par, :, :], ACT.Copy)\
                        .then_inc(sg.sem("hid_high_ready"), 1)
                    if split_next:
                        high(l, q + 2, it)
                    elif which == 0:
                        high(l, Q_MIX)

                step(0, 0)
                step(1, 1)
                with act.Fori(1, PAIRS) as it:
                    step(0, it * 2, it)
                    step(1, it * 2 + 1, it)
                step(0, LAST)

            def mixer(l):
                def copy(dst, src, name, func=ACT.Copy, **kw):
                    act.activation(dst, src, func, **kw).then_inc(sg.inc(name), 1)

                act.wait_ge(*sg.at("pads_ready", l))
                for i in range(3):
                    act.wait_ge(*products_done(l, Q_MIX + i))
                    copy(z[:, 2 * i:2 * i + 2, 3:3 + S], b2(i), "z_copied")
                    high(l, Q_MIX + 2 + i)
                act.wait_ge(*sg.at("ab_projected", l))
                copy(ab, bank[3][:, 0:16].rearrange("p (t c) -> p t c", t=NT), "ab_copied")
                act.activation(alog, b_alog, ACT.Exp)
                act.wait_ge(*sg.at("soft_in", l))
                act.activation(ga2, ga2, ACT.Exp)
                link(act.activation(beta, beta, ACT.Exp, scale=-1.0), l)
                copy(ga3, ga2, "soft_ln", ACT.Ln, bias=1.0)
                for i in range(2):
                    act.wait_ge(*sg.at("conv_qk", l, 2 * i + 2))
                    copy(cv[:, 2 * i:2 * i + 2, :], cv[:, 2 * i:2 * i + 2, :], "silu_done", ACT.Silu)
                act.wait_ge(*products_done(l, Q_MIX + 3))
                copy(R[:, :, 0:4, :], b2(4).rearrange("p t (h c) -> p t h c", h=4), "q_copied")
                high(l, Q_MIX + 5)
                act.wait_ge(*products_done(l, Q_MIX + 4))
                for t in range(NT):
                    copy(cn[:, t, :], b2(5)[:, t, 0:LAT], "msa_ready", ACT.Square, scale=float(LAT) ** -0.5,
                         accum_out=msa[:, t:t + 1])
                copy(R[:, :, 4:6, :], b2(5)[:, :, LAT:256].rearrange("p t (h c) -> p t h c", h=2), "iq0_copied")
                high(l, Q_MIX + 6)
                for t in range(NT):
                    act.wait_ge(*sg.at("qkv_transposed", l, t + 1))
                    copy(Bm[0][:, t, :, :].rearrange("p h c -> p (h c)"), bank[t][:, :], "qk_squared", ACT.Square)
                act.wait_ge(*sg.at("conv_v", l))
                copy(cv[:, 4:6, :], cv[:, 4:6, :], "silu_done", ACT.Silu)
                act.wait_ge(*products_done(l, Q_MIX + 5))
                for t in range(NT):
                    copy(R[:, t, 8, :], b2(6)[:, t, P:P + HD], "msa_ready", ACT.Square, scale=float(HD) ** -0.5,
                         accum_out=msa[:, 2 + t:3 + t])
                copy(R[:, :, 6:8, :], b2(6)[:, :, 0:P].rearrange("p t (h c) -> p t h c", h=2), "iq1_scalar")
                copy(iw, b2(6)[:, :, P + HD:P + HD + H], "iq1_scalar", scale=0.0625)
                high(l, Q_MIX + 7)
                act.wait_ge(*sg.at("gates_summed", l))
                copy(gc, bank[3][:, 32:40], "gc_ready")
                copy(ngc, bank[3][:, 32:40], "gc_ready", scale=-1.0)
                act.activation(egl, bank[3][:, 96:112].rearrange("p (c h) -> p c h", c=NCH), ACT.Exp)
                act.activation(egc, bank[3][:, 32:40], ACT.Exp).then_inc(sg.inc("egc_ready"), 1)
                act.wait_ge(*sg.at("ekd_in", l))
                copy(ekd, ekd, "sums_copied", ACT.Exp)
                act.wait_ge(*products_done(l, Q_MIX + 6))
                copy(sgv, b2(7), "sgv_gelu", ACT.Gelu_apprx_tanh)
                high(l, Q_MIX + 8)
                act.wait_ge(*sg.at("sgv_gelu", l))
                for t in range(NT):
                    copy(sgn[:, t, :], sgv[:, t, :], "mss_ready", ACT.Square, scale=float(GW) ** -0.5,
                         accum_out=mss[:, t:t + 1])
                act.wait_ge(*products_done(l, Q_MIX + 7))
                copy(sgu, b2(6), "sgu_gelu", ACT.Gelu_apprx_tanh)
                act.wait_ge(*sg.at("qkv_transposed", l))
                copy(gv[:, :, :], b2(2), "v_copied")
                for t in range(NT):
                    act.wait_ge(*sg.at("kv_up", l, t + 1))
                    copy(dv[:, t, :], b2(4 + t)[:, 1, :], "kv_copied")
                    copy(dk[:, t, :], b2(4 + t)[:, 0, :], "kv_copied")
                for t in range(NT):
                    act.wait_ge(*sg.at("ET_in", l, t + 1))
                    for h in range(H):
                        copy(ET[:, t, h, :], ET[:, t, h, :], "ET_ready", ACT.Exp, bias=ngc[:, H * t + h:H * t + h + 1])
                act.wait_ge(*products_done(l, Q_MIX + 8))
                copy(scz[:, :, 2:2 + S], b2(7), "scc_copied")
                for i, dst in enumerate((kT, kbT, qT, qgT)):
                    act.wait_ge(*sg.at("gT_transposed", l, i + 1))
                    copy(dst, b2(i % 2), "gT_copied")
                act.wait_ge(*unit_used(U_SCH, l))
                copy(sch[:, :, :], b2(6), "sch_copied")
                for i, (dst, src) in enumerate(((dqT[:, :, :], b2(4)), (diqT[:, :, :], b2(5)), (dikT[:, :], bank[4][:, 0:S]),
                                                (dkT[:, :, :], b2(5)))):
                    act.wait_ge(*sg.at("dT_transposed", l, i + 1))
                    copy(dst, src, "dT_copied")
                for t in range(NT):
                    n = 2 * P * (t + 1)
                    for odd in range(2):
                        act.wait_ge(*sg.at("index_scores", l, 2 * t + odd + 1))
                        if t:
                            act.wait_ge(*sg.at("score_added", l))
                        copy(rel[:, n * odd:n * odd + n], bank[4 + odd][:, 0:n], "relu_done", ACT.Relu)
                act.wait_ge(*unit_used(U_SCB, l))
                copy(yT[:, 2:4, :], b2(7), "scb_copied")
                for i in range(1, len(LEVELS)):
                    for t in range(NT):
                        act.wait_ge(*sg.at("U_done", l, NT * i + t + 1))
                        copy(Um[:, t, :, :], b4(2 * t), "U_copied")
                    if i == 1:
                        act.wait_ge(*unit_used(U_GG, l))
                        copy(gate[:, :, :], b2(6), "gate_read", ACT.Silu)
                    else:
                        act.wait_ge(*unit_used(U_XK + i - 2, l))
                        copy(kxT[:, 2 * (i - 2):2 * (i - 2) + 2, :], b2(7 - (i - 2) % 2), "xkv_copied")

                def value_copy(i):
                    act.wait_ge(*unit_used(U_XV + i, l))
                    copy(vx[:, :, 256 * i:256 * i + 256], b2(VALUE_UNIT_BANK[i]), "xkv_copied")

                def read_copy(c):
                    t, r = c // 2, CH * (c % 2)
                    act.wait_ge(*sg.at("vnew_ready", l, 2 * c + 2))
                    for odd in range(2):
                        act.activation(os_[r:r + CH, t, odd:H:2, :],
                                       bank[odd][r:r + CH, P:2 * P].rearrange("p (b c) -> p b c", b=2), ACT.Copy)\
                            .then_inc(sg.inc("qs_copied"), 1)

                value_copy(0)
                act.wait_ge(*sg.at("u_done", l))
                copy(us, b2(0), "uw_copied")
                act.wait_ge(*sg.at("w_done", l))
                copy(wT[:, :, :], b2(1), "uw_copied")
                value_copy(1)

                def dsa_exp(t):
                    act.wait_ge(*sg.at("dmx_ready", l, t + 1))
                    n, Pd = P * (t + 1), Pds[t]
                    for h in range(H):
                        copy(Pd[:, n * h:n * h + n], Pd[:, n * h:n * h + n], "dexp_done", ACT.Exp,
                             bias=dmx[:, 4 * t + h:4 * t + h + 1], accum_out=dsum[:, 4 * t + h:4 * t + h + 1])

                read_copy(0)
                dsa_exp(0)
                read_copy(1)
                value_copy(2)
                read_copy(2)
                value_copy(3)
                dsa_exp(1)
                read_copy(3)
                act.wait_ge(*sg.at("sg_transposed", l))
                copy(yT[:, 0:2, :], b2(6), "yT_ready")
                act.wait_ge(*sg.at("PT_transposed", l, 1))
                copy(PT[:, 0:512], bank[7][:, :], "PT_copied")
                act.wait_ge(*sg.at("PT_transposed", l, 2))
                copy(PT[:, 512:1024], bank[5][:, :], "PT_copied")
                act.wait_ge(*sg.at("PT_transposed", l, 3))
                copy(PT[:, 1024:1536], bank[4][:, :], "PT_copied")
                act.wait_ge(*sg.at("dsa_out", l))
                copy(yT[:, 4:6, :], b2(5), "yT_ready")
                act.wait_ge(*sg.at("gdn_transposed", l))
                copy(hid_parts[0][:, 0, :, :], b2(0), "yT_ready")
                high(l, Q_OUT3), high(l, Q_XQ)

            def cross(l):
                def queries(h):
                    act.wait_ge(*products_done(l, Q_XQ + h))
                    act.activation(xqT[:, 2 * h:2 * h + 2, :], b2(4 * (h % 2)), ACT.Copy).then_inc(sg.inc("xq_copied"), 1)

                def exps(h):
                    act.wait_ge(*sg.at("xmax_ready", l, h + 1))
                    if h >= 2:
                        act.wait_ge(*sg.at("xPT", l, h - 1))
                    for t in range(NT):
                        act.activation(xP[:, h % 2, t, :], b2((1, 5, 1, 0)[h])[:, t, :], ACT.Exp, scale=1.0 / 16,
                                       bias=xnb[:, 2 * h + t:2 * h + t + 1], accum_out=xsum[:, 2 * h + t:2 * h + t + 1])\
                            .then_inc(sg.inc("xexp_done"), 1)

                def pt(h):
                    act.wait_ge(*sg.at("xPT", l, h + 1))
                    if h >= 2:
                        act.wait_ge(*sg.at("xvalues", l, h - 1))
                    act.activation(xPT[:, h % 2, :, :], b2(2), ACT.Copy).then_inc(sg.inc("xPT_copied"), 1)

                def outs(h):
                    act.wait_ge(*sg.at("xvalues", l, h + 1))
                    if h >= 2:
                        act.wait_ge(*products_done(l, Q_XO + h - 2))
                    act.activation(oT_parts[0][:, h % 2, :, :], b2(VALUES_BANK[h]), ACT.Copy).then_inc(sg.inc("oT_high"), 1)

                high(l, Q_XQ + 2), queries(0), high(l, Q_XQ + 3), queries(1), high(l, Q_XO)
                exps(0), queries(2), high(l, Q_XO + 1), exps(1), pt(0), queries(3), high(l, Q_XO + 2), outs(0)
                exps(2), pt(1), outs(1), pt(2), high(l, Q_XO + 3), exps(3), outs(2), pt(3), outs(3)
                high(l, Q_FFN[1]), high(l, Q_FFN[1] + 1)

            with act.Fori(0, DEPTH) as l:
                norm(l, 0, R_FFN1)
                ffn(l, 0)
                norm(l, 1, R_MIX)
                mixer(l)
                norm(l, 2, R_XA)
                cross(l)
                norm(l, 3, R_FFN2)
                ffn(l, 1)
            mean_squares(DEPTH, 0, lambda: sg.sem("ms_ready"))

        @block.gpsimd
        def _(pool):
            made = sg.sem("pool_made")
            n_made = [0]

            def step(ins):
                n_made[0] += 1
                ins.then_inc(made, 1)
                pool.wait_ge(made, n_made[0])

            def select(dst, src, op, fill, base, mult, pattern):
                step(pool.affine_select(out=dst, in_=src, compare_op=op, fill=fill, base=base,
                                        channel_multiplier=mult, pattern=pattern))

            step(pool.memset(zeros, 0.0))
            step(pool.memset(onesm[:, :], 1.0))
            select(ident[:, :], zeros, ALU.not_equal, 1.0, 0, 1, [[-1, P]])
            pool.memset(mhalf[:, :], -0.5).then_inc(sg.sem("ident_ready"), 1)
            pool.wait_ge(sg.sem("ident_ready"), 1)
            pool.wait_ge(sg.sem("mem_ms"), 2)
            step(pool.tensor_scalar(msb[:, 0:2], msb[:, 2:4], 1.0, EPS, ALU.mult, ALU.add))
            pool.tensor_tensor(msb[:, 4:6], msb[:, 0:2], mhalf[:, 0:2], ALU.pow).then_inc(sg.sem("mem_rstd"), 1)
            def norm(l, k, signal=sg.inc):
                for t in range(NT):
                    pool.wait_ge(*sg.at("ms_ready", l, 4 * k + 2 * t + 2))
                    if not isinstance(l, int):
                        apart(pool)
                    pool.tensor_scalar(mean[:, t:t + 1], ms[:, 2 * t:2 * t + 1], ms[:, 2 * t + 1:2 * t + 2], EPS,
                                       ALU.add, ALU.add).then_inc(signal("mean_ready"), 1)
                    pool.wait_ge(*sg.at("mean_ready", l, NT * k + t + 1))
                    pool.tensor_tensor(rstd[:, t:t + 1], mean[:, t:t + 1], mhalf[:, 0:1], ALU.pow)\
                        .then_inc(signal("rstd_ready"), 1)

            norm(0, 0, sg.sem)
            select(up[:, :], onesm[:, :], ALU.is_ge, 0.0, 0, -1, [[1, P]])
            select(half[:, 0, :], onesm[:, :], ALU.is_ge, 0.0, CH - 1, -1, [[0, P]])
            select(half[:, 1, :], onesm[:, :], ALU.is_ge, 0.0, -CH, 1, [[0, P]])

            def block_diagonal(dst, src, s):
                v = dst.rearrange("p (b c) -> p b c", c=s)
                select(v, src.rearrange("p (b c) -> p b c", c=s), ALU.is_ge, 0.0, 0, 1, [[-s, P // s], [0, s]])
                select(v, v, ALU.is_ge, 0.0, s - 1, -1, [[s, P // s], [0, s]])

            block_diagonal(same[:, :], onesm[:, :], CH)
            block_diagonal(incl[:, :], up[:, :], CH)
            step(pool.tensor_scalar(away[:, :], incl[:, :], -AWAY, AWAY, ALU.mult, ALU.add))
            for n, s in enumerate(LEVELS):
                block_diagonal(lev[:, n, :], up[:, :], 2 * s)
                if s > 1:
                    block_diagonal(stairs, up[:, :], s)
                    step(pool.tensor_tensor(lev[:, n, :], lev[:, n, :], stairs, ALU.subtract))
                else:
                    step(pool.tensor_tensor(lev[:, n, :], lev[:, n, :], ident[:, :], ALU.subtract))
            step(pool.memset(cfill[:, :], 0.0))
            for off in (0, 2 * P):
                select(cfill[:, off:off + P], cfill[:, off:off + P], ALU.is_ge, FILL, 0, 1, [[-1, P]])
            pool.memset(scz[:, :, 0:2], 0.0).then_inc(made, 1)
            pool.wait_ge(made, n_made[0] + 1)
            pool.memset(score[:, :], 0.0).then_inc(made, 1)
            pool.wait_ge(made, n_made[0] + 2)

            def link(ins, l):
                ins.then_inc(sg.inc("pool_link"), 1)
                pool.wait_ge(*sg.at("pool_link", l, sg.counts["pool_link"]))

            def rsqrt(dst, src, n, l, name, add=EPS):
                apart(pool)
                link(pool.tensor_scalar(msb[:, 0:n], src, 1.0, add, ALU.mult, ALU.add), l)
                pool.tensor_tensor(dst, msb[:, 0:n], mhalf[:, 0:n], ALU.pow).then_inc(sg.inc(name), 1)
                pool.wait_ge(*sg.at(name, l, sg.counts[name]))

            def mixer(l):
                apart(pool)
                pool.memset(z[:, :, 0:3], 0.0).then_inc(sg.inc("pads_ready"), 1)
                pool.wait_ge(*sg.at("z_copied", l))
                for j in range(4):
                    w = broadcast_last(gcw[:, 4:6, j], S)
                    src = z[:, 4:6, j:j + S]
                    if j == 0:
                        link(pool.tensor_tensor(cv[:, 4:6, :], src, w, ALU.mult), l)
                        continue
                    link(pool.tensor_tensor(sco[:, :, :], src, w, ALU.mult), l)
                    last = pool.tensor_tensor(cv[:, 4:6, :], cv[:, 4:6, :], sco[:, :, :], ALU.add)
                    if j < 3:
                        link(last, l)
                last.then_inc(sg.inc("conv_v"), 1)
                pool.wait_ge(*sg.at("l2_summed", l))
                rsqrt(l2r, l2s, 16, l, "l2_ready")
                pool.wait_ge(*sg.at("msa_ready", l))
                rsqrt(rsa, msa, 4, l, "rsa_ready")
                pool.wait_ge(*sg.at("mss_ready", l))
                rsqrt(rss, mss, 2, l, "rss_ready")
                pool.wait_ge(mem_loaded, 16 * (l + 1))
                apart(pool)
                for c in range(KC):
                    pool.tensor_scalar(memn[:, c, :], memn[:, c, :], cols[:, R_MEM + c:R_MEM + c + 1], 1.0,
                                       ALU.mult, ALU.mult).then_inc(sg.inc("memn_ready"), 1)
                pool.wait_ge(*sg.at("AE_ready", l))
                pool.wait_ge(*sg.at("l2_read", l))
                for i in range(len(LEVELS)):
                    for t in range(NT):
                        if i >= 2:
                            pool.wait_ge(*sg.at("U_done", l, NT * (i - 2) + t + 1))
                        if i == 2:
                            pool.wait_ge(*sg.at("TS_ready", l, 2 * t + 2))
                        pool.tensor_tensor(Bm[i % 2][:, t, :, :], AE[:, t, :, :],
                                           lev[:, i, :].unsqueeze(1).broadcast_to([P, H, P]), ALU.mult)\
                            .then_inc(sg.inc("B_ready"), 1)
                pool.wait_ge(*sg.at("scc_copied", l))
                pool.wait_ge(*sg.at("sch_copied", l))
                link(pool.tensor_tensor(scz[:, :, 2:2 + S], scz[:, :, 2:2 + S], sch[:, :, :], ALU.mult), l)
                link(pool.tensor_tensor(sco[:, :, :], scz[:, :, 0:S], broadcast_last(scw[:, :, 0], S), ALU.mult), l)
                for j in (1, 2):
                    link(pool.tensor_tensor(sch[:, :, :], scz[:, :, j:j + S], broadcast_last(scw[:, :, j], S), ALU.mult), l)
                    link(pool.tensor_tensor(sco[:, :, :], sco[:, :, :], sch[:, :, :], ALU.add), l)
                pool.wait_ge(*sg.at("scb_copied", l))
                pool.tensor_tensor(yT[:, 2:4, :], sco[:, :, :], yT[:, 2:4, :], ALU.mult).then_inc(sg.inc("sc_out"), 1)
                pool.wait_ge(*sg.at("gos_ready", l))
                rsqrt(gor, gos, 8, l, "gor_ready")

            with pool.Fori(0, DEPTH) as l:
                norm(l, 1)
                mixer(l)
                norm(l, 2)
                norm(l, 3)
                norm(l + 1, 0)

        @block.vector
        def _(dve):
            def link(ins, l):
                ins.then_inc(sg.inc("vector_link"), 1)
                dve.wait_ge(*sg.at("vector_link", l, sg.counts["vector_link"]))

            sg.begin(dve, "x_updated")
            dve.sem_inc(sg.sem("hid_ready"), 4)
            setup = sg.sem("vector_setup")
            n_setup = [0]

            def step(ins):
                n_setup[0] += 1
                ins.then_inc(setup, 1)
                dve.wait_ge(setup, n_setup[0])

            two_pi = 2 * np.pi
            p1 = 6.28125
            p2 = float(np.float32(np.floor((two_pi - p1) * 2.0 ** 21) / 2.0 ** 21))
            p3 = float(np.float32(two_pi - p1 - p2))
            magic = 1.5 * 2.0 ** 23
            pi_in = 3.1415925
            ang, kk, red = rtmp[:, :, 0, 0:ROT], rtmp[:, :, 2, 0:ROT], rtmp[:, :, 3, 0:ROT]
            cosa = rtmp[:, :, 1, 0:ROT]
            for j in range(ROT):
                step(dve.memset(inv[:, j:j + 1], float(np.float32(THETA) ** np.float32(-j * 2.0 / (2 * ROT)))))
            dve.wait_ge(small_loaded, 16)
            step(dve.tensor_copy(posf[:, :], posi[:, :]))
            step(dve.tensor_tensor(ang, broadcast_last(posf[:, :], ROT),
                                   inv[:, :].unsqueeze(1).broadcast_to([P, NT, ROT]), ALU.mult))
            step(dve.tensor_scalar(kk, ang, 1.0 / two_pi, None, ALU.mult))
            step(dve.tensor_scalar(kk, kk, magic, None, ALU.add))
            step(dve.tensor_scalar(kk, kk, -magic, None, ALU.add))
            for part in (p1, p2, p3):
                step(dve.scalar_tensor_tensor(out=ang, in0=kk, scalar=-part, in1=ang, op0=ALU.mult, op1=ALU.add))
            step(dve.tensor_scalar(cosa, ang, np.pi / 2, None, ALU.add))
            step(dve.tensor_scalar(red, cosa, pi_in, -two_pi, ALU.is_gt, ALU.mult))
            step(dve.tensor_tensor(cosa, cosa, red, ALU.add))
            dve.tensor_scalar(cosa, cosa, pi_in, -pi_in, ALU.min, ALU.max).then_inc(sg.sem("set_up_vector"), 1)
            dve.tensor_scalar(ang, ang, pi_in, -pi_in, ALU.min, ALU.max).then_inc(sg.sem("set_up_vector"), 1)
            dve.wait_ge(sg.sem("mem_rstd"), 1)
            for t in range(NT):
                dve.tensor_scalar(vx[:, t, :], vx[:, t, :], msb[:, 4 + t:5 + t], None, ALU.mult)\
                    .then_inc(sg.sem("set_up_vector"), 1)
            dve.wait_ge(sg.sem("trig_done"), 4)

            def gain(row, c):
                return broadcast_last(cols[:, row + c:row + c + 4], P)

            def normalise(l, k, t, signal=sg.inc):
                dve.wait_ge(*sg.at("rstd_ready", l, NT * k + t + 1))
                dve.tensor_scalar(hn[:, t, :], x[:, t, :], rstd[:, t:t + 1], None, ALU.mult)\
                    .then_inc(signal("hn_ready"), 1)

            def hT_piece(l, k, j, row):
                dve.wait_ge(*sg.at("hT_transposed", l, 4 * k + j + 1))
                dve.tensor_tensor(piece(hT, j), b4(norm_bank(k) + j), gain(row, 4 * (j % 2)), ALU.mult)\
                    .then_inc(sg.inc("hT_ready"), 1)

            def low_xT(l, k, j):
                dve.wait_ge(*sg.at("xT_high_ready", l, 4 * k + j + 1))
                high_, low_ = xm_parts if k == 1 else xT_parts
                dve.tensor_tensor(piece(low_, j), piece(hT, j), piece(high_, j), ALU.subtract)\
                    .then_inc(sg.inc("xT_low_ready"), 1)

            def norm(l, k, row):
                hT_piece(l, k, 0, row)
                if k:
                    normalise(l, k, 1)
                for j in (1, 2, 3):
                    hT_piece(l, k, j, row)
                for j in range(4):
                    low_xT(l, k, j)
                first = (0, Q_MIX, Q_XQ, Q_FFN[1])[k]
                if k == 0:
                    low(l, first)
                low(l, first + 1)

            def low(l, q, it=0):
                pos, ((high_, low_), n) = position(q), parts_of(q)
                dve.wait_ge(high_ready, nth(l, it * 6 + q))
                dve.tensor_tensor(low_[:, 0:n], ring[pos % RING][:, 0:n], high_[:, 0:n], ALU.subtract).then_inc(low_ready, 1)

            def add_product(l, k, bk, scale, all_done):
                for t in range(NT):
                    for n in range(2):
                        if (t, n) == (NT - 1, 1):
                            normalise(*((l, k + 1) if k < 3 else (l + 1, 0)), 0)
                        dve.wait_ge(*(all_done if (t, n) == (NT - 1, 1) else
                                      sg.at("bank_summed", l, 3 * k + 2 * t + n + 1)))
                        xs = x[:, t, 512 * n:512 * n + 512]
                        dve.scalar_tensor_tensor(out=xs, in0=bank[bk + 2 * t + n][:, :], scalar=scale, in1=xs,
                                                 op0=ALU.mult, op1=ALU.add).then_inc(sg.inc("x_updated"), 1)
                if k == 3:
                    normalise(l + 1, 0, 1)

            def ffn(l, which):
                q0 = Q_FFN[which]

                def step(par, s, it=0):
                    q = q0 + 3 * par + 2
                    split_next = s is not LAST
                    if split_next:
                        low(l, q, it)
                    else:
                        s = STEPS - 1
                    if not (isinstance(s, int) and s < 2):
                        dve.wait_ge(sg.sem("hid_low_ready"), step_of(l, which, s - 2))
                    for b in range(2):
                        dve.wait_ge(sg.sem("silu_ready"), (l * 2 + which) * 2 * STEPS + s * 2 + b + 1)
                        dve.tensor_tensor(hid[:, par, b, :], b2(4 + 2 * par + b)[:, 1, :], sil[:, par, b, :], ALU.mult)\
                            .then_inc(sg.sem("hid_ready"), 1)
                    if split_next:
                        low(l, q + 1, it)
                    else:
                        low(l, q0 + FFN_UNITS - 1)
                    dve.wait_ge(sg.sem("hid_high_ready"), step_of(l, which, s))
                    dve.tensor_tensor(hid_parts[1][:, par, :, :], hid[:, par, :, :], hid_parts[0][:, par, :, :], ALU.subtract)\
                        .then_inc(sg.sem("hid_low_ready"), 1)
                    if split_next:
                        low(l, q + 2, it)

                step(0, 0)
                step(1, 1)
                with dve.Fori(1, PAIRS) as it:
                    step(0, it * 2, it)
                    step(1, it * 2 + 1, it)
                step(0, LAST)
                if which == 0:
                    low(l, Q_MIX)
                add_product(l, 3 * which, 0, 0.5, products_done(l, q0 + FFN_UNITS - 1))

            def rope(v, heads, l, name):
                t1, t2 = rtmp[:, :, 0:heads, :], rtmp2[:, :, 0:heads, :]
                cb = rc[:, :, :].unsqueeze(2).broadcast_to([P, NT, heads, 2 * ROT])
                sb_ = rs[:, :, :].unsqueeze(2).broadcast_to([P, NT, heads, 2 * ROT])
                dve.tensor_tensor(t1, v[:, :, :, 0:2 * ROT], cb, ALU.mult)
                dve.tensor_tensor(t2[:, :, :, 0:ROT], v[:, :, :, ROT:2 * ROT], sb_[:, :, :, 0:ROT], ALU.mult)
                link(dve.tensor_tensor(t2[:, :, :, ROT:2 * ROT], v[:, :, :, 0:ROT], sb_[:, :, :, ROT:2 * ROT], ALU.mult), l)
                return dve.tensor_tensor(v[:, :, :, 0:2 * ROT], t1, t2, ALU.add)

            def mixer(l):
                def heads(ap):
                    return broadcast_last(ap.rearrange("p (t h) -> p t h", t=NT), HD)

                def by_head(ap):
                    return ap.rearrange("p t (h c) -> p t h c", h=H)

                for b in range(4):
                    if b % 2 == 0:
                        low(l, Q_MIX + 2 + b // 2)
                    dve.wait_ge(*sg.at("z_copied", l, b // 2 + 1))
                    link(dve.tensor_scalar(cv[:, b, :], z[:, b, 0:S], gcw[:, b, 0:1], None, ALU.mult), l)
                    for j in (1, 2, 3):
                        ins = dve.scalar_tensor_tensor(out=cv[:, b, :], in0=z[:, b, j:j + S], scalar=gcw[:, b, j:j + 1],
                                                       in1=cv[:, b, :], op0=ALU.mult, op1=ALU.add)
                        if j < 3:
                            link(ins, l)
                    ins.then_inc(sg.inc("conv_qk"), 1)
                low(l, Q_MIX + 4)
                dve.wait_ge(*sg.at("ab_copied", l))
                link(dve.tensor_tensor(ga1.rearrange("p (t h) -> p t h", t=NT), ab[:, :, 0:4],
                                       b_dt.unsqueeze(1).broadcast_to([P, NT, H]), ALU.add), l)
                dve.tensor_copy(beta.rearrange("p (t h) -> p t h", t=NT), ab[:, :, 4:8])
                link(dve.tensor_scalar(ga2, ga1, -1.0, None, ALU.mult), l)
                dve.tensor_tensor(ga2, ga1, ga2, ALU.min).then_inc(sg.inc("soft_in"), 1)
                low(l, Q_MIX + 5)
                dve.wait_ge(*sg.at("soft_ln", l))
                dve.tensor_scalar(beta, beta, 1.0, None, ALU.add)
                link(dve.scalar_tensor_tensor(out=ga1, in0=ga1, scalar=0.0, in1=ga3, op0=ALU.max, op1=ALU.add), l)
                dve.reciprocal(beta, beta)
                dve.scalar_tensor_tensor(out=gg_.rearrange("p (t h) -> p t h", t=NT),
                                         in0=ga1.rearrange("p (t h) -> p t h", t=NT), scalar=-1.0,
                                         in1=alog.unsqueeze(1).broadcast_to([P, NT, H]), op0=ALU.mult, op1=ALU.mult)\
                    .then_inc(sg.inc("g_ready"), 1)
                dve.wait_ge(*sg.at("g_ready", l))
                for t in range(NT):
                    last = dve.tensor_tensor(Sm[:, t, :, :], incl[:, :].unsqueeze(1).broadcast_to([P, H, P]),
                                             broadcast_last(gg_[:, 4 * t:4 * t + 4], P), ALU.mult)
                last.then_inc(sg.inc("gm_ready"), 1)
                for t in range(NT):
                    dve.wait_ge(*sg.at("qk_squared", l, t + 1))
                    last = dve.tensor_reduce(l2s[:, 8 * t:8 * t + 8],
                                             Bm[0][:, t, :, :].rearrange("p a b -> p (a b)").rearrange("p (h c) -> p h c", c=HD),
                                             AX, ALU.add)
                last.then_inc(sg.inc("l2_summed"), 1)
                low(l, Q_MIX + 6)
                dve.wait_ge(*sg.at("l2_ready", l))
                l2q = l2r.rearrange("p (t h) -> p t h", t=NT)[:, :, 0:4]
                link(dve.tensor_scalar(l2q, l2q, float(HD) ** -0.5, None, ALU.mult), l)
                for t in range(NT):
                    last = dve.tensor_tensor(qk[:, t, :, :], bank[t][:, :].rearrange("p (h c) -> p h c", c=HD),
                                             broadcast_last(l2r[:, 8 * t:8 * t + 8], HD), ALU.mult)
                    last.then_inc(sg.inc("qk_scaled"), 1)
                dve.wait_ge(*sg.at("qk_scaled", l))
                dve.tensor_tensor(by_head(kb), qk[:, :, 4:8, :], heads(beta), ALU.mult).then_inc(sg.inc("kb_ready"), 1)
                dve.wait_ge(*sg.at("rsa_ready", l))
                dve.wait_ge(*sg.at("iq0_copied", l))
                for t in range(NT):
                    dve.tensor_scalar(cn[:, t, :], b2(5)[:, t, 0:LAT], rsa[:, t:t + 1], None, ALU.mult)\
                        .then_inc(sg.inc("cn_ready"), 1)
                dve.wait_ge(*sg.at("iq1_scalar", l))
                for t in range(NT):
                    for i in (8, 9):
                        last = dve.scalar_tensor_tensor(out=R[:, t, i, :], in0=b2(6)[:, t, P:P + HD],
                                                        scalar=rsa[:, 2 + t:3 + t], in1=b_ikn, op0=ALU.mult, op1=ALU.mult)
                last.then_inc(sg.inc("iq1_copied"), 1)
                low(l, Q_MIX + 7)
                dve.wait_ge(*sg.at("c_transposed", l))
                dve.tensor_scalar(cT[:, :], bank[4][:, 0:S], cols[:, R_KV:R_KV + 1], None, ALU.mult)\
                    .then_inc(sg.inc("cT_ready"), 1)
                dve.wait_ge(*sg.at("gc_ready", l))
                dve.wait_ge(*sg.at("egc_ready", l))
                dve.tensor_tensor(ekd, bank[3][:, 64:72], gc, ALU.subtract).then_inc(sg.inc("ekd_in"), 1)
                dve.wait_ge(*sg.at("iq1_copied", l))
                dve.wait_ge(*sg.at("iq0_copied", l))
                last = rope(R[:, :, 0:9, :], 9, l, "q")
                link(last, l)
                dve.tensor_copy(R[:, :, 9, 0:2 * ROT], R[:, :, 8, 0:2 * ROT]).then_inc(sg.inc("rope_q"), 1)
                dve.wait_ge(*sg.at("sums_copied", l))
                dve.tensor_tensor(by_head(qg), qk[:, :, 0:4, :], heads(egc), ALU.mult).then_inc(sg.inc("qg_ready"), 1)
                low(l, Q_MIX + 8)
                for t in range(NT):
                    dve.wait_ge(*sg.at("gc_rows", l, t + 1))
                    dve.tensor_tensor(ET[:, t, :, :], b4(3 - t), away[:, :].unsqueeze(1).broadcast_to([P, H, P]), ALU.add)\
                        .then_inc(sg.inc("ET_in"), 1)
                dve.wait_ge(*sg.at("v_copied", l))
                dve.tensor_tensor(by_head(vb), by_head(gv[:, :, :]), heads(beta), ALU.mult)
                dve.wait_ge(*sg.at("kb_ready", l))
                dve.tensor_tensor(by_head(kbg), by_head(kb), heads(egc), ALU.mult)
                dve.tensor_tensor(by_head(kd), qk[:, :, 4:8, :], heads(ekd), ALU.mult).then_inc(sg.inc("ET_read"), 1)
                dve.wait_ge(*sg.at("kv_copied", l))
                rope(dk[:, :, :].rearrange("p t (h c) -> p t h c", h=H), H, l, "k").then_inc(sg.inc("rope_k"), 1)
                dve.wait_ge(*sg.at("rss_ready", l))
                for t in range(NT):
                    dve.scalar_tensor_tensor(out=sgn[:, t, :], in0=sgv[:, t, :], scalar=rss[:, t:t + 1], in1=b_sgn,
                                             op0=ALU.mult, op1=ALU.mult).then_inc(sg.inc("sgn_ready"), 1)
                dve.wait_ge(*sg.at("ET_ready", l))
                for t in range(NT):
                    for odd in range(2):
                        dve.wait_ge(*sg.at("kq_done", l, 2 * t + odd + 1))
                        for i, dst in enumerate((AE, AT)):
                            pair = (slice(None), t, slice(odd, H, 2), slice(None))
                            dve.tensor_tensor(dst[pair], b4(2 * t + odd)[:, 2 * i:2 * i + 2, :], ET[pair], ALU.mult)\
                                .then_inc(sg.inc("AE_ready"), 1)
                dve.wait_ge(*sg.at("qk_squared", l))
                dve.memset(state[:, :, :], 0.0).then_inc(sg.inc("l2_read"), 1)

                def weigh(t, h, src):
                    link(dve.scalar_tensor_tensor(out=work[t], in0=src, scalar=iw[:, t, h:h + 1],
                                                  in1=cfills[t] if h == 0 else work[t], op0=ALU.mult, op1=ALU.add), l)

                for t in range(NT):
                    n = P * (t + 1)
                    for i, h in enumerate((0, 2, 1, 3)):
                        if i % 2 == 0:
                            dve.wait_ge(*sg.at("relu_done", l, 2 * t + i // 2 + 1))
                        weigh(t, h, rel[:, n * i:n * i + n])
                    if t == 0:
                        dve.nop().then_inc(sg.inc("score_added"), 1)

                def take(t):
                    apart(dve)
                    link(dve.max(m8[:, t, :], work[t]), l)
                    apart(dve)
                    link(dve.match_replace(out=work[t], in_to_replace=m8[:, t, :], in_values=work[t],
                                           imm_value=TAKEN), l)

                takes = [0] * (TOPK // 8) + [1] * (TOPK // 8)
                for t in range(NT):
                    dve.wait_ge(*sg.at("B_ready", l, t + 1))
                    dve.tensor_tensor(Sm[:, t, :, :], ident[:, :].unsqueeze(1).broadcast_to([P, H, P]), Bm[0][:, t, :, :],
                                      ALU.subtract).then_inc(sg.inc("TS_ready"), 1)
                    dve.wait_ge(*sg.at("U_done", l, t + 1))
                    dve.tensor_tensor(Tm[:, t, :, :], ident[:, :].unsqueeze(1).broadcast_to([P, H, P]), b4(2 * t),
                                      ALU.subtract).then_inc(sg.inc("TS_ready"), 1)
                n = 0
                for i in range(1, len(LEVELS)):
                    for _ in range(3):
                        take(takes[n])
                        n += 1
                    for t in range(NT):
                        last_level = i == len(LEVELS) - 1
                        k = 2 * NT * (i - 1) + (t if last_level else 2 * t)
                        for j, (m, bk) in enumerate([(Tm, 2 * t + 1), (Sm, 2 * t)][last_level:]):
                            dve.wait_ge(*sg.at("TS_done", l, k + j + 1))
                            dve.tensor_tensor(m[:, t, :, :], m[:, t, :, :], b4(bk), ALU.subtract)\
                                .then_inc(sg.inc("TS_ready"), 1)
                take(takes[n])

                def selected(t):
                    link(dve.tensor_scalar(nb[t], work[t], TAKEN_BELOW, -AWAY, ALU.is_lt, ALU.mult), l)
                    link(dve.scalar_tensor_tensor(out=nb[t], in0=nb[t], scalar=AWAY, in1=cfills[t],
                                                  op0=ALU.add, op1=ALU.add), l)

                selected(0)
                selected(1)
                dve.wait_ge(*sg.at("egc_ready", l))
                eg = egl.rearrange("p c (b two) -> p c b two", two=2)
                dve.tensor_copy(egl2[0:HD], eg[0:HD, :, :, 0])
                dve.tensor_copy(egl2[HD:P], eg[HD:P, :, :, 1]).then_inc(sg.inc("state_ready"), 1)

                def chunk_new(c):
                    t, r = c // 2, CH * (c % 2)
                    dve.wait_ge(*sg.at("state_ready", l, c + 1))
                    dve.tensor_tensor(state_d[:, :, :], state[:, :, :], broadcast_last(egl2[:, c, :], HD), ALU.mult)
                    dve.wait_ge(*sg.at("ws_done", l, c + 1))
                    for odd in range(2):
                        pair = (slice(r, r + CH), t, slice(odd, H, 2), slice(None))
                        dve.tensor_tensor(by_head(vnew[:, :, :])[pair], by_head(us)[pair],
                                          bank[odd][r:r + CH, 0:P].rearrange("p (b c) -> p b c", b=2), ALU.subtract)\
                            .then_inc(sg.inc("vnew_ready"), 1)

                def chunk_state(c):
                    dve.wait_ge(*sg.at("kv_done", l, c + 1))
                    dve.tensor_tensor(state[:, :, :], state_d[:, :, :],
                                      bank[2][:, 0:2 * HD].rearrange("p (b c) -> p b c", b=2), ALU.add)\
                        .then_inc(sg.inc("state_ready"), 1)

                def logits(t):
                    dve.wait_ge(*sg.at("logits_done", l, t + 1))
                    n = P * (t + 1)
                    for odd in range(2):
                        dve.scalar_tensor_tensor(
                            out=Pds[t][:, 2 * n * odd:2 * n * odd + 2 * n].rearrange("p (b s) -> p b s", b=2),
                            in0=bank[4 + odd][:, 0:2 * n].rearrange("p (b s) -> p b s", b=2), scalar=float(HD) ** -0.5,
                            in1=nb[t].unsqueeze(1).broadcast_to([P, 2, n]), op0=ALU.mult, op1=ALU.add)\
                            .then_inc(sg.inc("logits_read"), 1)

                def row_max(t):
                    dst = dmx[:, 4 * t:4 * t + 4]
                    n = 4 * P * (t + 1)
                    dve.tensor_reduce(dst, Pds[t][:, 0:n].rearrange("p (h s) -> p h s", h=4), AX, ALU.max, negate=True)\
                        .then_inc(sg.inc("dmx_ready"), 1)

                def probs(t):
                    dve.wait_ge(*sg.at("dexp_done", l, 4 * t + 4))
                    d = dsum[:, 4 * t:4 * t + 4]
                    link(dve.reciprocal(d, d), l)
                    n = P * (t + 1)
                    v = Pds[t][:, 0:4 * n].rearrange("p (h s) -> p h s", h=4)
                    dve.tensor_tensor(v, v, broadcast_last(d, n), ALU.mult).then_inc(sg.inc("probs_ready"), 1)

                chunk_new(0)
                logits(0)
                dve.wait_ge(*sg.at("logits_read", l, 2))
                row_max(0)
                chunk_state(0)
                chunk_new(1)
                dve.wait_ge(*sg.at("sgw_transposed", l))
                dve.tensor_tensor(sgwT, b4(7), up[:, :].unsqueeze(1).broadcast_to([P, H, P]), ALU.mult)\
                    .then_inc(sg.inc("sgwT_ready"), 1)
                probs(0)
                dve.wait_ge(*sg.at("gate_read", l))
                link(dve.tensor_tensor(by_head(gate[:, :, :]), by_head(gate[:, :, :]),
                                       b_gon.unsqueeze(1).unsqueeze(1).broadcast_to([P, NT, H, HD]), ALU.mult), l)
                chunk_state(1)
                chunk_new(2)
                dve.wait_ge(*sg.at("sg_mixed", l))
                dve.wait_ge(*sg.at("sgu_gelu", l))
                link(dve.tensor_tensor(by_head(sgj), by_head(b2(6)),
                                       broadcast_last(cols[:, R_SGB:R_SGB + H], HD).unsqueeze(1).broadcast_to([P, NT, H, HD]), ALU.add), l)
                dve.tensor_tensor(sgj, sgj, sgu, ALU.mult).then_inc(sg.inc("sg_out"), 1)
                logits(1)
                dve.wait_ge(*sg.at("logits_read", l))
                row_max(1)
                chunk_state(2)
                chunk_new(3)
                chunk_state(3)
                probs(1)
                dve.wait_ge(*sg.at("o_done", l))
                dve.wait_ge(*sg.at("U_copied", l))
                dve.wait_ge(*sg.at("qs_copied", l))
                link(dve.tensor_tensor(by_head(us), by_head(b2(3)), os_, ALU.add), l)
                link(dve.tensor_tensor(kbg, us, us, ALU.mult), l)
                link(dve.tensor_reduce(gos, by_head(kbg), AX, ALU.add), l)
                dve.tensor_scalar(gos, gos, 1.0 / HD, None, ALU.mult).then_inc(sg.inc("gos_ready"), 1)
                dve.wait_ge(*sg.at("gor_ready", l))
                link(dve.tensor_tensor(by_head(us), by_head(us), heads(gor), ALU.mult), l)
                dve.tensor_tensor(vnew[:, :, :], us, gate[:, :, :], ALU.mult).then_inc(sg.inc("gdn_out"), 1)
                dve.wait_ge(*sg.at("yT_ready", l))
                dve.tensor_tensor(hid_parts[1][:, 0, :, :], b2(0), hid_parts[0][:, 0, :, :], ALU.subtract)\
                    .then_inc(sg.inc("y_low"), 1)
                low(l, Q_OUT3), low(l, Q_XQ)
                add_product(l, 1, 4, 1.0, products_done(l, Q_OUT3))

            def cross(l):
                def maxima(h):
                    dve.wait_ge(*sg.at("xlogits", l, h + 1))
                    m = xmx[:, 2 * h:2 * h + 2]
                    link(dve.tensor_reduce(m, b2((1, 5, 1, 0)[h]), AX, ALU.max), l)
                    dve.tensor_scalar(xnb[:, 2 * h:2 * h + 2], m, -1.0 / 16, None, ALU.mult)\
                        .then_inc(sg.inc("xmax_ready"), 1)

                def probs(h):
                    dve.wait_ge(*sg.at("xexp_done", l, NT * h + NT))
                    s = xsum[:, 2 * h:2 * h + 2]
                    link(dve.reciprocal(s, s), l)
                    v = xP[:, h % 2, :, :]
                    dve.tensor_tensor(v, v, broadcast_last(s, S), ALU.mult).then_inc(sg.inc("xprobs"), 1)

                def low_out(h):
                    dve.wait_ge(*sg.at("oT_high", l, h + 1))
                    dve.tensor_tensor(oT_parts[1][:, h % 2, :, :], b2(VALUES_BANK[h]), oT_parts[0][:, h % 2, :, :], ALU.subtract)\
                        .then_inc(sg.inc("oT_low"), 1)

                low(l, Q_XQ + 2), maxima(0), probs(0), low(l, Q_XQ + 3), maxima(1), probs(1), low(l, Q_XO), low_out(0)
                maxima(2), probs(2), low(l, Q_XO + 1), low_out(1), maxima(3), probs(3), low(l, Q_XO + 2), low_out(2)
                low(l, Q_XO + 3), low_out(3), low(l, Q_FFN[1])
                add_product(l, 2, 4, 1.0, products_done(l, Q_XO + 3))

            for t in range(NT):
                normalise(0, 0, t, sg.sem)
            with dve.Fori(0, DEPTH) as l:
                dve.wait_ge(*sg.at("rows_transposed", l))
                dve.tensor_copy(cols[:, :], bank[7][:, 0:N_ROWS]).then_inc(sg.inc("cols_ready"), 1)
                dve.wait_ge(*sg.at("cols_ready", l))
                norm(l, 0, R_FFN1)
                ffn(l, 0)
                norm(l, 1, R_MIX)
                mixer(l)
                norm(l, 2, R_XA)
                dve.nop().then_inc(sg.inc("params_used"), 1)
                cross(l)
                norm(l, 3, R_FFN2)
                ffn(l, 1)
            dve.wait_ge(small_loaded, 32)
            dve.wait_ge(*sg.at("hn_ready", DEPTH, NT))
            for t in range(NT):
                dve.tensor_tensor(hn[:, t, :], hn[:, t, :], vx[:, 0, :], ALU.mult).then_inc(sg.sem("out_ready"), 1)

        return dict(sg.counts)


def kernel(**inputs):
    import concourse.bacc as bacc
    from concourse.bass_utils import run_bass_kernel_spmd

    def program(arrays, per):
        nc = bacc.Bacc("TRN2", target_bir_lowering=False, num_devices=1)
        a = {n: nc.dram_tensor(f"in_{n}", v.shape, mybir.dt.from_np(v.dtype), kind="ExternalInput").ap()
             for n, v in arrays.items()}
        out = nc.dram_tensor("out", (1, S, D), F32, kind="ExternalOutput").ap()
        mem_scratch = nc.dram_tensor("mem_scratch", (P, KC, S), F32, kind="Internal").ap()
        return nc, build(nc, a, out, mem_scratch, per)

    arrays = {n: np.ascontiguousarray(inputs[n]) for n in NAMES}
    _, per = program(arrays, {})
    nc, _ = program(arrays, per)
    r = run_bass_kernel_spmd(nc, [{f"in_{n}": v for n, v in arrays.items()}], core_ids=[0])
    return r.results[0]["out"]
```
